# Optimizing a Trainium2 kernel written in Bass

```python
import jax, jax.numpy as jnp
from jax import lax
import numpy as np

D_MODEL = 1024
BATCH = 1
SEQ = 1024
DEPTH = 1
DEC_BATCH = 8
DEC_SEQ = 1
PAST_LEN = 1024
PAGE_SIZE = 128

D_MIX = D_MODEL
RET_HEADS = 4
RET_DK = 128
RET_DV = 128
RET_QK_WIDTH = RET_HEADS * RET_DK
RET_WIDTH = RET_HEADS * RET_DV
RET_CHUNK = 128
ROPE_BASE = 10000.0
SWA_Q_HEADS = 8
SWA_KV_HEADS = 2
SWA_HD = 64
SWA_GROUP = SWA_Q_HEADS // SWA_KV_HEADS
SWA_WIDTH = SWA_Q_HEADS * SWA_HD
SWA_KV_WIDTH = SWA_KV_HEADS * SWA_HD
WINDOW = 128
SWA_BLOCK = WINDOW
IN_WIDTHS = (RET_QK_WIDTH, RET_QK_WIDTH, RET_WIDTH, RET_WIDTH, SWA_WIDTH, SWA_KV_WIDTH, SWA_KV_WIDTH)
D_IN = sum(IN_WIDTHS)
IN_SPLITS = tuple(int(v) for v in np.cumsum(IN_WIDTHS)[:-1])
PEER_HEADS = 8
PEER_N_KEYS = 128
PEER_N_EXPERTS = PEER_N_KEYS * PEER_N_KEYS
PEER_D_QUERY = 256
PEER_D_HALF = PEER_D_QUERY // 2
PEER_TOPK = 16
PEER_BLOCK = 128
RMS_EPS = 1e-6

kernel_name = "hymba_retention_swa_sink_peer_step"

def rms_norm(x, g):
    xf = x.astype(jnp.float32)
    y = xf * lax.rsqrt(jnp.mean(xf * xf, axis=-1, keepdims=True) + RMS_EPS)
    return (y * g.astype(jnp.float32)).astype(x.dtype)

def rotate_pairs(x, pos):
    half = x.shape[-1] // 2
    inv = 1.0 / (ROPE_BASE ** jnp.linspace(0.0, 1.0, half, dtype=jnp.float32))
    ang = pos.astype(jnp.float32)[:, None] * inv[None, :]
    cos = jnp.cos(ang)[:, None, :].astype(x.dtype)
    sin = jnp.sin(ang)[:, None, :].astype(x.dtype)
    xr = x.reshape(*x.shape[:-1], half, 2)
    x1, x2 = xr[..., 0], xr[..., 1]
    return jnp.stack([x1 * cos - x2 * sin, x1 * sin + x2 * cos], axis=-1).reshape(x.shape)

def project_in(xn, w_in, pos):
    b, l, _ = xn.shape
    qr, kr, vr, gr, qs, ks, vs = jnp.split(xn @ w_in, IN_SPLITS, axis=-1)
    qr = rotate_pairs(qr.reshape(b, l, RET_HEADS, RET_DK), pos)
    kr = rotate_pairs(kr.reshape(b, l, RET_HEADS, RET_DK), pos) * (RET_DK ** -0.5)
    vr = vr.reshape(b, l, RET_HEADS, RET_DV)
    qs = qs.reshape(b, l, SWA_Q_HEADS, SWA_HD)
    ks = ks.reshape(b, l, SWA_KV_HEADS, SWA_HD)
    vs = vs.reshape(b, l, SWA_KV_HEADS, SWA_HD)
    return qr, kr, vr, gr, qs, ks, vs

def ret_log_decay():
    return jnp.log(1.0 - 2.0 ** (-5.0 - jnp.arange(RET_HEADS, dtype=jnp.float32)))

def retention_chunk(q, k, v, state):
    L = q.shape[1]
    lg = ret_log_decay()
    t = jnp.arange(L, dtype=jnp.float32)
    diff = t[:, None] - t[None, :]
    causal = diff >= 0
    dmask = jnp.where(causal[None], jnp.exp(jnp.where(causal, diff, 0.0)[None] * lg[:, None, None]), 0.0)
    scores = jnp.einsum('blhd,bmhd->bhlm', q, k) * dmask.astype(q.dtype)[None]
    o = jnp.einsum('bhlm,bmhe->blhe', scores, v)
    q_decay = jnp.exp((t + 1.0)[:, None] * lg[None, :]).astype(q.dtype)
    o = o + jnp.einsum('blhd,bhde->blhe', q, state) * q_decay[None, :, :, None]
    k_decay = jnp.exp((L - 1.0 - t)[:, None] * lg[None, :]).astype(q.dtype)
    new_state = (state * jnp.exp(L * lg).astype(q.dtype)[None, :, None, None]
                 + jnp.einsum('blhd,blhe->bhde', k * k_decay[None, :, :, None], v))
    return o, new_state

def retention_prompt(q, k, v):
    b, s = q.shape[0], q.shape[1]
    nc = s // RET_CHUNK
    to_chunks = lambda a: jnp.moveaxis(a.reshape(b, nc, RET_CHUNK, *a.shape[2:]), 1, 0)
    s0 = jnp.zeros((b, RET_HEADS, RET_DK, RET_DV), v.dtype)

    def step(st, qkv):
        o, st = retention_chunk(qkv[0], qkv[1], qkv[2], st)
        return st, o

    s_final, o = lax.scan(step, s0, (to_chunks(q), to_chunks(k), to_chunks(v)))
    return jnp.moveaxis(o, 0, 1).reshape(b, s, RET_HEADS, RET_DV), s_final

def retention_output(o, g):
    of = o.astype(jnp.float32)
    of = of * lax.rsqrt(jnp.mean(of * of, axis=-1, keepdims=True) + RMS_EPS)
    o = of.astype(o.dtype).reshape(*o.shape[:2], RET_WIDTH)
    return o * jax.nn.silu(g)

def sink_attention(q, k, v, q_pos, k_pos, sinks):
    qg = q.reshape(*q.shape[:-2], SWA_KV_HEADS, SWA_GROUP, SWA_HD)
    s = jnp.einsum('...qkgd,...skd->...kgqs', qg, k).astype(jnp.float32) * (SWA_HD ** -0.5)
    rel = q_pos[..., :, None] - k_pos[..., None, :]
    mask = (rel >= 0) & (rel < WINDOW) & (k_pos[..., None, :] >= 0)
    s = jnp.where(mask[..., None, None, :, :], s, -jnp.inf)
    sink = sinks.astype(jnp.float32).reshape(SWA_KV_HEADS, SWA_GROUP, 1, 1)
    m = jnp.maximum(jnp.max(s, axis=-1, keepdims=True), sink)
    p = jnp.exp(s - m)
    p = p / (jnp.sum(p, axis=-1, keepdims=True) + jnp.exp(sink - m))
    o = jnp.einsum('...kgqs,...skd->...qkgd', p.astype(v.dtype), v)
    return o.reshape(*q.shape[:-2], SWA_WIDTH)

def swa_prompt(q, k, v, sinks):
    b, s = q.shape[0], q.shape[1]
    nb = s // SWA_BLOCK
    qb = q.reshape(b, nb, SWA_BLOCK, SWA_Q_HEADS, SWA_HD)
    kb = k.reshape(b, nb, SWA_BLOCK, SWA_KV_HEADS, SWA_HD)
    vb = v.reshape(b, nb, SWA_BLOCK, SWA_KV_HEADS, SWA_HD)
    prev = lambda a: jnp.concatenate([jnp.zeros_like(a[:, :1]), a[:, :-1]], axis=1)
    kk = jnp.concatenate([prev(kb), kb], axis=2)
    vv = jnp.concatenate([prev(vb), vb], axis=2)
    pos_b = jnp.arange(s, dtype=jnp.int32).reshape(nb, SWA_BLOCK)
    k_pos = jnp.concatenate([pos_b - SWA_BLOCK, pos_b], axis=1)
    o = sink_attention(qb, kk, vv, pos_b, k_pos, sinks)
    return o.reshape(b, s, SWA_WIDTH)

def peer_block(xt, peer_w_q, peer_sub_keys, peer_u, peer_v):
    t = xt.shape[0]
    q = (xt @ peer_w_q).reshape(t, PEER_HEADS, 2, PEER_D_HALF)
    s = jnp.einsum('thcd,hcnd->thcn', q, peer_sub_keys).astype(jnp.float32)
    sv, si = lax.top_k(s, PEER_TOPK)
    cand = sv[..., 0, :, None] + sv[..., 1, None, :]
    cand_idx = si[..., 0, :, None] * PEER_N_KEYS + si[..., 1, None, :]
    best, sel = lax.top_k(cand.reshape(t, PEER_HEADS, PEER_TOPK * PEER_TOPK), PEER_TOPK)
    idx = jnp.take_along_axis(cand_idx.reshape(t, PEER_HEADS, PEER_TOPK * PEER_TOPK), sel, axis=-1)
    gates = jax.nn.softmax(best, axis=-1).astype(xt.dtype)
    h = jnp.einsum('thkd,td->thk', peer_u[idx], xt)
    a = jax.nn.gelu(h, approximate=False) * gates
    return jnp.einsum('thk,thkd->td', a, peer_v[idx])

def peer_ffn(x, peer_w_q, peer_sub_keys, peer_u, peer_v):
    shape = x.shape
    xt = x.reshape(-1, shape[-1])
    t = xt.shape[0]
    nb = -(-t // PEER_BLOCK)
    xt = jnp.pad(xt, ((0, nb * PEER_BLOCK - t), (0, 0))).reshape(nb, PEER_BLOCK, shape[-1])
    out = lax.map(lambda xb: peer_block(xb, peer_w_q, peer_sub_keys, peer_u, peer_v), xt)
    return out.reshape(-1, shape[-1])[:t].reshape(shape)

def finish_layer(x, o_ret, g_ret, o_swa, w_out, norm2_g, peer_w_q, peer_sub_keys, peer_u, peer_v, final_g):
    h = x + jnp.concatenate([retention_output(o_ret, g_ret), o_swa], axis=-1) @ w_out
    h = h + peer_ffn(rms_norm(h, norm2_g), peer_w_q, peer_sub_keys, peer_u, peer_v)
    return rms_norm(h, final_g)

def setup_inputs(seed: int = 0) -> dict:
    key = jax.random.key(seed)
    ks = jax.random.split(key, 15)
    f = jnp.float32
    nrm = lambda k, shp, sc: jax.random.normal(k, shp, f) * sc
    return {
        "x_prompt": nrm(ks[0], (BATCH, SEQ, D_MODEL), 1.0),
        "x_sample": nrm(ks[1], (DEC_BATCH, DEC_SEQ, D_MODEL), 1.0),
        "state_ret": nrm(ks[2], (DEC_BATCH, RET_HEADS, RET_DK, RET_DV), 1.0),
        "cache_swa_k": nrm(ks[3], (DEC_BATCH, WINDOW, SWA_KV_HEADS, SWA_HD), 1.0),
        "cache_swa_v": nrm(ks[4], (DEC_BATCH, WINDOW, SWA_KV_HEADS, SWA_HD), 1.0),
        "norm1_g": 1.0 + nrm(ks[5], (D_MODEL,), 0.02),
        "w_in": nrm(ks[6], (D_MODEL, D_IN), D_MODEL ** -0.5),
        "swa_sinks": nrm(ks[7], (SWA_Q_HEADS,), 0.5),
        "w_out": nrm(ks[8], (D_MIX, D_MODEL), D_MIX ** -0.5),
        "norm2_g": 1.0 + nrm(ks[9], (D_MODEL,), 0.02),
        "peer_w_q": nrm(ks[10], (D_MODEL, PEER_HEADS * PEER_D_QUERY), D_MODEL ** -0.5),
        "peer_sub_keys": nrm(ks[11], (PEER_HEADS, 2, PEER_N_KEYS, PEER_D_HALF), PEER_D_HALF ** -0.5),
        "peer_u": nrm(ks[12], (PEER_N_EXPERTS, D_MODEL), D_MODEL ** -0.5),
        "peer_v": nrm(ks[13], (PEER_N_EXPERTS, D_MODEL), PEER_HEADS ** -0.5),
        "final_g": 1.0 + nrm(ks[14], (D_MODEL,), 0.02),
    }

def reference(x_prompt, x_sample, state_ret, cache_swa_k, cache_swa_v, norm1_g, w_in, swa_sinks,
              w_out, norm2_g, peer_w_q, peer_sub_keys, peer_u, peer_v, final_g):
    y_p = x_prompt
    y_s = x_sample
    for _ in range(DEPTH):
        s_len = y_p.shape[1]
        pos_p = jnp.arange(s_len, dtype=jnp.int32)
        qr, kr, vr, gr, qs, ks, vs = project_in(rms_norm(y_p, norm1_g), w_in, pos_p)
        o_ret, state_ret_p = retention_prompt(qr, kr, vr)
        o_swa = swa_prompt(qs, ks, vs, swa_sinks)
        swa_k_p = ks[:, -WINDOW:]
        swa_v_p = vs[:, -WINDOW:]
        y_p = finish_layer(y_p, o_ret, gr, o_swa, w_out, norm2_g, peer_w_q, peer_sub_keys,
                           peer_u, peer_v, final_g)

        d_len = y_s.shape[1]
        pos_s = PAST_LEN + jnp.arange(d_len, dtype=jnp.int32)
        qr, kr, vr, gr, qs, ks, vs = project_in(rms_norm(y_s, norm1_g), w_in, pos_s)
        o_ret, state_ret_s = retention_chunk(qr, kr, vr, state_ret.astype(vr.dtype))
        kk = jnp.concatenate([cache_swa_k.astype(ks.dtype), ks], axis=1)
        vv = jnp.concatenate([cache_swa_v.astype(vs.dtype), vs], axis=1)
        k_pos = jnp.concatenate([PAST_LEN - WINDOW + jnp.arange(WINDOW, dtype=jnp.int32), pos_s])
        o_swa = sink_attention(qs, kk, vv, pos_s, k_pos, swa_sinks)
        swa_k_s = kk[:, -WINDOW:]
        swa_v_s = vv[:, -WINDOW:]
        y_s = finish_layer(y_s, o_ret, gr, o_swa, w_out, norm2_g, peer_w_q, peer_sub_keys,
                           peer_u, peer_v, final_g)
    return (y_p, y_s, state_ret_p, swa_k_p, swa_v_p, state_ret_s, swa_k_s, swa_v_s)


_drawn_inputs = setup_inputs


def setup_inputs(seed=0):
    import zlib

    import numpy as np

    out = dict(_drawn_inputs(seed))
    spreads = {}
    factors = {'swa_sinks': 30.469, 'final_g': 8.122}
    for name, (base, spread) in spreads.items():
        noise = np.random.default_rng([zlib.crc32(name.encode()), seed]).standard_normal(out[name].shape)
        drawn = base * np.exp(spread * noise) if base else spread * noise
        out[name] = __import__('jax').numpy.asarray(drawn.astype(out[name].dtype))
    for name, factor in factors.items():
        out[name] = (out[name] * factor).astype(out[name].dtype)
    return out
```

```python
from contextlib import ExitStack

import numpy as np

import concourse.bass as bass
from concourse import mybir

F32 = mybir.dt.float32
U32 = mybir.dt.uint32
ALU = mybir.AluOpType
ACT = mybir.ActivationFunctionType
AX = mybir.AxisListType.X

P = 128
D = 1024
KC = D // P
SEQ = 1024
NB = SEQ // P
NS = 8
NTOK = SEQ + NS
RH, HD = 4, 128
QH, KVH, SD = 8, 2, 64
GRP = QH // KVH
D_IN = 4 * RH * HD + QH * SD + 2 * KVH * SD
C_Q, C_K, C_V, C_G = 0, 512, 1024, 1536
C_QS, C_KS, C_VS = 2048, 2560, 2688
C_MIX = C_G
PH, TK, NK = 8, 16, 128
NHC = 2 * PH
NSC = NHC * NK
SLOTS = PH * TK
HALF = SLOTS // 2
RING = 8
ROWW = 2 * D
GROUPS = SLOTS // RING
PAIR = 2
PAIRS = RING // PAIR
NCH = 8
CW = D_IN // NCH
STG = 6
EPS = 1e-6
K_SCALE = HD ** -0.5
S_SCALE = SD ** -0.5
LOG_DECAY = np.log(1.0 - 2.0 ** (-5.0 - np.arange(RH)))
STEP_DECAY = [float(v) for v in np.exp(LOG_DECAY)]
BLOCK_DECAY = [float(v) for v in np.exp(P * LOG_DECAY)]
MASKED = -1e30
TAKEN = -3.0e38


class Steps:

    def __init__(self, eng, sem):
        self.eng, self.sem, self.n, self.base = eng, sem, 0, 0

    def did(self, ins):
        self.n += 1
        ins.then_inc(self.sem, 1)

    def sync(self):
        self.eng.wait_ge(self.sem, self.base + self.n)

    def enter(self, turn, per):
        self.first, self.per = self.n, per
        self.base = turn * per

    def leave(self, turns):
        assert self.n - self.first == self.per, (self.n - self.first, self.per)
        self.base, self.n = 0, self.first + turns * self.per


def hold(eng, sem, count):
    eng.wait_ge(sem, count)
    eng.nop(nofuse=True)


def build(nc, A, out):
    ctx = ExitStack()
    with ctx:
        def sb(name, shape, dt=F32):
            return ctx.enter_context(nc.sbuf_tensor(name, shape, dt))

        def sem(name):
            return ctx.enter_context(nc.semaphore(name))

        ring = sb("ring", [P, RING * ROWW])
        keyw = sb("keyw", [P, KC, NSC])
        wo = sb("wo", [P, KC, D])
        proj = sb("proj", [P, D_IN])
        work = sb("work", [P, 2 * D])
        h = sb("h", [P, D])
        x2g = sb("x2g", [P, D])
        g2b = sb("g2b", [P, D])
        gfb = sb("gfb", [P, D])
        qsT = sb("qsT", [P, 512])
        kTb = sb("kTb", [P, 2 * P])
        vprev = sb("vprev", [P, P])
        state = sb("state", [P, RH, HD])
        dmaskT = sb("dmaskT", [P, RH, P])
        wmask = sb("wmask", [P, 2 * P])
        ident = sb("ident", [P, P])
        idx = sb("idx", [P, SLOTS], U32)
        gates = sb("gates", [P, SLOTS])
        idxg = sb("idxg", [P, SLOTS], U32)
        gateg = sb("gateg", [P, SLOTS])
        idxst = sb("idxst", [P, 2 * RING], U32)
        small = sb("small", [P, 160])
        mixTs = sb("mixTs", [P, KC * NS])
        ps = ctx.enter_context(nc.psum_tensor("ps", [P, 8, 512], F32))
        acc = ps[:, 0:2, :].rearrange("p a b -> p (a b)")
        F = [ps[:, 2 + i, :] for i in range(6)]

        def FF(a, b):
            return ps[:, 2 + a:2 + b, :].rearrange("p a b -> p (a b)")

        row_u = [ring[:, r * ROWW:r * ROWW + D] for r in range(RING)]
        row_v = [ring[:, r * ROWW + D:(r + 1) * ROWW] for r in range(RING)]
        row = [ring[:, r * ROWW:(r + 1) * ROWW] for r in range(RING)]
        x2, xT = work[:, 0:D], work[:, D:2 * D]
        rope = qsT[:, 0:256]

        at = [0]

        def cols(n):
            at[0] += n
            return small[:, at[0] - n:at[0]]

        g1c, qdec, kdec, sinkb, iota16 = cols(8), cols(4), cols(4), cols(8), cols(16)
        ssq, rstd, mx, nmx, rs, es, rden = cols(4), cols(4), cols(8), cols(8), cols(8), cols(8), cols(8)
        hs1, hs2, fs1, fs2 = cols(1), cols(1), cols(1), cols(1)
        ssum, srec = cols(8), cols(8)
        dot, gel = cols(RING), cols(RING)
        qk, sinks64, m64, n64, r64, e64 = cols(4), cols(1), cols(1), cols(1), cols(1), cols(1)

        xTall = ring[:, 0:KC * NTOK].rearrange("p (k t) -> p k t", k=KC)
        wbuf = [ring[:, KC * NTOK + c * KC * CW:KC * NTOK + (c + 1) * KC * CW].rearrange("p (k n) -> p k n", k=KC)
                for c in range(2)]
        top = KC * NTOK + 2 * KC * CW
        wqT = [ring[:, top + c * D:top + (c + 1) * D] for c in range(2)]
        skT = wo[:, 0:2, :].rearrange("p a b -> p (a b)")
        xa = [h[:, :], x2g[:, :]]
        staging = [work[:, 0:CW * 5].rearrange("p (s n) -> p s n", s=5)[:, i, :] for i in range(5)]
        staging.append(qsT[:, 0:CW])
        o1 = [0]

        def part(n):
            o1[0] += n
            return ring[:, o1[0] - n:o1[0]]

        kw = part(NS * P).rearrange("p (s c) -> p s c", s=NS)
        vw = part(NS * P).rearrange("p (s c) -> p s c", s=NS)
        st_s = part(NS * RH * HD).rearrange("p (s h e) -> p s h e", s=NS, h=RH)
        kwT = part(NS * P)
        sel8 = part(NS * P)
        sT = part(96)
        ss = part(64)
        sr = part(P)
        pts = part(64)
        osT = part(32)
        mask0 = part(2 * P)

        ld_const, ld_skT = sem("ld_const"), sem("ld_skT")
        ld_wq = [sem("ld_wq0"), sem("ld_wq1")]
        ld_x = [sem("ld_x0"), sem("ld_x1")]
        ld_w = [sem("ld_w0"), sem("ld_w1")]
        ld_wo = sem("ld_wo")
        keyw_mm, keyw_out = sem("keyw_mm"), sem("keyw_out")
        root_in, root_out = sem("root_in"), sem("root_out")
        xn_ready, xn_T, xn_out = sem("xn_ready"), sem("xn_T"), sem("xn_out")
        pj_mm, pj_out = sem("pj_mm"), sem("pj_out")
        st_pj = [sem(f"st_pj{i}") for i in range(STG)]
        zeroed = sem("zeroed")
        dve_steps, act_steps = sem("dve_steps"), sem("act_steps")
        ld_proj, ld_res, ld_mask0 = sem("ld_proj"), sem("ld_res"), sem("ld_mask0")
        roped, kd_ready = sem("roped"), sem("kd_ready")
        qkT_mm, qkT_out = sem("qkT_mm"), sem("qkT_out")
        st_mm, stm_ready, ret_mm, silu_ready, mixr_ready = (sem("st_mm"), sem("stm_ready"), sem("ret_mm"),
                                                            sem("silu_ready"), sem("mixr_ready"))
        qsT_mm, qsT_out, sw_mm, sw_nmax, sw_exp = (sem("qsT_mm"), sem("qsT_out"), sem("sw_mm"), sem("sw_nmax"),
                                                   sem("sw_exp"))
        pT_mm, pT_out, sw_o, mixs_ready = (sem("pT_mm"), sem("pT_out"), sem("sw_o"),
                                                        sem("mixs_ready"))
        mixT_mm, mixT_out, o_mm, x2_ready = sem("mixT_mm"), sem("mixT_out"), sem("o_mm"), sem("x2_ready")
        x2T_mm, x2T_out, sc_mm, sc_out = sem("x2T_mm"), sem("x2T_out"), sem("sc_mm"), sem("sc_out")
        best_shift, best_exp, topk_done = sem("best_shift"), sem("best_exp"), sem("topk_done")
        idx_taken, acc_out = sem("idx_taken"), sem("acc_out")
        ld_row = [sem(f"ld_row{r}") for r in range(RING)]
        staged, dots, gelus, diags, used = sem("staged"), sem("dots"), sem("gelus"), sem("diags"), sem("used")
        residual_in, y_ready, st_y = sem("residual_in"), sem("y_ready"), sem("st_y")
        st_misc, st_state = sem("st_misc"), sem("st_state")
        sm = {n: sem("smp_" + n) for n in (
            "kw", "sel", "qT", "qT_out", "kwT", "kwT_out", "s", "s_out", "sr", "nmax", "exp", "p", "pT", "pT_out",
            "o", "o_out", "qS", "qS_out", "qSn", "mixr", "mixT", "mixT_out", "vb", "vb_used", "silu", "st", "tok",
            "spread", "idx8", "rowsx")}

        proj_d = nc.dram_tensor("proj_scratch", [NTOK, D_IN], F32).ap()
        w_in_v = A["w_in"].rearrange("(k p) n -> p k n", p=P)
        x_p = A["x_prompt"].rearrange("a t d -> (a t) d")
        x_s = A["x_sample"].rearrange("a t d -> (a t) d")
        y_p = out[0].rearrange("a t d -> (a t) d")
        y_s = out[1].rearrange("a t d -> (a t) d")
        N_CONST = 10 + NS

        block = ctx.enter_context(nc.Block())

        def rows_of(vector, n):
            return vector.rearrange("(a n) -> a n", a=1).to_broadcast([P, n])

        @block.sync
        def _(sp):
            for i in range(2):
                sp.dma_start(xa[i], x_p[i * P:(i + 1) * P, :]).then_inc(ld_x[i], 16)
            loads = [(ident[:], A["c_ident"]), (g1c, A["norm1_g"].rearrange("(k p) -> p k", p=P)),
                     (qdec, A["c_qdec"]), (kdec, A["c_kdec"]), (iota16, A["c_iota"]),
                     (sinkb, rows_of(A["swa_sinks"], QH)),
                     (dmaskT[:].rearrange("p h m -> p (h m)"), A["c_dmaskT"]), (wmask[:], A["c_wmask"]),
                     (g2b[:], rows_of(A["norm2_g"], D)), (gfb[:], rows_of(A["final_g"], D))]
            loads += [(sinks64[s * QH:(s + 1) * QH, :], A["swa_sinks"].rearrange("(q a) -> q a", a=1))
                      for s in range(NS)]
            for dst, src in loads:
                sp.dma_start(dst, src, allow_slow_non_contiguous=True).then_inc(ld_const, 16)
            sp.dma_start(skT, A["sub_keysT"]).then_inc(ld_skT, 16)
            sp.dma_start(wqT[0], A["wqT"][0]).then_inc(ld_wq[0], 16)
            sp.dma_start(wqT[1], A["wqT"][1]).then_inc(ld_wq[1], 16)
            for c in range(2):
                sp.dma_start(wbuf[c], w_in_v[:, :, c * CW:(c + 1) * CW]).then_inc(ld_w[c], 16)

            def load_wqT(i, a):
                sp.wait_ge(keyw_mm, i * 8 + (2 * a - 2))
                sp.dma_start(wqT[a % 2], A["wqT"][bass.ds(i * 4 + a, 1)].rearrange("a p n -> p (a n)")
                             ).then_inc(ld_wq[a % 2], 16)

            with sp.Fori(0, NB // 2 - 1) as i:
                load_wqT(i, 2)
                load_wqT(i, 3)
                for c in range(2):
                    sp.wait_ge(xn_T, i * 2 + (c + 1))
                    sp.dma_start(xa[c], x_p[bass.ds(i * (2 * P) + (2 + c) * P, P), :]).then_inc(ld_x[c], 16)
                load_wqT(i, 4)
                load_wqT(i, 5)
            load_wqT(NB // 2 - 1, 2)
            load_wqT(NB // 2 - 1, 3)
            sp.wait_ge(keyw_mm, 2 * NHC)
            sp.dma_start(wo[:], A["w_out"].rearrange("(k p) n -> p k n", p=P)).then_inc(ld_wo, 16)
            sp.wait_ge(xn_T, NB - 1)
            sp.dma_start(xa[0][0:NS, :], x_s).then_inc(ld_x[0], 16)

            def store_tile(c, i, tile, turn):
                rows = P if i < NB else NS
                sp.wait_ge(pj_out, turn * (2 * (NB + 1)) + tile + 1)
                sp.dma_start(proj_d[i * P:i * P + rows, bass.ds(turn * (2 * CW) + c * CW, CW)],
                             staging[tile % STG][0:rows, :]).then_inc(st_pj[tile % STG], 16)

            with sp.Fori(0, NCH // 2 - 1) as t:
                for c in range(2):
                    for i in range(NB + 1):
                        store_tile(c, i, c * (NB + 1) + i, t)
                    sp.wait_ge(pj_mm, t * (2 * (NB + 1)) + (c + 1) * (NB + 1))
                    sp.dma_start(wbuf[c], w_in_v[:, :, bass.ds(t * (2 * CW) + (c + 2) * CW, CW)]
                                 ).then_inc(ld_w[c], 16)
            for c in range(2):
                for i in range(NB + 1):
                    store_tile(c, i, c * (NB + 1) + i, NCH // 2 - 1)
            for i in range(STG):
                sp.wait_ge(st_pj[i], 16 * NCH * (NB + 1) // STG)

            sp.dma_start(proj[0:NS, :], proj_d[SEQ:NTOK, :]).then_inc(sm["kw"], 16)
            sp.dma_start(rope[0:NS, :], A["c_rope"][SEQ:NTOK, :]).then_inc(sm["kw"], 16)
            for s in range(NS):
                sp.dma_start(kw[0:P - 1, s, :], A["cache_swa_k"][s, 1:P].rearrange("w k d -> w (k d)")
                             ).then_inc(sm["kw"], 16)
                sp.dma_start(vw[0:P - 1, s, :], A["cache_swa_v"][s, 1:P].rearrange("w k d -> w (k d)")
                             ).then_inc(sm["kw"], 16)
            sp.dma_start(kw[P - 1:P, :, :], proj_d[SEQ:NTOK, C_KS:C_VS].rearrange("(a s) c -> a s c", a=1)
                         ).then_inc(sm["kw"], 16)
            sp.dma_start(vw[P - 1:P, :, :], proj_d[SEQ:NTOK, C_VS:D_IN].rearrange("(a s) c -> a s c", a=1)
                         ).then_inc(sm["kw"], 16)
            sp.dma_start(sel8[0:NS, :], A["c_sel8"]).then_inc(sm["kw"], 16)
            sp.dma_start(st_s.rearrange("p s h e -> p (s h) e"),
                         A["state_ret"].rearrange("s h d e -> d (s h) e")).then_inc(sm["kw"], 16)
            sp.dma_start(mask0, A["c_wmask0"]).then_inc(sm["kw"], 16)
            sp.wait_ge(sm["kw"], 16 * (2 + 2 * NS + 5))
            sp.dma_start(out[6].rearrange("s w k d -> w s (k d)"), kw).then_inc(st_misc, 16)
            sp.dma_start(out[7].rearrange("s w k d -> w s (k d)"), vw).then_inc(st_misc, 16)
            sp.dma_start(out[3][0].rearrange("w k d -> w (k d)"), proj_d[SEQ - P:SEQ, C_KS:C_VS]).then_inc(st_misc, 16)
            sp.dma_start(out[4][0].rearrange("w k d -> w (k d)"), proj_d[SEQ - P:SEQ, C_VS:D_IN]).then_inc(st_misc, 16)
            sp.wait_ge(sm["mixr"], 1)
            sp.wait_ge(sm["mixT"], 1)
            sp.dma_start(proj[:], proj_d[0:P, :]).then_inc(ld_proj, 16)
            sp.dma_start(rope, A["c_rope"][0:P, :]).then_inc(ld_proj, 16)
            sp.dma_start(h[:], x_p[0:P, :]).then_inc(ld_res, 16)
            sp.wait_ge(sm["st"], 1)
            sp.dma_start(out[5].rearrange("s h d e -> d (s h) e"), st_s.rearrange("p s h e -> p (s h) e")
                         ).then_inc(st_state, 16)
            sp.wait_ge(st_state, 16)
            sp.wait_ge(st_misc, 64)
            sp.sem_inc(sm["tok"], 1)

            def load_columns(b):
                sp.dma_start(proj[:], proj_d[bass.ds(b * P, P), :]).then_inc(ld_proj, 16)
                sp.dma_start(rope, A["c_rope"][bass.ds(b * P, P), :]).then_inc(ld_proj, 16)

            def load_residual(b):
                sp.wait_ge(residual_in, b)
                sp.dma_start(h[:], x_p[bass.ds(b * P, P), :]).then_inc(ld_res, 16)

            def store_y(b):
                sp.wait_ge(y_ready, b + 1)
                sp.dma_start(y_p[bass.ds(b * P, P), :], xT).then_inc(st_y, 16)

            sp.wait_ge(topk_done, 2)
            load_columns(1)
            with sp.Fori(0, NB - 2) as b:
                load_residual(b + 1)
                store_y(b)
                sp.wait_ge(st_y, b * 16 + 16)
                load_columns(b + 2)
            load_residual(NB - 1)
            store_y(NB - 2)
            sp.wait_ge(st_y, 16 * (NB - 1))
            sp.wait_ge(residual_in, NB)
            sp.dma_start(h[0:NS, :], x_s).then_inc(ld_res, 16)
            sp.wait_ge(mixs_ready, NB)
            sp.dma_start(out[2][0].rearrange("h d e -> d h e"), state[:]).then_inc(st_misc, 16)
            sp.dma_start(qsT[0:NS, 0:P], A["c_spread"]).then_inc(sm["sel"], 16)
            sp.dma_start(qsT[:, P:2 * P + NS], A["c_pick"]).then_inc(sm["sel"], 16)
            sp.wait_ge(y_ready, NB)
            sp.dma_start(y_p[(NB - 1) * P:NB * P, :], xT).then_inc(st_y, 16)
            sp.wait_ge(y_ready, NB + 1)
            sp.dma_start(y_s, work[0:NS, 0:D]).then_inc(st_y, 16)
            sp.wait_ge(st_y, 16 * (NB + 1))
            sp.wait_ge(st_misc, 80)

        @block.gpsimd
        def _(pool):
            pool.wait_ge(sm["tok"], 1)

            def fetch(r, col):
                nc.gpsimd.indirect_dma_start(row[r], None, A["peer_uv"],
                                             bass.IndirectOffsetOnAxis(ap=idxst[:, col:col + 1], axis=0)
                                             ).then_inc(ld_row[r], 16)

            with pool.Fori(0, NB) as b:
                for half in range(2):
                    hold(pool, topk_done, b * 2 + (half + 1))
                    own = slice(half * HALF, (half + 1) * HALF)
                    nc.gpsimd.tensor_copy(idxg[:, own], idx[:, own]).then_inc(idx_taken, 1)
                    hold(pool, idx_taken, b * 2 + (half + 1))
                    with pool.Fori(0, PH // 2) as hd:
                        for part_ in range(2):
                            c0 = part_ * RING
                            nc.gpsimd.tensor_copy(idxst[:, c0:c0 + RING],
                                                  idxg[:, bass.ds(hd * TK + (half * HALF + c0), RING)]
                                                  ).then_inc(staged, 1)
                            hold(pool, staged, b * (2 * PH) + hd * 2 + (half * PH + part_ + 1))
                            for r in range(RING):
                                hold(pool, used, b * SLOTS + hd * TK + (half * HALF + c0 + r + 1))
                                fetch(r, c0 + r)
            pool.wait_ge(sm["idx8"], 1)
            for hd in range(PH):
                hold(pool, used, NB * SLOTS + hd + 1)
                nc.gpsimd.indirect_dma_start(row[hd], None, A["peer_uv"],
                                             bass.IndirectOffsetOnAxis(ap=idx[:, hd:hd + 1], axis=0)
                                             ).then_inc(ld_row[hd], 16)

        @block.tensor
        def _(pe):
            def T(o, i, n=P):
                return nc.tensor.transpose(o, i, ident[0:n, 0:n])

            pe.wait_ge(ld_const, 16 * N_CONST)
            pe.wait_ge(ld_skT, 16)

            TB = [acc, FF(4, 6)]

            def key_weights(i, a, first):
                pe.wait_ge(ld_wq[a % 2], i * 32 + 16 * (a // 2 + 1))
                for half in range(2):
                    bank = 2 * (a % 2) + half
                    if not first or a >= 2:
                        pe.wait_ge(keyw_out, i * 8 + (2 * a + half - 3))
                    for k in range(4):
                        mm = nc.tensor.matmul(F[bank][:, k * P:(k + 1) * P],
                                              wqT[a % 2][:, (half * 4 + k) * P:(half * 4 + k + 1) * P],
                                              skT[:, bass.ds(i * (4 * NK) + a * NK, NK)], start=True, stop=True)
                    mm.then_inc(keyw_mm, 1)

            def token_transposes(c, n, first, rows=P):
                pe.wait_ge(xn_ready, n + 1)
                if not first:
                    pe.wait_ge(xn_out, n - 1)
                for k in range(KC):
                    t = T(TB[c][:, k * P:k * P + rows], xa[c][0:rows, k * P:(k + 1) * P], rows)
                t.then_inc(xn_T, 1)

            def weights_and_tokens(i, first):
                for a in range(4):
                    key_weights(i, a, first)
                for c in range(2):
                    token_transposes(c, i * 2 + c, first)

            weights_and_tokens(0, True)
            with pe.Fori(1, NB // 2) as i:
                weights_and_tokens(i, False)
            token_transposes(0, NB, False, NS)

            def project(t, first):
                for c in range(2):
                    pe.wait_ge(ld_w[c], t * 16 + 16)
                    for i in range(NB + 1):
                        tile = c * (NB + 1) + i
                        rows = P if i < NB else NS
                        if not first or tile >= STG:
                            pe.wait_ge(pj_out, t * (2 * (NB + 1)) + (tile - STG + 1))
                        for k in range(KC):
                            mm = nc.tensor.matmul(F[tile % STG][0:rows, 0:CW], xTall[:, k, i * P:i * P + rows],
                                                  wbuf[c][:, k, :], start=(k == 0), stop=(k == KC - 1))
                        mm.then_inc(pj_mm, 1)

            pe.wait_ge(xn_out, NB + 1)
            project(0, True)
            with pe.Fori(1, NCH // 2) as t:
                project(t, False)

            pe.wait_ge(pj_out, NCH * (NB + 1))
            pe.wait_ge(roped, 2)
            for j in range(8):
                T(F[0][:, j * NS:(j + 1) * NS], proj[0:NS, j * P:(j + 1) * P], NS)
            for j in range(4):
                t = T(F[0][:, 64 + j * NS:64 + (j + 1) * NS], proj[0:NS, C_QS + j * P:C_QS + (j + 1) * P], NS)
            t.then_inc(sm["qT"], 1)
            for s in range(NS):
                t = T(FF(1, 3)[:, s * P:(s + 1) * P], kw[:, s, :])
            t.then_inc(sm["kwT"], 1)
            pe.wait_ge(sm["qT_out"], 1)
            pe.wait_ge(sm["kwT_out"], 1)
            sq = sT[:, 64:96].rearrange("p (i s) -> p i s", i=GRP)
            for s in range(NS):
                for j in range(KVH):
                    mm = nc.tensor.matmul(F[3 + j][:, s * GRP:(s + 1) * GRP],
                                          kwT[j * SD:(j + 1) * SD, s * P:(s + 1) * P],
                                          sq[j * SD:(j + 1) * SD, :, s], start=True, stop=True)
            mm.then_inc(sm["s"], 1)
            for hh in range(RH):
                for s in range(NS):
                    mm = nc.tensor.matmul(F[5][:, hh * NS + s:hh * NS + s + 1], st_s[:, s, hh, :],
                                          sT[:, hh * NS + s:hh * NS + s + 1], start=True, stop=True)
            mm.then_inc(sm["qS"], 1)
            pe.wait_ge(sm["s_out"], 1)
            T(F[0][0:64, 0:P], ss).then_inc(sm["sr"], 1)
            pe.wait_ge(sm["qS_out"], 1)
            for hh in range(RH):
                t = T(F[1][0:NS, hh * P:(hh + 1) * P], osT[:, hh * NS:(hh + 1) * NS])
            t.then_inc(sm["qSn"], 1)
            pe.wait_ge(sm["p"], 1)
            T(F[2][:, 0:64], sr[0:64, :], 64).then_inc(sm["pT"], 1)
            pe.wait_ge(sm["pT_out"], 1)
            ov = F[3][:, 0:32].rearrange("p (c s) -> p c s", c=4)
            pv = pts.rearrange("p (s j a b) -> p s j a b", s=NS, j=KVH, a=2)
            for s in range(NS):
                for j in range(KVH):
                    for half in range(2):
                        mm = nc.tensor.matmul(ov[half * SD:(half + 1) * SD, 2 * j:2 * j + 2, s],
                                              vw[:, s, j * SD:(j + 1) * SD], pv[:, s, j, :, half],
                                              start=True, stop=True)
            mm.then_inc(sm["o"], 1)
            for s in range(NS):
                if s >= 2:
                    pe.wait_ge(sm["vb_used"], s - 1)
                nc.tensor.matmul(F[4 + s % 2], sel8[0:NS, s * P:(s + 1) * P], proj[0:NS, C_V:C_V + 512],
                                 start=True, stop=True).then_inc(sm["vb"], 1)
            pe.wait_ge(sm["mixr"], 1)
            for hh in range(RH):
                t = T(F[0][:, hh * NS:(hh + 1) * NS], proj[0:NS, C_MIX + hh * P:C_MIX + (hh + 1) * P], NS)
            t.then_inc(sm["mixT"], 1)

            def transposes(b):
                pe.wait_ge(roped, b * 2 + 4)
                for j in range(8):
                    t = T(FF(0, 2)[:, j * P:(j + 1) * P], proj[:, j * P:(j + 1) * P])
                t.then_inc(qkT_mm, 1)
                for j in range(4):
                    T(F[2][:, j * P:(j + 1) * P], proj[:, C_QS + j * P:C_QS + (j + 1) * P])
                T(F[3][:, 0:P], proj[:, C_KS:C_VS]).then_inc(qsT_mm, 1)

            def retention_scores(b):
                pe.wait_ge(qkT_out, b + 1)
                for hh in range(RH):
                    mm = nc.tensor.matmul(F[0][:, hh * P:(hh + 1) * P], xT[:, 512 + hh * P:512 + (hh + 1) * P],
                                          xT[:, hh * P:(hh + 1) * P], start=True, stop=True)
                mm.then_inc(st_mm, 1)
                pe.wait_ge(qsT_out, b + 1)
                for hh in range(RH):
                    nc.tensor.matmul(F[3][:, hh * P:(hh + 1) * P], xT[:, hh * P:(hh + 1) * P], state[:, hh, :],
                                     start=True, stop=True)
                pe.wait_ge(kd_ready, b + 1)
                for hh in range(RH):
                    nc.tensor.matmul(F[4][:, hh * P:(hh + 1) * P], x2[:, 512 + hh * P:512 + (hh + 1) * P],
                                     proj[:, C_V + hh * P:C_V + (hh + 1) * P], start=True, stop=True)

            def retention_values(b):
                pe.wait_ge(stm_ready, b + 1)
                for hh in range(RH):
                    mm = nc.tensor.matmul(F[5][:, hh * P:(hh + 1) * P], x2[:, hh * P:(hh + 1) * P],
                                          proj[:, C_V + hh * P:C_V + (hh + 1) * P], start=True, stop=True)
                mm.then_inc(ret_mm, 1)

            def window_scores(b):
                pe.wait_ge(mixr_ready, b + 1)
                for j in range(KVH):
                    for i in range(GRP):
                        bank = F[2 + 2 * j + i // 2]
                        mm = nc.tensor.matmul(bank[:, i % 2 * 256:i % 2 * 256 + 256],
                                              qsT[j * SD:(j + 1) * SD, i * P:(i + 1) * P],
                                              kTb[j * SD:(j + 1) * SD, :], start=True, stop=True)
                mm.then_inc(sw_mm, 1)

            def window_transposes(b):
                pe.wait_ge(sw_exp, b + 1)
                for j in range(KVH):
                    for q in range(8):
                        t = T(FF(2 * j, 2 * j + 2)[:, q * P:(q + 1) * P],
                              work[:, j * D + q * P:j * D + (q + 1) * P])
                    t.then_inc(pT_mm, 1)

            def window_values(b):
                pe.wait_ge(pT_out, b * 2 + 2)
                for j in range(KVH):
                    for i in range(GRP):
                        o = F[4][:, (j * GRP + i) * SD:(j * GRP + i + 1) * SD]
                        pT = work[:, j * D + i * 256:j * D + (i + 1) * 256]
                        nc.tensor.matmul(o, pT[:, 0:P], vprev[:, j * SD:(j + 1) * SD], start=True, stop=False)
                        mm = nc.tensor.matmul(o, pT[:, P:2 * P], proj[:, C_VS + j * SD:C_VS + (j + 1) * SD],
                                              start=False, stop=True)
                mm.then_inc(sw_o, 1)

            def mix_transposes(b):
                pe.wait_ge(mixs_ready, b + 1)
                for k in range(KC):
                    t = T(FF(0, 2)[:, k * P:(k + 1) * P], proj[:, C_MIX + k * P:C_MIX + (k + 1) * P])
                t.then_inc(mixT_mm, 1)

            def output_projection(b, n, rows=P):
                if rows == P and n == 0:
                    pe.wait_ge(mixT_out, b + 1)
                for k in range(KC):
                    lhsT = xT[:, k * P:(k + 1) * P] if rows == P else mixTs[:, k * NS:(k + 1) * NS]
                    mm = nc.tensor.matmul(F[2 + n][0:rows, :], lhsT, wo[:, k, n * 512:(n + 1) * 512],
                                          start=(k == 0), stop=(k == KC - 1))
                mm.then_inc(o_mm, 1)

            def token_transposes2(b, rows=P):
                pe.wait_ge(x2_ready, b + 1)
                for k in range(KC):
                    t = T(FF(0, 2)[:, k * P:k * P + rows], x2[0:rows, k * P:(k + 1) * P], rows)
                t.then_inc(x2T_mm, 1)

            def key_scores(b, n, rows=P):
                if n == 0:
                    pe.wait_ge(x2T_out, b + 1)
                for k in range(KC):
                    mm = nc.tensor.matmul(F[2 + n][0:rows, :], xT[:, k * P:k * P + rows],
                                          keyw[:, k, n * 512:(n + 1) * 512],
                                          start=(k == 0), stop=(k == KC - 1))
                mm.then_inc(sc_mm, 1)

            def front_mid(step, b, rows=P):
                if step == 9:
                    output_projection(b, 1, rows)
                elif step == 11:
                    key_scores(b, 1, rows)
                elif step == 12:
                    key_scores(b, 3, rows)

            def front(step, b, rows=P):
                if step == 1:
                    transposes(b)
                elif step == 2:
                    retention_scores(b)
                elif step == 3:
                    retention_values(b)
                elif step == 4:
                    window_scores(b)
                elif step == 5:
                    window_transposes(b)
                elif step == 6:
                    window_values(b)
                elif step == 7:
                    mix_transposes(b)
                elif step == 8:
                    output_projection(b, 0, rows)
                elif step == 9:
                    token_transposes2(b, rows)
                elif step == 10:
                    key_scores(b, 0, rows)
                elif step == 11:
                    key_scores(b, 2, rows)

            def add_residual(b):
                for n in range(2):
                    mm = nc.tensor.matmul(acc[:, n * 512:(n + 1) * 512], ident[:], h[:, n * 512:(n + 1) * 512],
                                          start=True, stop=False, skip_group_check=True)
                mm.then_inc(residual_in, 1)

            def add_experts(b, g, pairs=range(PAIRS)):
                for p in pairs:
                    pe.wait_ge(diags, b * (GROUPS * PAIRS) + (g * PAIRS + p + 1))
                    for r in range(p * PAIR, (p + 1) * PAIR):
                        for n in range(2):
                            mm = nc.tensor.matmul(acc[:, n * 512:(n + 1) * 512], row_u[r][:, 0:P],
                                                  row_v[r][:, n * 512:(n + 1) * 512],
                                                  start=False, stop=False, skip_group_check=True)
                        mm.then_inc(used, 1)

            pe.wait_ge(sm["mixT_out"], 1)
            pe.wait_ge(zeroed, 1)
            pe.wait_ge(ld_wo, 16)
            for step in range(1, GROUPS):
                front_mid(step, 0)
                front(step, 0)
            add_residual(0)
            add_experts(0, 0)
            with pe.Fori(0, NB - 1) as b:
                for g in range(1, GROUPS):
                    add_experts(b, g, range(0, 2))
                    front_mid(g, b + 1)
                    add_experts(b, g, range(2, PAIRS))
                    front(g, b + 1)
                pe.wait_ge(acc_out, b + 1)
                add_residual(b + 1)
                add_experts(b + 1, 0)
            for g in range(1, GROUPS):
                add_experts(NB - 1, g)
                if g >= SAMPLE_STEP:
                    front_mid(g + 8 - SAMPLE_STEP, NB, NS)
                    front(g + 8 - SAMPLE_STEP, NB, NS)
            pe.wait_ge(sm["spread"], 1)
            pe.wait_ge(sm["sel"], 32)
            spread = qsT[0:NS, 0:P]
            for n in range(2):
                nc.tensor.matmul(F[n], spread, x2[0:NS, n * 512:(n + 1) * 512], start=True, stop=True)
            nc.tensor.matmul(F[2][:, 0:P], spread, xT[0:NS, 0:P], start=True, stop=True)
            nc.tensor.matmul(F[2][:, P:2 * P], spread, gates[0:NS, :], start=True, stop=True
                             ).then_inc(sm["rowsx"], 1)
            pe.wait_ge(acc_out, NB)
            for n in range(2):
                mm = nc.tensor.matmul(acc[0:NS, n * 512:(n + 1) * 512], ident[0:NS, 0:NS],
                                      h[0:NS, n * 512:(n + 1) * 512], start=True, stop=False, skip_group_check=True)
            mm.then_inc(residual_in, 1)
            for p in range(PAIRS):
                pe.wait_ge(diags, NB * GROUPS * PAIRS + p + 1)
                for r in range(p * PAIR, (p + 1) * PAIR):
                    for n in range(2):
                        mm = nc.tensor.matmul(acc[0:NS, n * 512:(n + 1) * 512], row_u[r][:, 0:NS],
                                              row_v[r][:, n * 512:(n + 1) * 512],
                                              start=False, stop=(r == RING - 1), skip_group_check=True)
                    mm.then_inc(used, 1)

        @block.scalar
        def _(act):
            me = Steps(act, act_steps)

            def copy(o, i, **kw_):
                return nc.scalar.activation(o, i, ACT.Copy, **kw_)

            roots = Steps(act, root_in)

            def root(o):
                roots.n += 1
                roots.sync()
                nc.scalar.activation(o, o, ACT.Sqrt).then_inc(root_out, 1)

            def keyw_copy(i, a, half):
                hold(act, keyw_mm, i * 8 + (2 * a + half + 1))
                o = keyw[:, half * 4:half * 4 + 4, bass.ds(i * (4 * NK) + a * NK, NK)]
                copy(o, F[2 * (a % 2) + half].rearrange("p (k n) -> p k n", k=4)).then_inc(keyw_out, 1)

            with act.Fori(0, NB // 2) as i:
                roots.enter(i, 2)
                root(hs2)
                root(fs2)
                for a in range(4):
                    for half in range(2):
                        keyw_copy(i, a, half)
                roots.leave(NB // 2)
            root(hs2[0:NS, :])

            def tiles(t, first):
                for tile in range(2 * (NB + 1)):
                    rows = P if tile % (NB + 1) < NB else NS
                    act.wait_ge(pj_mm, t * (2 * (NB + 1)) + tile + 1)
                    if not first or tile >= STG:
                        act.wait_ge(st_pj[tile % STG], t * (16 * 3) + 16 * (tile // STG))
                    copy(staging[tile % STG][0:rows, :], F[tile % STG][0:rows, 0:CW]).then_inc(pj_out, 1)

            act.wait_ge(xn_out, NB + 1)
            tiles(0, True)
            with act.Fori(1, NCH // 2) as t:
                tiles(t, False)

            act.wait_ge(sm["qT"], 1)
            copy(sT, F[0][:, 0:96]).then_inc(sm["qT_out"], 1)
            act.wait_ge(sm["kwT"], 1)
            copy(kwT, FF(1, 3)).then_inc(sm["kwT_out"], 1)
            act.wait_ge(sm["s"], 1)
            sv = ss.rearrange("p (s j i) -> p j s i", s=NS, j=KVH)
            for j in range(KVH):
                me.did(copy(sv[:, j], F[3 + j][:, 0:32].rearrange("p (s i) -> p s i", s=NS), scale=S_SCALE))
            me.sync()
            act.nop(nofuse=True).then_inc(sm["s_out"], 1)
            act.wait_ge(sm["qS"], 1)
            copy(osT, F[5][:, 0:32]).then_inc(sm["qS_out"], 1)
            act.wait_ge(sm["nmax"], 1)
            me.did(nc.scalar.activation(sr[0:64, :], sr[0:64, :], ACT.Exp, bias=n64[0:64, :], accum_out=r64[0:64, :]))
            nc.scalar.activation(e64[0:64, :], sinks64[0:64, :], ACT.Exp, bias=n64[0:64, :]).then_inc(sm["exp"], 1)
            act.wait_ge(sm["silu"], 1)
            nc.scalar.activation(x2[0:NS, 512:1024], proj[0:NS, C_G:C_G + 512], ACT.Silu).then_inc(silu_ready, 1)
            root(rstd[0:NS, :])
            act.wait_ge(sm["pT"], 1)
            copy(pts, F[2][:, 0:64]).then_inc(sm["pT_out"], 1)
            act.wait_ge(sm["o"], 1)
            me.did(copy(mixTs[:, 32:64], F[3][:, 0:32]))
            act.wait_ge(sm["mixT"], 1)
            me.did(copy(mixTs[:, 0:32], F[0][:, 0:32]))
            me.sync()
            act.nop(nofuse=True).then_inc(sm["mixT_out"], 1)

            def transposes_out(b):
                act.wait_ge(qkT_mm, b + 1)
                copy(xT, FF(0, 2)).then_inc(qkT_out, 1)
                act.wait_ge(qsT_mm, b + 1)
                me.did(copy(kTb[:, 0:P], kTb[:, P:2 * P]))
                me.sync()
                me.did(copy(kTb[:, P:2 * P], F[3][:, 0:P]))
                copy(qsT[:], F[2]).then_inc(qsT_out, 1)

            def silu(b):
                act.wait_ge(ret_mm, b + 1)
                nc.scalar.activation(x2[:, 0:512], proj[:, C_G:C_G + 512], ACT.Silu).then_inc(silu_ready, 1)
                root(rstd)

            def window_exp(b):
                act.wait_ge(sw_nmax, b + 1)
                for q in range(QH):
                    me.did(nc.scalar.activation(work[:, q * 256:(q + 1) * 256], work[:, q * 256:(q + 1) * 256],
                                                ACT.Exp, bias=nmx[:, q:q + 1], accum_out=rs[:, q:q + 1]))
                nc.scalar.activation(es, es, ACT.Exp).then_inc(sw_exp, 1)

            def probs_out(b):
                for j in range(KVH):
                    act.wait_ge(pT_mm, b * 2 + (j + 1))
                    copy(work[:, j * D:(j + 1) * D], FF(2 * j, 2 * j + 2)).then_inc(pT_out, 1)

            def mix_out(b):
                act.wait_ge(sw_o, b + 1)
                copy(vprev[:], proj[:, C_VS:D_IN])
                act.wait_ge(mixT_mm, b + 1)
                copy(xT, FF(0, 2)).then_inc(mixT_out, 1)

            def tokens_out(b, rows=P):
                act.wait_ge(x2T_mm, b + 1)
                src, dst = FF(0, 2), xT
                if rows < P:
                    src = src.rearrange("p (k t) -> p k t", k=KC)[:, :, 0:rows]
                    dst = dst.rearrange("p (k t) -> p k t", k=KC)[:, :, 0:rows]
                copy(dst, src).then_inc(x2T_out, 1)

            def scores_out(b, half, rows=P):
                act.wait_ge(sc_mm, b * 4 + (2 * half + 2))
                copy(proj[0:rows, half * D:(half + 1) * D], FF(2 + 2 * half, 4 + 2 * half)[0:rows, :]
                     ).then_inc(sc_out, 1)

            def gates_exp(b, half, rows=P):
                act.wait_ge(best_shift, b * 2 + (half + 1))
                part_ = gates[0:rows, half * HALF:(half + 1) * HALF]
                nc.scalar.activation(part_, part_, ACT.Exp).then_inc(best_exp, 1)

            def front(step, b, rows=P):
                if step == 2:
                    transposes_out(b)
                elif step == 4:
                    silu(b)
                elif step == 5:
                    window_exp(b)
                elif step == 6:
                    probs_out(b)
                elif step == 8 and rows == P:
                    mix_out(b)
                elif step == 9:
                    root(hs2[0:rows, :])
                elif step == 10:
                    tokens_out(b, rows)
                elif step == 11:
                    scores_out(b, 0, rows)
                elif step == 12:
                    scores_out(b, 1, rows)
                    gates_exp(b, 0, rows)
                elif step == 14:
                    gates_exp(b, 1, rows)

            def expert_gelus(b, g):
                for p in range(PAIRS):
                    act.wait_ge(dots, b * (GROUPS * PAIRS) + (g * PAIRS + p + 1))
                    nc.scalar.activation(gel[:, p * PAIR:(p + 1) * PAIR], dot[:, p * PAIR:(p + 1) * PAIR],
                                         ACT.Gelu).then_inc(gelus, 1)

            def sum_out(b):
                act.wait_ge(topk_done, b * 2 + 4)
                act.nop(nofuse=True)
                act.wait_ge(used, b * SLOTS + (SLOTS + RING))
                copy(xT, acc).then_inc(acc_out, 1)

            for step in range(1, GROUPS):
                front(step, 0)
            expert_gelus(0, 0)
            with act.Fori(0, NB - 1) as b:
                me.enter(b, 2 + QH)
                roots.enter(b, 3)
                for g in range(1, GROUPS):
                    expert_gelus(b, g)
                    front(g, b + 1)
                sum_out(b)
                expert_gelus(b + 1, 0)
                root(fs2)
                me.leave(NB - 1)
                roots.leave(NB - 1)
            for g in range(1, GROUPS):
                expert_gelus(NB - 1, g)
                if g >= SAMPLE_STEP:
                    front(g + 8 - SAMPLE_STEP, NB, NS)
            act.wait_ge(sm["rowsx"], 1)
            sum_out(NB - 1)
            root(fs2)
            expert_gelus(NB, 0)
            root(fs2[0:NS, :])

        @block.vector
        def _(v):
            me, roots = Steps(v, dve_steps), Steps(v, root_out)
            tt = nc.vector.tensor_tensor
            stt = nc.vector.scalar_tensor_tensor
            ts = nc.vector.tensor_scalar

            def tell(sem_, n=1):
                v.nop(nofuse=True).then_inc(sem_, n)

            me.did(nc.vector.memset(state[:], 0.0))
            me.did(nc.vector.memset(kTb[:], 0.0))
            me.did(nc.vector.memset(vprev[:], 0.0))
            me.sync()
            tell(zeroed, 1)
            tell(used, RING)

            def root(o, i, scale):
                ts(o, i, scale, EPS, ALU.mult, ALU.add).then_inc(root_in, 1)
                roots.n += 1
                roots.sync()
                me.did(nc.vector.reciprocal(o, o))
                me.sync()

            def norm_tokens(c, i, rows=P):
                v.wait_ge(ld_x[c], (i // 2 if isinstance(i, int) else i) * 16 + 16)
                xv = xa[c][0:rows, :]
                total, root_ = ((hs1, hs2), (fs1, fs2))[c]
                me.did(stt(work[0:rows, 0:D], xv, 1.0, xv, ALU.mult, ALU.mult, accum_out=total[0:rows, :]))
                me.sync()
                root(root_[0:rows, :], total[0:rows, :], 1.0 / D)
                ts(xv, xv, root_[0:rows, :], None, ALU.mult).then_inc(xn_ready, 1)

            def out_tokens(c, i, n, rows=P):
                v.wait_ge(xn_T, n + 1)
                v.nop(nofuse=True)
                for k in range(KC):
                    dst = xTall[:, k, bass.ds(i * (2 * P) + c * P, rows)]
                    ins = ts(dst, (acc, FF(4, 6))[c][:, k * P:k * P + rows], g1c[:, k:k + 1], None, ALU.mult)
                ins.then_inc(xn_out, 1)

            v.wait_ge(ld_const, 16 * N_CONST)
            with v.Fori(0, NB // 2) as i:
                me.enter(i, 4)
                roots.enter(i, 2)
                for c in range(2):
                    norm_tokens(c, i)
                for c in range(2):
                    out_tokens(c, i, i * 2 + c)
                me.leave(NB // 2)
                roots.leave(NB // 2)
            norm_tokens(0, NB, NS)
            out_tokens(0, NB // 2, NB, NS)

            def rotate(rows):
                qk4 = proj[0:rows, 0:1024].rearrange("p (c h d t) -> p c h d t", c=2, h=RH, t=2)
                tab = rope[0:rows, :].rearrange("p (c f d) -> p c f d", c=2, f=2)
                t1 = work[0:rows, :].rearrange("p (n c h d) -> p n c h d", n=4, c=2, h=RH)
                for n, (half, trig) in enumerate(((0, 0), (1, 1), (0, 1), (1, 0))):
                    for c in range(2):
                        me.did(tt(t1[:, n, c], qk4[:, c, :, :, half],
                                  tab[:, c, trig, :].rearrange("p (a d) -> p a d", a=1).to_broadcast([rows, RH, 64]),
                                  ALU.mult))
                me.sync()
                for half, (a, b_, op) in enumerate(((0, 1, ALU.subtract), (2, 3, ALU.add))):
                    for c in range(2):
                        ins = tt(qk4[:, c, :, :, half], t1[:, a, c], t1[:, b_, c], op)
                        if c == 0:
                            me.did(ins)
                        else:
                            ins.then_inc(roped, 1)

            def gated_norm(rows, o, sq, silu, wait):
                ov = o.rearrange("p (h e) -> p h e", h=RH)
                me.did(tt(sq, o, o, ALU.mult))
                me.sync()
                me.did(nc.vector.tensor_reduce(ssq[0:rows, :], sq.rearrange("p (h e) -> p h e", h=RH), AX, ALU.add))
                me.sync()
                root(rstd[0:rows, :], ssq[0:rows, :], 1.0 / HD)
                me.did(tt(ov, ov, rstd[0:rows, :].rearrange("p (h a) -> p h a", a=1).to_broadcast([rows, RH, HD]),
                          ALU.mult))
                v.wait_ge(silu_ready, wait)
                v.nop(nofuse=True)
                me.sync()
                return tt(proj[0:rows, C_MIX:C_MIX + 512], o, silu, ALU.mult)

            v.wait_ge(sm["kw"], 16 * (2 + 2 * NS + 5))
            rotate(NS)
            v.wait_ge(sm["sr"], 1)
            s64, sp64 = F[0][0:64, 0:P], sr[0:64, :]
            me.did(nc.vector.tensor_copy(sp64, s64))
            me.did(nc.vector.tensor_reduce(m64[0:64, :], s64, AX, ALU.max))
            me.sync()
            me.did(tt(m64[0:64, :], m64[0:64, :], sinks64[0:64, :], ALU.max))
            me.sync()
            ts(n64[0:64, :], m64[0:64, :], -1.0, None, ALU.mult).then_inc(sm["nmax"], 1)
            v.wait_ge(sm["exp"], 1)
            me.did(tt(m64[0:64, :], r64[0:64, :], e64[0:64, :], ALU.add))
            me.sync()
            me.did(nc.vector.reciprocal(m64[0:64, :], m64[0:64, :]))
            me.sync()
            ts(sp64, sp64, m64[0:64, :], None, ALU.mult).then_inc(sm["p"], 1)
            prod = work[0:NS, 1024:1536]
            me.did(tt(prod, proj[0:NS, C_Q:C_Q + 512], proj[0:NS, C_K:C_K + 512], ALU.mult))
            me.sync()
            me.did(nc.vector.tensor_reduce(qk[0:NS, :], prod.rearrange("p (h e) -> p h e", h=RH), AX, ALU.add))
            me.sync()
            tell(sm["silu"])
            o_s = work[0:NS, 0:512]
            v.wait_ge(sm["qSn"], 1)
            for hh in range(RH):
                me.did(ts(prod[:, hh * P:(hh + 1) * P], F[1][0:NS, hh * P:(hh + 1) * P], STEP_DECAY[hh], None,
                          ALU.mult))
            me.sync()
            for hh in range(RH):
                me.did(stt(o_s[:, hh * P:(hh + 1) * P], proj[0:NS, C_V + hh * P:C_V + (hh + 1) * P],
                           qk[0:NS, hh:hh + 1], prod[:, hh * P:(hh + 1) * P], ALU.mult, ALU.add))
            me.sync()
            gated_norm(NS, o_s, prod, x2[0:NS, 512:1024], 1).then_inc(sm["mixr"], 1)
            v.wait_ge(sm["qS_out"], 1)
            for hh in range(RH):
                me.did(ts(st_s[:, :, hh, :], st_s[:, :, hh, :], STEP_DECAY[hh], None, ALU.mult))
            me.sync()
            for s in range(NS):
                v.wait_ge(sm["vb"], s + 1)
                for hh in range(RH):
                    me.did(stt(st_s[:, s, hh, :], F[4 + s % 2][:, hh * P:(hh + 1) * P],
                               sT[:, 32 + hh * NS + s:33 + hh * NS + s], st_s[:, s, hh, :], ALU.mult, ALU.add))
                me.sync()
                tell(sm["vb_used"])
            tell(sm["st"])

            def rotation(b):
                v.wait_ge(ld_proj, b * 32 + 32)
                v.nop(nofuse=True)
                rotate(P)
                v.wait_ge(roped, b * 2 + 4)
                tt(x2[:, 512:1024].rearrange("p (h e) -> p h e", h=RH),
                   proj[:, C_K:C_K + 512].rearrange("p (h e) -> p h e", h=RH),
                   kdec.rearrange("p (h a) -> p h a", a=1).to_broadcast([P, RH, HD]), ALU.mult).then_inc(kd_ready, 1)

            def decay_scores(b):
                v.wait_ge(st_mm, b + 1)
                tt(x2[:, 0:512], F[0], dmaskT[:].rearrange("p h m -> p (h m)"), ALU.mult).then_inc(stm_ready, 1)

            def retention_out(b):
                v.wait_ge(ret_mm, b + 1)
                o = xT[:, 0:512]
                me.did(tt(o.rearrange("p (h e) -> p h e", h=RH), F[3].rearrange("p (h e) -> p h e", h=RH),
                          qdec.rearrange("p (h a) -> p h a", a=1).to_broadcast([P, RH, HD]), ALU.mult))
                for hh in range(RH):
                    me.did(stt(state[:, hh, :], state[:, hh, :], BLOCK_DECAY[hh], F[4][:, hh * P:(hh + 1) * P],
                               ALU.mult, ALU.add))
                me.sync()
                me.did(tt(o, o, F[5], ALU.add))
                me.sync()
                gated_norm(P, o, xT[:, 512:1024], x2[:, 0:512], b + 2).then_inc(mixr_ready, 1)

            def window_max(b, mask):
                v.wait_ge(sw_mm, b + 1)
                v.nop(nofuse=True)
                v.wait_ge(mixr_ready, b + 1)
                s3 = work[:].rearrange("p (q s) -> p q s", q=QH)
                me.did(stt(s3, FF(2, 6).rearrange("p (q s) -> p q s", q=QH), S_SCALE,
                           mask.rearrange("p (a s) -> p a s", a=1).to_broadcast([P, QH, 2 * P]), ALU.mult, ALU.add))
                me.sync()
                me.did(nc.vector.tensor_reduce(mx, s3, AX, ALU.max))
                me.sync()
                me.did(tt(mx, mx, sinkb, ALU.max))
                me.sync()
                me.did(tt(es, sinkb, mx, ALU.subtract))
                me.sync()
                ts(nmx, mx, -1.0, None, ALU.mult).then_inc(sw_nmax, 1)

            def window_out(b):
                v.wait_ge(sw_exp, b + 1)
                me.did(tt(rden, rs, es, ALU.add))
                me.sync()
                me.did(nc.vector.reciprocal(rden, rden))
                v.wait_ge(sw_o, b + 1)
                v.nop(nofuse=True)
                me.sync()
                tt(proj[:, C_MIX + 512:C_MIX + 1024].rearrange("p (q d) -> p q d", q=QH),
                   F[4].rearrange("p (q d) -> p q d", q=QH),
                   rden.rearrange("p (q a) -> p q a", a=1).to_broadcast([P, QH, SD]), ALU.mult
                   ).then_inc(mixs_ready, 1)

            def norm_output(b, rows=P):
                v.wait_ge(ld_res, b * 16 + 16)
                v.nop(nofuse=True)
                v.wait_ge(o_mm, b * 2 + 2)
                hv, xv = h[0:rows, :], x2[0:rows, :]
                me.did(tt(hv, hv, FF(2, 4)[0:rows, :], ALU.add))
                me.sync()
                me.did(stt(xv, hv, 1.0, hv, ALU.mult, ALU.mult, accum_out=hs1[0:rows, :]))
                me.sync()
                root(hs2[0:rows, :], hs1[0:rows, :], 1.0 / D)
                stt(xv, hv, hs2[0:rows, :], g2b[0:rows, :], ALU.mult, ALU.mult).then_inc(x2_ready, 1)

            sc3 = proj[:, 0:NSC].rearrange("p (c n) -> p c n", c=NHC)
            cand8 = proj[:, 0:NSC].rearrange("p (h c) -> p h c", h=PH)
            HH = PH // 2

            def beside(at_, n, like=None):
                return proj[:, NSC + at_:NSC + at_ + n]

            vals, inds, indf = beside(0, 2 * HALF), beside(128, 2 * HALF), beside(256, 2 * HALF)
            best, posn, chosen = beside(384, HALF), beside(448, HALF), beside(512, 2 * HALF)
            ab, abf, numbers = vals, inds, beside(640, SLOTS)

            def rank(js, rowsof, v16, i16):
                for r8 in range(2):
                    for j in js:
                        me.did(nc.vector.max(v16(j)[:, r8 * 8:r8 * 8 + 8], rowsof(j)))
                    hold(v, me.sem, me.base + me.n)
                    for j in js:
                        me.did(nc.vector.max_index(i16(j)[:, r8 * 8:r8 * 8 + 8], v16(j)[:, r8 * 8:r8 * 8 + 8],
                                                   rowsof(j)))
                    hold(v, me.sem, me.base + me.n)
                    if r8 == 0:
                        for j in js:
                            me.did(nc.vector.match_replace(rowsof(j), v16(j)[:, 0:8], rowsof(j), TAKEN))
                        hold(v, me.sem, me.base + me.n)

            def rank_halves(b, half, rows=P):
                hold(v, sc_out, b * 2 + (half + 1))
                v3 = vals[0:rows].rearrange("p (c k) -> p c k", k=TK)
                i3 = inds.bitcast(U32)[0:rows].rearrange("p (c k) -> p c k", k=TK)
                rank(range(PH), lambda j: sc3[0:rows, half * PH + j, :], lambda j: v3[:, j, :],
                     lambda j: i3[:, j, :])
                for hh in range(HH):
                    me.did(tt(cand8[0:rows, half * HH + hh, :].rearrange("p (a b) -> p a b", a=TK),
                              v3[:, 2 * hh, :].rearrange("p (k a) -> p k a", a=1).to_broadcast([rows, TK, TK]),
                              v3[:, 2 * hh + 1, :].rearrange("p (a k) -> p a k", a=1).to_broadcast([rows, TK, TK]),
                              ALU.add))
                me.did(nc.vector.tensor_copy(indf[0:rows], inds.bitcast(U32)[0:rows]))
                hold(v, me.sem, me.base + me.n)

            def choose(b, half, rows=P):
                b3 = best[0:rows].rearrange("p (h k) -> p h k", h=HH)
                pu = posn.bitcast(U32)[0:rows]
                p3 = pu.rearrange("p (h k) -> p h k", h=HH)
                rank(range(HH), lambda j: cand8[0:rows, half * HH + j, :], lambda j: b3[:, j, :],
                     lambda j: p3[:, j, :])
                abu = ab.bitcast(U32)[0:rows]
                me.did(ts(abu[:, 0:HALF], pu, 4, None, ALU.logical_shift_right))
                me.did(ts(abu[:, HALF:], pu, 15, None, ALU.bitwise_and))
                g3 = gates[0:rows, half * HALF:(half + 1) * HALF].rearrange("p (h k) -> p h k", h=HH)
                tt(g3, b3, b3[:, :, 0:1].to_broadcast([rows, HH, TK]), ALU.subtract).then_inc(best_shift, 1)
                me.sync()
                me.did(nc.vector.tensor_copy(abf[0:rows], abu))
                me.sync()
                one = proj[0:rows, half * D:(half + 1) * D].rearrange("p (n a) -> p n a", a=TK)
                iot = iota16[0:rows, :].rearrange("p (a k) -> p a k", a=1).to_broadcast([rows, HALF, TK])
                i4 = indf[0:rows].rearrange("p (h c k) -> p h c k", h=HH, c=2)
                for c in range(2):
                    me.did(tt(one, abf[0:rows, c * HALF:(c + 1) * HALF].rearrange("p (n a) -> p n a", a=1)
                              .to_broadcast([rows, HALF, TK]), iot, ALU.is_equal))
                    me.sync()
                    for hh in range(HH):
                        o3 = one[:, hh * TK:(hh + 1) * TK, :]
                        me.did(tt(o3, o3, i4[:, hh, c, :].rearrange("p (a k) -> p a k", a=1)
                                  .to_broadcast([rows, TK, TK]), ALU.mult))
                    me.sync()
                    me.did(nc.vector.tensor_reduce(chosen[0:rows, c * HALF:(c + 1) * HALF], one, AX, ALU.add))
                    me.sync()
                num = numbers[0:rows, half * HALF:(half + 1) * HALF]
                me.did(stt(num, chosen[0:rows, 0:HALF], float(NK), chosen[0:rows, HALF:], ALU.mult, ALU.add))
                v.wait_ge(best_exp, b * 2 + (half + 1))
                v.nop(nofuse=True)
                me.sync()
                if not isinstance(b, int) or b > 0:
                    v.wait_ge(idx_taken, b * 2)
                me.did(nc.vector.tensor_copy(idx[0:rows, half * HALF:(half + 1) * HALF], num))
                me.did(nc.vector.tensor_reduce(ssum[0:rows, 0:HH], g3, AX, ALU.add))
                me.sync()
                me.did(nc.vector.reciprocal(srec[0:rows, 0:HH], ssum[0:rows, 0:HH]))
                me.sync()
                tt(g3, g3, srec[0:rows, 0:HH].rearrange("p (h a) -> p h a", a=1).to_broadcast([rows, HH, TK]),
                   ALU.mult).then_inc(topk_done, 1)

            def front(step, b, mask, rows=P):
                if step == 1:
                    rotation(b)
                elif step == 3:
                    decay_scores(b)
                elif step == 4:
                    retention_out(b)
                elif step == 5:
                    window_max(b, mask)
                elif step == 7:
                    window_out(b)
                elif step == 9:
                    norm_output(b, rows)
                elif step == 11:
                    rank_halves(b, 0, rows)
                elif step == 12:
                    choose(b, 0, rows)
                elif step == 13:
                    hold(v, topk_done, b * 2 + 1)
                    rank_halves(b, 1, rows)
                elif step == 14:
                    choose(b, 1, rows)

            def take_over(b):
                v.wait_ge(topk_done, b * 2 + 2)
                if not isinstance(b, int) or b > 0:
                    v.nop(nofuse=True)
                    v.wait_ge(diags, b * (GROUPS * PAIRS))
                me.did(nc.vector.tensor_copy(x2g[:], x2))
                me.did(nc.vector.tensor_copy(gateg[:], gates[:]))
                me.sync()

            def expert_dots(b, g):
                def diagonals(p):
                    v.wait_ge(gelus, b * (GROUPS * PAIRS) + (g * PAIRS + p + 1))
                    for r in range(p * PAIR, (p + 1) * PAIR):
                        ins = ts(row_u[r][:, 0:P], ident[:], gel[:, r:r + 1],
                                 gateg[:, g * RING + r:g * RING + r + 1], ALU.mult, ALU.mult)
                    ins.then_inc(diags, 1)

                for p in range(PAIRS):
                    for r in range(p * PAIR, (p + 1) * PAIR):
                        v.wait_ge(ld_row[r], b * (GROUPS * 16) + (g * 16 + 16))
                        ins = stt(row_u[r], row_u[r], 1.0, x2g[:], ALU.mult, ALU.mult, accum_out=dot[:, r:r + 1])
                    ins.then_inc(dots, 1)
                    if p:
                        diagonals(p - 1)
                diagonals(PAIRS - 1)

            def block_out(b):
                v.wait_ge(acc_out, b + 1)
                me.did(stt(x2, xT, 1.0, xT, ALU.mult, ALU.mult, accum_out=fs1))
                me.sync()
                root(fs2, fs1, 1.0 / D)
                stt(xT, xT, fs2, gfb[:], ALU.mult, ALU.mult).then_inc(y_ready, 1)

            for step in range(1, GROUPS):
                front(step, 0, mask0)
            take_over(0)
            expert_dots(0, 0)
            with v.Fori(0, NB - 1) as b:
                me.enter(b, STEPS_PER_BLOCK)
                roots.enter(b, 3)
                for g in range(1, GROUPS):
                    expert_dots(b, g)
                    front(g, b + 1, wmask[:])
                take_over(b + 1)
                expert_dots(b + 1, 0)
                block_out(b)
                me.leave(NB - 1)
                roots.leave(NB - 1)
            for g in range(1, GROUPS):
                expert_dots(NB - 1, g)
                if g >= SAMPLE_STEP:
                    front(g + 8 - SAMPLE_STEP, NB, None, NS)
                if g + 8 - SAMPLE_STEP == 15:
                    v.wait_ge(topk_done, NB * 2 + 2)
                    nc.vector.tensor_copy(xT[0:NS, 0:P], numbers[0:NS, :]).then_inc(sm["spread"], 1)
            v.wait_ge(sm["rowsx"], 1)
            xr = x2g[:]
            me.did(nc.vector.tensor_copy(xr, FF(0, 2)))
            pick = qsT[:, P:2 * P]
            both = proj[:, 0:2 * P]
            for n in range(2):
                me.did(tt(both[:, n * P:(n + 1) * P], F[2][:, n * P:(n + 1) * P], pick, ALU.mult))
            me.sync()
            me.did(nc.vector.tensor_reduce(proj[:, 256:256 + 2 * PH],
                                           both.rearrange("p (n k) -> p n k", k=TK), AX, ALU.add))
            me.sync()
            nc.vector.tensor_copy(idx[:, 0:PH], proj[:, 256:256 + PH]).then_inc(sm["idx8"], 1)
            block_out(NB - 1)
            v.wait_ge(sm["idx8"], 1)
            for p in range(PAIRS):
                for r in range(p * PAIR, (p + 1) * PAIR):
                    v.wait_ge(ld_row[r], NB * GROUPS * 16 + 16)
                    ins = stt(row_u[r], row_u[r], 1.0, xr, ALU.mult, ALU.mult, accum_out=dot[:, r:r + 1])
                ins.then_inc(dots, 1)
            own = qsT[:, 2 * P:2 * P + NS]
            for p in range(PAIRS):
                v.wait_ge(gelus, NB * GROUPS * PAIRS + p + 1)
                for r in range(p * PAIR, (p + 1) * PAIR):
                    ins = ts(row_u[r][:, 0:NS], own, gel[:, r:r + 1], proj[:, 256 + PH + r:257 + PH + r],
                             ALU.mult, ALU.mult)
                ins.then_inc(diags, 1)
            v.wait_ge(used, NB * SLOTS + 2 * RING)
            ys = work[0:NS, 0:D]
            me.did(nc.vector.tensor_copy(ys, acc[0:NS, :]))
            me.sync()
            me.did(stt(row_u[0][0:NS, :], ys, 1.0, ys, ALU.mult, ALU.mult, accum_out=fs1[0:NS, :]))
            me.sync()
            root(fs2[0:NS, :], fs1[0:NS, :], 1.0 / D)
            stt(ys, ys, fs2[0:NS, :], gfb[0:NS, :], ALU.mult, ALU.mult).then_inc(y_ready, 1)


SAMPLE_STEP = 4
STEPS_PER_BLOCK = 201


_INS = ["x_prompt", "x_sample", "state_ret", "cache_swa_k", "cache_swa_v", "norm1_g", "swa_sinks", "w_out",
        "norm2_g", "final_g"]
_OUTS = [(1, SEQ, D), (NS, 1, D), (1, RH, HD, HD), (1, P, KVH, SD), (1, P, KVH, SD), (NS, RH, HD, HD),
         (NS, P, KVH, SD), (NS, P, KVH, SD)]


def constants():
    f = np.float32
    half = HD // 2
    inv = (f(1.0) / (f(10000.0) ** np.linspace(0.0, 1.0, half, dtype=f))).astype(f)
    pos = np.concatenate([np.arange(SEQ), np.full(NS, SEQ)]).astype(f)
    ang = (pos[:, None] * inv[None, :]).astype(f).astype(np.float64)
    cos, sin = np.cos(ang), np.sin(ang)
    t = np.arange(P)
    diff = t[None, :] - t[:, None]
    dmask = np.where(diff[:, None, :] >= 0, np.exp(np.maximum(diff, 0)[:, None, :] * LOG_DECAY[None, :, None]), 0.0)
    prev = np.where(t[None, :] > t[:, None], 0.0, MASKED)
    cur = np.where(t[None, :] <= t[:, None], 0.0, MASKED)
    s8, p16 = np.arange(NS), t // TK
    pick = np.tile(t[:, None] % TK == np.arange(TK)[None, :], (1, PH))
    out = {
        "c_rope": np.concatenate([cos, sin, cos * K_SCALE, sin * K_SCALE], 1),
        "c_ident": np.eye(P),
        "c_dmaskT": dmask.reshape(P, RH * P),
        "c_qdec": np.exp((t[:, None] + 1.0) * LOG_DECAY[None, :]),
        "c_kdec": np.exp((P - 1.0 - t[:, None]) * LOG_DECAY[None, :]),
        "c_iota": np.tile(np.arange(TK), (P, 1)),
        "c_wmask": np.concatenate([prev, cur], 1),
        "c_wmask0": np.concatenate([np.full((P, P), MASKED), cur], 1),
        "c_sel8": np.repeat(np.eye(NS), P, axis=1),
        "c_spread": (s8[:, None] == p16[None, :]),
        "c_pick": np.concatenate([pick, p16[:, None] == s8[None, :]], 1),
    }
    return {k: np.ascontiguousarray(v.astype(f)) for k, v in out.items()}


def kernel(**inputs):
    import concourse.bacc as _bacc
    from concourse.bass_utils import run_bass_kernel_spmd as _run

    nc = _bacc.Bacc("TRN2", target_bir_lowering=False, num_devices=1)
    arrays = {n: np.ascontiguousarray(inputs[n]) for n in _INS}
    w_in = np.asarray(inputs["w_in"])
    qs = w_in[:, C_QS:C_KS].reshape(D, KVH, GRP, SD).transpose(0, 2, 1, 3).reshape(D, QH * SD)
    arrays["w_in"] = np.concatenate([w_in[:, :C_QS], qs, w_in[:, C_KS:]], axis=1)
    arrays["wqT"] = np.ascontiguousarray(np.asarray(inputs["peer_w_q"]).reshape(D, NHC, NK).transpose(1, 2, 0))
    arrays["sub_keysT"] = np.ascontiguousarray(
        np.asarray(inputs["peer_sub_keys"]).transpose(3, 0, 1, 2).reshape(NK, NSC))
    arrays["peer_uv"] = np.concatenate([np.asarray(inputs["peer_u"]), np.asarray(inputs["peer_v"])], axis=1)
    arrays.update(constants())
    args = {n: nc.dram_tensor("in_" + n, a.shape, mybir.dt.from_np(a.dtype), kind="ExternalInput").ap()
            for n, a in arrays.items()}
    outs = [nc.dram_tensor(f"out_{i}", shape, F32, kind="ExternalOutput").ap() for i, shape in enumerate(_OUTS)]
    build(nc, args, outs)
    r = _run(nc, [{"in_" + n: a for n, a in arrays.items()}], core_ids=[0])
    return tuple(r.results[0][f"out_{i}"] for i in range(len(_OUTS)))
```

```python
from contextlib import ExitStack

import numpy as np

import concourse.bass as bass
from concourse import mybir

F32 = mybir.dt.float32
U32 = mybir.dt.uint32
ALU = mybir.AluOpType
ACT = mybir.ActivationFunctionType
AX = mybir.AxisListType.X

P = 128
D = 1024
KC = D // P
SEQ = 1024
NB = SEQ // P
NS = 8
NTOK = SEQ + NS
RH, HD = 4, 128
QH, KVH, SD = 8, 2, 64
GRP = QH // KVH
D_IN = 4 * RH * HD + QH * SD + 2 * KVH * SD
C_Q, C_K, C_V, C_G = 0, 512, 1024, 1536
C_QS, C_KS, C_VS = 2048, 2560, 2688
C_MIX = C_G
PH, TK, NK = 8, 16, 128
NHC = 2 * PH
NSC = NHC * NK
SLOTS = PH * TK
HALF = SLOTS // 2
RING = 8
ROWW = 2 * D
GROUPS = SLOTS // RING
PAIR = 2
PAIRS = RING // PAIR
NCH = 8
CW = D_IN // NCH
BANKS = 6
STG = 4
TILES = NB + 1
EPS = 1e-6
K_SCALE = HD ** -0.5
S_SCALE = SD ** -0.5
LOG_DECAY = np.log(1.0 - 2.0 ** (-5.0 - np.arange(RH)))
STEP_DECAY = [float(v) for v in np.exp(LOG_DECAY)]
BLOCK_DECAY = [float(v) for v in np.exp(P * LOG_DECAY)]
MASKED = -1e30
TAKEN = -3.0e38


class Steps:

    def __init__(self, eng, sem):
        self.eng, self.sem, self.n, self.base = eng, sem, 0, 0

    def did(self, ins):
        self.n += 1
        ins.then_inc(self.sem, 1)

    def sync(self):
        self.eng.wait_ge(self.sem, self.base + self.n)

    def enter(self, turn, per):
        self.first, self.per = self.n, per
        self.base = turn * per

    def leave(self, turns):
        assert self.n - self.first == self.per, (self.n - self.first, self.per)
        self.base, self.n = 0, self.first + turns * self.per


def hold(eng, sem, count):
    eng.wait_ge(sem, count)
    eng.nop(nofuse=True)


def build(nc, A, out):
    ctx = ExitStack()
    with ctx:
        def sb(name, shape, dt=F32):
            return ctx.enter_context(nc.sbuf_tensor(name, shape, dt))

        def sem(name):
            return ctx.enter_context(nc.semaphore(name))

        ring = sb("ring", [P, RING * ROWW])
        keyw = sb("keyw", [P, KC, NSC])
        wo = sb("wo", [P, KC, D])
        proj = sb("proj", [P, D_IN])
        work = sb("work", [P, 2 * D])
        h = sb("h", [P, D])
        x2g = sb("x2g", [P, D])
        g2b = sb("g2b", [P, D])
        gfb = sb("gfb", [P, D])
        qsT = sb("qsT", [P, 512])
        kTb = sb("kTb", [P, 2 * P])
        vprev = sb("vprev", [P, P])
        state = sb("state", [P, RH, HD])
        dmaskT = sb("dmaskT", [P, RH, P])
        wmask = sb("wmask", [P, 2 * P])
        ident = sb("ident", [P, P])
        idx = sb("idx", [P, SLOTS], U32)
        gates = sb("gates", [P, SLOTS])
        idxg = sb("idxg", [P, SLOTS], U32)
        gateg = sb("gateg", [P, SLOTS])
        idxst = sb("idxst", [P, 2 * RING], U32)
        small = sb("small", [P, 160])
        mixTs = sb("mixTs", [P, KC * NS])
        ps = ctx.enter_context(nc.psum_tensor("ps", [P, 8, 512], F32))
        acc = ps[:, 0:2, :].rearrange("p a b -> p (a b)")
        F = [ps[:, 2 + i, :] for i in range(6)]

        def FF(a, b):
            return ps[:, 2 + a:2 + b, :].rearrange("p a b -> p (a b)")

        row_u = [ring[:, r * ROWW:r * ROWW + D] for r in range(RING)]
        row_v = [ring[:, r * ROWW + D:(r + 1) * ROWW] for r in range(RING)]
        row = [ring[:, r * ROWW:(r + 1) * ROWW] for r in range(RING)]
        x2, xT = work[:, 0:D], work[:, D:2 * D]
        rope = qsT[:, 0:256]

        at = [0]

        def cols(n):
            at[0] += n
            return small[:, at[0] - n:at[0]]

        g1c, qdec, kdec, sinkb, iota16 = cols(8), cols(4), cols(4), cols(8), cols(16)
        ssq, rstd, mx, nmx, rs, es, rden = cols(4), cols(4), cols(8), cols(8), cols(8), cols(8), cols(8)
        hs1, hs2, fs1, fs2 = cols(1), cols(1), cols(1), cols(1)
        ssum, srec = cols(8), cols(8)
        dot, gel = cols(RING), cols(RING)
        qk, sinks64, m64, n64, r64, e64 = cols(4), cols(1), cols(1), cols(1), cols(1), cols(1)
        ssqs, rstds = cols(4), cols(4)
        tok_sum, tok_root = (hs1, fs1), (hs2, fs2)

        xTall = ring[:, 0:KC * NTOK].rearrange("p (k t) -> p k t", k=KC)
        wbuf = [ring[:, KC * NTOK + c * KC * CW:KC * NTOK + (c + 1) * KC * CW].rearrange("p (k n) -> p k n", k=KC)
                for c in range(2)]
        top = KC * NTOK + 2 * KC * CW
        wqT = [ring[:, top + c * D:top + (c + 1) * D] for c in range(2)]
        skT = wo[:, 0:2, :].rearrange("p a b -> p (a b)")
        xa = [h[:, :], x2g[:, :]]
        staging = [work[:, i * CW:(i + 1) * CW] for i in range(STG)]
        o1 = [0]

        def part(n):
            o1[0] += n
            return ring[:, o1[0] - n:o1[0]]

        kw = part(NS * P).rearrange("p (s c) -> p s c", s=NS)
        vw = part(NS * P).rearrange("p (s c) -> p s c", s=NS)
        st_s = part(NS * RH * HD).rearrange("p (s h e) -> p s h e", s=NS, h=RH)
        kwT = part(NS * P)
        sel8 = part(NS * P)
        sT = part(96)
        ss = part(64)
        sr = part(P)
        pts = part(64)
        osT = part(32)
        mask0 = part(2 * P)
        projs = part(D_IN)
        works = part(2 * D)
        ropes = part(256)

        ld_first, ld_const, ld_skT = sem("ld_first"), sem("ld_const"), sem("ld_skT")
        ld_wq = [sem("ld_wq0"), sem("ld_wq1")]
        ld_x = [sem("ld_x0"), sem("ld_x1")]
        ld_w = [sem("ld_w0"), sem("ld_w1")]
        ld_wo = sem("ld_wo")
        keyw_mm, keyw_out = sem("keyw_mm"), sem("keyw_out")
        root_in, root_out = sem("root_in"), sem("root_out")
        xn_ready, xn_T, xn_out = sem("xn_ready"), sem("xn_T"), sem("xn_out")
        pj_mm, pj_out = sem("pj_mm"), sem("pj_out")
        st_pj = [sem(f"st_pj{i}") for i in range(STG)]
        zeroed = sem("zeroed")
        dve_steps, act_steps = sem("dve_steps"), sem("act_steps")
        ld_proj, ld_res, ld_mask0 = sem("ld_proj"), sem("ld_res"), sem("ld_mask0")
        roped, kd_ready = sem("roped"), sem("kd_ready")
        qkT_mm, qkT_out = sem("qkT_mm"), sem("qkT_out")
        st_mm, stm_ready, ret_mm, silu_ready, mixr_ready = (sem("st_mm"), sem("stm_ready"), sem("ret_mm"),
                                                            sem("silu_ready"), sem("mixr_ready"))
        qsT_mm, qsT_out, sw_mm, sw_nmax, sw_exp = (sem("qsT_mm"), sem("qsT_out"), sem("sw_mm"), sem("sw_nmax"),
                                                   sem("sw_exp"))
        pT_mm, pT_out, sw_o, mixs_ready = (sem("pT_mm"), sem("pT_out"), sem("sw_o"),
                                                        sem("mixs_ready"))
        mixT_mm, mixT_out, o_mm, x2_ready = sem("mixT_mm"), sem("mixT_out"), sem("o_mm"), sem("x2_ready")
        x2T_mm, x2T_out, sc_mm, sc_out = sem("x2T_mm"), sem("x2T_out"), sem("sc_mm"), sem("sc_out")
        best_shift, best_exp, topk_done = sem("best_shift"), sem("best_exp"), sem("topk_done")
        idx_taken, acc_out = sem("idx_taken"), sem("acc_out")
        ld_row = [sem(f"ld_row{r}") for r in range(RING)]
        staged, dots, gelus, diags, used = sem("staged"), sem("dots"), sem("gelus"), sem("diags"), sem("used")
        residual_in, y_ready, st_y = sem("residual_in"), sem("y_ready"), sem("st_y")
        st_misc, st_state = sem("st_misc"), sem("st_state")
        sm = {n: sem("smp_" + n) for n in (
            "kw", "vw", "sel", "qT", "qT_out", "kwT", "kwT_out", "s", "s_out", "sr", "nmax", "exp", "p", "pT", "pT_out",
            "o", "o_out", "qS", "qS_out", "qSn", "mixr", "mixT", "mixT_out", "vb", "vb_used", "silu", "st", "tok",
            "spread", "idx8", "rowsx", "roped", "columns", "silu_out")}

        proj_d = nc.dram_tensor("proj_scratch", [NTOK, D_IN], F32).ap()
        w_in_v = A["w_in"].rearrange("(k p) n -> p k n", p=P)
        x_p = A["x_prompt"].rearrange("a t d -> (a t) d")
        x_s = A["x_sample"].rearrange("a t d -> (a t) d")
        y_p = out[0].rearrange("a t d -> (a t) d")
        y_s = out[1].rearrange("a t d -> (a t) d")
        N_CONST = 9 + NS

        block = ctx.enter_context(nc.Block())

        def rows_of(vector, n):
            return vector.rearrange("(a n) -> a n", a=1).to_broadcast([P, n])

        @block.sync
        def _(sp):
            sp.dma_start(xa[0], x_p[0:P, :]).then_inc(ld_x[0], 16)
            for dst, src in [(ident[:], A["c_ident"]), (g1c, A["norm1_g"].rearrange("(k p) -> p k", p=P))]:
                sp.dma_start(dst, src, allow_slow_non_contiguous=True).then_inc(ld_first, 16)
            sp.dma_start(xa[1], x_p[P:2 * P, :]).then_inc(ld_x[1], 16)

            def load_w(c):
                return sp.dma_start(wbuf[c], w_in_v[:, :, c * CW:(c + 1) * CW])

            load_w(0).then_inc(ld_w[0], 16)

            def load_x(n):
                rows = P if n < NB else NS
                sp.wait_ge(xn_T, n - 1)
                src = x_p[n * P:(n + 1) * P, :] if n < NB else x_s
                sp.dma_start(xa[n % 2][0:rows, :], src).then_inc(ld_x[n % 2], 16)

            load_x(2)
            load_w(1).then_inc(ld_w[1], 16)
            load_x(3)
            sp.dma_start(skT, A["sub_keysT"]).then_inc(ld_skT, 16)
            for n in range(2):
                sp.dma_start(wqT[n], A["wqT"][n]).then_inc(ld_wq[n], 16)
            load_x(4)
            loads = [(qdec, A["c_qdec"]), (kdec, A["c_kdec"]), (iota16, A["c_iota"]),
                     (sinkb, rows_of(A["swa_sinks"], QH)),
                     (dmaskT[:].rearrange("p h m -> p (h m)"), A["c_dmaskT"]), (wmask[:], A["c_wmask"]),
                     (g2b[:], rows_of(A["norm2_g"], D)), (gfb[:], rows_of(A["final_g"], D)),
                     (rope, A["c_rope"][0:P, :])]
            loads += [(sinks64[s * QH:(s + 1) * QH, :], A["swa_sinks"].rearrange("(q a) -> q a", a=1))
                      for s in range(NS)]
            load_x(5)

            def store_tile(i, tile, col0):
                rows = P if i < NB else NS
                sp.wait_ge(pj_out, tile + 1)
                sp.dma_start(proj_d[i * P:i * P + rows, bass.ds(col0, CW)],
                             staging[(i - 1) % STG][0:rows, :]).then_inc(st_pj[(i - 1) % STG], 16)

            def load_wqT(n, a):
                sp.wait_ge(keyw_mm, n * 2 + (2 * a - 2))
                sp.dma_start(wqT[a % 2], A["wqT"][bass.ds(n + a, 1)].rearrange("a p n -> p (a n)")
                             ).then_inc(ld_wq[a % 2], 16)

            for i in range(1, TILES):
                store_tile(i, i, 0)
                if i + 5 < TILES:
                    load_x(i + 5)
            for dst, src in loads:
                sp.dma_start(dst, src, allow_slow_non_contiguous=True).then_inc(ld_const, 16)
            sp.wait_ge(xn_T, TILES)
            sp.dma_start(h[:], x_p[0:P, :]).then_inc(ld_res, 16)
            with sp.Fori(0, 3) as t:
                for cc in range(2):
                    sp.wait_ge(pj_mm, t * (2 * TILES) + (cc + 1) * TILES)
                    sp.dma_start(wbuf[cc], w_in_v[:, :, bass.ds(t * (2 * CW) + (2 + cc) * CW, CW)]
                                 ).then_inc(ld_w[cc], 16)
                    for i in range(TILES):
                        tile = cc * TILES + i
                        if i:
                            store_tile(i, t * (2 * TILES) + (TILES + tile), t * (2 * CW) + (1 + cc) * CW)
                        if tile % 4 == 0 and tile:
                            load_wqT(t * 4, tile // 4 + 1)
            for i in range(1, TILES):
                store_tile(i, (NCH - 1) * TILES + i, (NCH - 1) * CW)
                if i in (2, 4):
                    load_wqT(12, 1 + i // 2)
            for q in st_pj:
                sp.wait_ge(q, 16 * NCH * NB // STG)
            sp.wait_ge(pj_mm, NCH * TILES)

            sp.dma_start(projs[0:NS, :], proj_d[SEQ:NTOK, :]).then_inc(sm["columns"], 16)
            sp.dma_start(ropes[0:NS, :], A["c_rope"][SEQ:NTOK, :]).then_inc(sm["columns"], 16)
            for s in range(NS):
                sp.dma_start(kw[0:P - 1, s, :], A["cache_swa_k"][s, 1:P].rearrange("w k d -> w (k d)")
                             ).then_inc(sm["kw"], 16)
            sp.dma_start(kw[P - 1:P, :, :], proj_d[SEQ:NTOK, C_KS:C_VS].rearrange("(a s) c -> a s c", a=1)
                         ).then_inc(sm["kw"], 16)
            sp.dma_start(st_s.rearrange("p s h e -> p (s h) e"),
                         A["state_ret"].rearrange("s h d e -> d (s h) e")).then_inc(sm["kw"], 16)
            sp.dma_start(mask0, A["c_wmask0"]).then_inc(ld_mask0, 16)
            for s in range(NS):
                sp.dma_start(vw[0:P - 1, s, :], A["cache_swa_v"][s, 1:P].rearrange("w k d -> w (k d)")
                             ).then_inc(sm["vw"], 16)
            sp.dma_start(vw[P - 1:P, :, :], proj_d[SEQ:NTOK, C_VS:D_IN].rearrange("(a s) c -> a s c", a=1)
                         ).then_inc(sm["vw"], 16)
            sp.dma_start(sel8[0:NS, :], A["c_sel8"]).then_inc(sm["vw"], 16)
            sp.wait_ge(keyw_out, 2 * NHC + 2)
            sp.dma_start(wo[:], A["w_out"].rearrange("(k p) n -> p k n", p=P)).then_inc(ld_wo, 16)
            sp.wait_ge(sm["kw"], 16 * (NS + 2))
            sp.wait_ge(sm["vw"], 16 * (NS + 2))
            sp.dma_start(out[6].rearrange("s w k d -> w s (k d)"), kw).then_inc(st_misc, 16)
            sp.dma_start(out[7].rearrange("s w k d -> w s (k d)"), vw).then_inc(st_misc, 16)
            sp.dma_start(out[3][0].rearrange("w k d -> w (k d)"), proj_d[SEQ - P:SEQ, C_KS:C_VS]).then_inc(st_misc, 16)
            sp.dma_start(out[4][0].rearrange("w k d -> w (k d)"), proj_d[SEQ - P:SEQ, C_VS:D_IN]).then_inc(st_misc, 16)
            sp.wait_ge(sm["st"], 1)
            sp.dma_start(out[5].rearrange("s h d e -> d (s h) e"), st_s.rearrange("p s h e -> p (s h) e")
                         ).then_inc(st_state, 16)
            sp.wait_ge(st_state, 16)
            sp.wait_ge(st_misc, 64)
            sp.sem_inc(sm["tok"], 1)

            def load_columns(b):
                sp.dma_start(proj[:], proj_d[bass.ds(b * P, P), :]).then_inc(ld_proj, 16)
                sp.dma_start(rope, A["c_rope"][bass.ds(b * P, P), :]).then_inc(ld_proj, 16)

            def load_residual(b):
                sp.wait_ge(residual_in, b)
                sp.dma_start(h[:], x_p[bass.ds(b * P, P), :]).then_inc(ld_res, 16)

            def store_y(b):
                sp.wait_ge(y_ready, b + 1)
                sp.dma_start(y_p[bass.ds(b * P, P), :], xT).then_inc(st_y, 16)

            sp.wait_ge(topk_done, 2)
            load_columns(1)
            with sp.Fori(0, NB - 2) as b:
                load_residual(b + 1)
                store_y(b)
                sp.wait_ge(st_y, b * 16 + 16)
                load_columns(b + 2)
            load_residual(NB - 1)
            store_y(NB - 2)
            sp.wait_ge(st_y, 16 * (NB - 1))
            sp.wait_ge(residual_in, NB)
            sp.dma_start(h[0:NS, :], x_s).then_inc(ld_res, 16)
            sp.wait_ge(mixs_ready, NB)
            sp.dma_start(out[2][0].rearrange("h d e -> d h e"), state[:]).then_inc(st_misc, 16)
            sp.dma_start(qsT[0:NS, 0:P], A["c_spread"]).then_inc(sm["sel"], 16)
            sp.dma_start(qsT[:, P:2 * P + NS], A["c_pick"]).then_inc(sm["sel"], 16)
            sp.wait_ge(y_ready, NB)
            sp.dma_start(y_p[(NB - 1) * P:NB * P, :], xT).then_inc(st_y, 16)
            sp.wait_ge(y_ready, NB + 1)
            sp.dma_start(y_s, work[0:NS, 0:D]).then_inc(st_y, 16)
            sp.wait_ge(st_y, 16 * (NB + 1))
            sp.wait_ge(st_misc, 80)

        @block.gpsimd
        def _(pool):
            pool.wait_ge(sm["tok"], 1)

            def fetch(r, col):
                nc.gpsimd.indirect_dma_start(row[r], None, A["peer_uv"],
                                             bass.IndirectOffsetOnAxis(ap=idxst[:, col:col + 1], axis=0)
                                             ).then_inc(ld_row[r], 16)

            with pool.Fori(0, NB) as b:
                for half in range(2):
                    hold(pool, topk_done, b * 2 + (half + 1))
                    own = slice(half * HALF, (half + 1) * HALF)
                    nc.gpsimd.tensor_copy(idxg[:, own], idx[:, own]).then_inc(idx_taken, 1)
                    hold(pool, idx_taken, b * 2 + (half + 1))
                    with pool.Fori(0, PH // 2) as hd:
                        for part_ in range(2):
                            c0 = part_ * RING
                            nc.gpsimd.tensor_copy(idxst[:, c0:c0 + RING],
                                                  idxg[:, bass.ds(hd * TK + (half * HALF + c0), RING)]
                                                  ).then_inc(staged, 1)
                            hold(pool, staged, b * (2 * PH) + hd * 2 + (half * PH + part_ + 1))
                            for r in range(RING):
                                hold(pool, used, b * SLOTS + hd * TK + (half * HALF + c0 + r + 1))
                                fetch(r, c0 + r)
            pool.wait_ge(sm["idx8"], 1)
            for hd in range(PH):
                hold(pool, used, NB * SLOTS + hd + 1)
                nc.gpsimd.indirect_dma_start(row[hd], None, A["peer_uv"],
                                             bass.IndirectOffsetOnAxis(ap=idx[:, hd:hd + 1], axis=0)
                                             ).then_inc(ld_row[hd], 16)

        @block.tensor
        def _(pe):
            def T(o, i, n=P):
                return nc.tensor.transpose(o, i, ident[0:n, 0:n])

            pe.wait_ge(ld_first, 32)

            def token_transposes(n):
                rows = P if n < NB else NS
                pe.wait_ge(xn_ready, n + 1)
                if n:
                    pe.wait_ge(xn_out, n)
                for k in range(KC):
                    t = T(acc[:, k * P:k * P + rows], xa[n % 2][0:rows, k * P:(k + 1) * P], rows)
                t.then_inc(xn_T, 1)

            def project(c, i, tile, reuse):
                rows = P if i < NB else NS
                bank = F[(c * TILES + i) % BANKS]
                if reuse:
                    pe.wait_ge(pj_out, tile - (BANKS - 1))
                for k in range(KC):
                    mm = nc.tensor.matmul(bank[0:rows, 0:CW], xTall[:, k, i * P:i * P + rows],
                                          wbuf[c % 2][:, k, :], start=(k == 0), stop=(k == KC - 1))
                mm.then_inc(pj_mm, 1)

            def key_weights(t, a):
                pe.wait_ge(ld_wq[a % 2], t * 32 + 16 * (a // 2 + 1))
                for half in range(2):
                    pe.wait_ge(keyw_out, t * 8 + (2 * a + half + 1))
                    for k in range(4):
                        mm = nc.tensor.matmul(acc[:, (half * 4 + k) * P:(half * 4 + k + 1) * P],
                                              wqT[a % 2][:, (half * 4 + k) * P:(half * 4 + k + 1) * P],
                                              skT[:, bass.ds(t * (4 * NK) + a * NK, NK)], start=True, stop=True)
                    mm.then_inc(keyw_mm, 1)

            token_transposes(0)
            token_transposes(1)
            pe.wait_ge(ld_w[0], 16)
            for i in range(TILES):
                pe.wait_ge(xn_out, i + 1)
                project(0, i, i, i >= BANKS)
                if i + 2 < TILES:
                    token_transposes(i + 2)
            pe.wait_ge(ld_skT, 16)
            with pe.Fori(0, 3) as t:
                for cc in range(2):
                    pe.wait_ge(ld_w[1 - cc], t * 16 + 16 * (1 + cc))
                    for i in range(TILES):
                        tile = cc * TILES + i
                        project(1 + cc, i, t * (2 * TILES) + (TILES + tile), True)
                        if tile % 4 == 3:
                            key_weights(t, tile // 4)
            pe.wait_ge(ld_w[1], 16 * 4)
            for i in range(TILES):
                project(NCH - 1, i, (NCH - 1) * TILES + i, True)
                if i % 2 and i < 8:
                    key_weights(3, i // 2)

            SA, SB = acc[:, 0:512], acc[:, 512:1024]
            sq = sT[:, 64:96].rearrange("p (i s) -> p i s", i=GRP)

            def sample(step):
                if step == 2:
                    pe.wait_ge(sm["roped"], 1)
                    pe.wait_ge(keyw_out, 2 * NHC + 2)
                    for j in range(8):
                        T(SA[:, j * NS:(j + 1) * NS], projs[0:NS, j * P:(j + 1) * P], NS)
                    for j in range(4):
                        t = T(SA[:, 64 + j * NS:64 + (j + 1) * NS], projs[0:NS, C_QS + j * P:C_QS + (j + 1) * P], NS)
                    t.then_inc(sm["qT"], 1)
                    pe.wait_ge(sm["kw"], 16 * (NS + 2))
                    for s in range(4):
                        t = T(SB[:, s * P:(s + 1) * P], kw[:, s, :])
                    t.then_inc(sm["kwT"], 1)
                elif step == 3:
                    pe.wait_ge(sm["qT_out"], 1)
                    for hh in range(RH):
                        for s in range(NS):
                            mm = nc.tensor.matmul(SA[:, 96 + hh * NS + s:97 + hh * NS + s], st_s[:, s, hh, :],
                                                  sT[:, hh * NS + s:hh * NS + s + 1], start=True, stop=True)
                    mm.then_inc(sm["qS"], 1)
                    pe.wait_ge(sm["kwT_out"], 1)
                    for s in range(4, NS):
                        t = T(SB[:, (s - 4) * P:(s - 3) * P], kw[:, s, :])
                    t.then_inc(sm["kwT"], 1)
                elif step == 4:
                    pe.wait_ge(sm["kwT_out"], 2)
                    for s in range(NS):
                        for j in range(KVH):
                            o = (SA[:, 128:160], SB[:, 0:32])[j]
                            mm = nc.tensor.matmul(o[:, s * GRP:(s + 1) * GRP],
                                                  kwT[j * SD:(j + 1) * SD, s * P:(s + 1) * P],
                                                  sq[j * SD:(j + 1) * SD, :, s], start=True, stop=True)
                    mm.then_inc(sm["s"], 1)
                elif step == 5:
                    pe.wait_ge(sm["s_out"], 1)
                    T(SA[0:64, 160:288], ss).then_inc(sm["sr"], 1)
                    pe.wait_ge(sm["qS_out"], 1)
                    for hh in range(RH):
                        t = T(SB[0:NS, hh * P:(hh + 1) * P], osT[:, hh * NS:(hh + 1) * NS])
                    t.then_inc(sm["qSn"], 1)
                elif step == 6:
                    pe.wait_ge(sm["p"], 1)
                    T(SA[:, 288:352], sr[0:64, :], 64).then_inc(sm["pT"], 1)
                elif step == 7:
                    pe.wait_ge(sm["pT_out"], 1)
                    pe.wait_ge(sm["vw"], 16 * (NS + 2))
                    ov = SA[:, 352:384].rearrange("p (c s) -> p c s", c=4)
                    pv = pts.rearrange("p (s j a b) -> p s j a b", s=NS, j=KVH, a=2)
                    for s in range(NS):
                        for j in range(KVH):
                            for half in range(2):
                                nc.tensor.matmul(ov[half * SD:(half + 1) * SD, 2 * j:2 * j + 2, s],
                                                 vw[:, s, j * SD:(j + 1) * SD], pv[:, s, j, :, half],
                                                 start=True, stop=True)
                    pe.wait_ge(sm["mixr"], 1)
                    for hh in range(RH):
                        t = T(SA[:, 384 + hh * NS:384 + (hh + 1) * NS],
                              projs[0:NS, C_MIX + hh * P:C_MIX + (hh + 1) * P], NS)
                    t.then_inc(sm["mixT"], 1)
                elif step == 8:
                    pe.wait_ge(sm["mixT_out"], 1)
                    for s in range(NS):
                        if s >= 2:
                            pe.wait_ge(sm["vb_used"], s - 1)
                        nc.tensor.matmul((SA, SB)[s % 2], sel8[0:NS, s * P:(s + 1) * P], projs[0:NS, C_V:C_V + 512],
                                         start=True, stop=True).then_inc(sm["vb"], 1)

            def transposes(b):
                pe.wait_ge(roped, b + 1)
                for j in range(8):
                    t = T(FF(0, 2)[:, j * P:(j + 1) * P], proj[:, j * P:(j + 1) * P])
                t.then_inc(qkT_mm, 1)
                for j in range(4):
                    T(F[2][:, j * P:(j + 1) * P], proj[:, C_QS + j * P:C_QS + (j + 1) * P])
                T(F[3][:, 0:P], proj[:, C_KS:C_VS]).then_inc(qsT_mm, 1)

            def retention_scores(b):
                pe.wait_ge(qkT_out, b + 1)
                for hh in range(RH):
                    mm = nc.tensor.matmul(F[0][:, hh * P:(hh + 1) * P], xT[:, 512 + hh * P:512 + (hh + 1) * P],
                                          xT[:, hh * P:(hh + 1) * P], start=True, stop=True)
                mm.then_inc(st_mm, 1)
                pe.wait_ge(qsT_out, b + 1)
                for hh in range(RH):
                    nc.tensor.matmul(F[3][:, hh * P:(hh + 1) * P], xT[:, hh * P:(hh + 1) * P], state[:, hh, :],
                                     start=True, stop=True)
                pe.wait_ge(kd_ready, b + 1)
                for hh in range(RH):
                    nc.tensor.matmul(F[4][:, hh * P:(hh + 1) * P], x2[:, 512 + hh * P:512 + (hh + 1) * P],
                                     proj[:, C_V + hh * P:C_V + (hh + 1) * P], start=True, stop=True)

            def retention_values(b):
                pe.wait_ge(stm_ready, b + 1)
                for hh in range(RH):
                    mm = nc.tensor.matmul(F[5][:, hh * P:(hh + 1) * P], x2[:, hh * P:(hh + 1) * P],
                                          proj[:, C_V + hh * P:C_V + (hh + 1) * P], start=True, stop=True)
                mm.then_inc(ret_mm, 1)

            def window_scores(b):
                pe.wait_ge(mixr_ready, b + 1)
                for j in range(KVH):
                    for i in range(GRP):
                        bank = F[2 + 2 * j + i // 2]
                        mm = nc.tensor.matmul(bank[:, i % 2 * 256:i % 2 * 256 + 256],
                                              qsT[j * SD:(j + 1) * SD, i * P:(i + 1) * P],
                                              kTb[j * SD:(j + 1) * SD, :], start=True, stop=True)
                mm.then_inc(sw_mm, 1)

            def window_transposes(b):
                pe.wait_ge(sw_exp, b + 1)
                for j in range(KVH):
                    for q in range(8):
                        t = T(FF(2 * j, 2 * j + 2)[:, q * P:(q + 1) * P],
                              work[:, j * D + q * P:j * D + (q + 1) * P])
                    t.then_inc(pT_mm, 1)

            def window_values(b):
                pe.wait_ge(pT_out, b * 2 + 2)
                for j in range(KVH):
                    for i in range(GRP):
                        o = F[4][:, (j * GRP + i) * SD:(j * GRP + i + 1) * SD]
                        pT = work[:, j * D + i * 256:j * D + (i + 1) * 256]
                        nc.tensor.matmul(o, pT[:, 0:P], vprev[:, j * SD:(j + 1) * SD], start=True, stop=False)
                        mm = nc.tensor.matmul(o, pT[:, P:2 * P], proj[:, C_VS + j * SD:C_VS + (j + 1) * SD],
                                              start=False, stop=True)
                mm.then_inc(sw_o, 1)

            def mix_transposes(b):
                pe.wait_ge(mixs_ready, b + 1)
                for k in range(KC):
                    t = T(FF(0, 2)[:, k * P:(k + 1) * P], proj[:, C_MIX + k * P:C_MIX + (k + 1) * P])
                t.then_inc(mixT_mm, 1)

            def output_projection(b, n, rows=P):
                if rows == P and n == 0:
                    pe.wait_ge(mixT_out, b + 1)
                for k in range(KC):
                    lhsT = xT[:, k * P:(k + 1) * P] if rows == P else mixTs[:, k * NS:(k + 1) * NS]
                    mm = nc.tensor.matmul(F[2 + n][0:rows, :], lhsT, wo[:, k, n * 512:(n + 1) * 512],
                                          start=(k == 0), stop=(k == KC - 1))
                mm.then_inc(o_mm, 1)

            def token_transposes2(b, rows=P):
                pe.wait_ge(x2_ready, b + 1)
                for k in range(KC):
                    t = T(FF(0, 2)[:, k * P:k * P + rows], x2[0:rows, k * P:(k + 1) * P], rows)
                t.then_inc(x2T_mm, 1)

            def key_scores(b, n, rows=P):
                if n == 0:
                    pe.wait_ge(x2T_out, b + 1)
                for k in range(KC):
                    mm = nc.tensor.matmul(F[2 + n][0:rows, :], xT[:, k * P:k * P + rows],
                                          keyw[:, k, n * 512:(n + 1) * 512],
                                          start=(k == 0), stop=(k == KC - 1))
                mm.then_inc(sc_mm, 1)

            def front_mid(step, b, rows=P):
                if step == 9:
                    output_projection(b, 1, rows)
                elif step == 11:
                    key_scores(b, 1, rows)
                elif step == 12:
                    key_scores(b, 3, rows)

            def front(step, b, rows=P):
                if step == 1:
                    transposes(b)
                elif step == 2:
                    retention_scores(b)
                elif step == 3:
                    retention_values(b)
                elif step == 4:
                    window_scores(b)
                elif step == 5:
                    window_transposes(b)
                elif step == 6:
                    window_values(b)
                elif step == 7:
                    mix_transposes(b)
                elif step == 8:
                    output_projection(b, 0, rows)
                elif step == 9:
                    token_transposes2(b, rows)
                elif step == 10:
                    key_scores(b, 0, rows)
                elif step == 11:
                    key_scores(b, 2, rows)

            def add_residual(b):
                for n in range(2):
                    mm = nc.tensor.matmul(acc[:, n * 512:(n + 1) * 512], ident[:], h[:, n * 512:(n + 1) * 512],
                                          start=True, stop=False, skip_group_check=True)
                mm.then_inc(residual_in, 1)

            def add_experts(b, g, pairs=range(PAIRS)):
                for p in pairs:
                    pe.wait_ge(diags, b * (GROUPS * PAIRS) + (g * PAIRS + p + 1))
                    for r in range(p * PAIR, (p + 1) * PAIR):
                        for n in range(2):
                            mm = nc.tensor.matmul(acc[:, n * 512:(n + 1) * 512], row_u[r][:, 0:P],
                                                  row_v[r][:, n * 512:(n + 1) * 512],
                                                  start=False, stop=False, skip_group_check=True)
                        mm.then_inc(used, 1)

            pe.wait_ge(zeroed, 1)
            for step in range(1, GROUPS):
                if step == 8:
                    pe.wait_ge(ld_wo, 16)
                front_mid(step, 0)
                front(step, 0)
                sample(step - SAMPLE_LAG)
            pe.wait_ge(sm["vb_used"], NS)
            add_residual(0)
            add_experts(0, 0)
            with pe.Fori(0, NB - 1) as b:
                for g in range(1, GROUPS):
                    add_experts(b, g, range(0, 2))
                    front_mid(g, b + 1)
                    add_experts(b, g, range(2, PAIRS))
                    front(g, b + 1)
                pe.wait_ge(acc_out, b + 1)
                add_residual(b + 1)
                add_experts(b + 1, 0)
            for g in range(1, GROUPS):
                add_experts(NB - 1, g)
                if g >= SAMPLE_STEP:
                    front_mid(g + 8 - SAMPLE_STEP, NB, NS)
                    front(g + 8 - SAMPLE_STEP, NB, NS)
            pe.wait_ge(sm["spread"], 1)
            pe.wait_ge(sm["sel"], 32)
            spread = qsT[0:NS, 0:P]
            for n in range(2):
                nc.tensor.matmul(F[n], spread, x2[0:NS, n * 512:(n + 1) * 512], start=True, stop=True)
            nc.tensor.matmul(F[2][:, 0:P], spread, xT[0:NS, 0:P], start=True, stop=True)
            nc.tensor.matmul(F[2][:, P:2 * P], spread, gates[0:NS, :], start=True, stop=True
                             ).then_inc(sm["rowsx"], 1)
            pe.wait_ge(acc_out, NB)
            for n in range(2):
                mm = nc.tensor.matmul(acc[0:NS, n * 512:(n + 1) * 512], ident[0:NS, 0:NS],
                                      h[0:NS, n * 512:(n + 1) * 512], start=True, stop=False, skip_group_check=True)
            mm.then_inc(residual_in, 1)
            for p in range(PAIRS):
                pe.wait_ge(diags, NB * GROUPS * PAIRS + p + 1)
                for r in range(p * PAIR, (p + 1) * PAIR):
                    for n in range(2):
                        mm = nc.tensor.matmul(acc[0:NS, n * 512:(n + 1) * 512], row_u[r][:, 0:NS],
                                              row_v[r][:, n * 512:(n + 1) * 512],
                                              start=False, stop=(r == RING - 1), skip_group_check=True)
                    mm.then_inc(used, 1)

        @block.scalar
        def _(act):
            me = Steps(act, act_steps)

            def copy(o, i, **kw_):
                return nc.scalar.activation(o, i, ACT.Copy, **kw_)

            roots = Steps(act, root_in)

            def root(o):
                roots.n += 1
                roots.sync()
                nc.scalar.activation(o, o, ACT.Sqrt).then_inc(root_out, 1)

            def tokens_in(n):
                rows = P if n < NB else NS
                act.wait_ge(xn_T, n + 1)
                for k in range(KC):
                    ins = copy(xTall[:, k, n * P:n * P + rows], acc[:, k * P:k * P + rows], scale=g1c[:, k:k + 1])
                ins.then_inc(xn_out, 1)

            def tile_out(c, i, tile, col0, stored):
                rows = P if i < NB else NS
                src = F[(c * TILES + i) % BANKS][0:rows, 0:CW]
                hold(act, pj_mm, tile + 1)
                if i == 0:
                    copy(proj[:, bass.ds(col0, CW)], src).then_inc(pj_out, 1)
                else:
                    if stored is not None:
                        act.wait_ge(st_pj[(i - 1) % STG], stored)
                    copy(staging[(i - 1) % STG][0:rows, :], src).then_inc(pj_out, 1)

            def keyw_out_(t, a):
                for half in range(2):
                    hold(act, keyw_mm, t * 8 + (2 * a + half + 1))
                    o = keyw[:, half * 4:half * 4 + 4, bass.ds(t * (4 * NK) + a * NK, NK)]
                    copy(o, acc[:, half * 512:(half + 1) * 512].rearrange("p (k n) -> p k n", k=4)
                         ).then_inc(keyw_out, 1)

            act.wait_ge(ld_first, 32)
            for n in range(2):
                root(tok_root[n % 2])
                tokens_in(n)
            for i in range(TILES):
                if i + 2 < TILES:
                    root(tok_root[i % 2] if i + 2 < NB else tok_root[i % 2][0:NS, :])
                tile_out(0, i, i, 0, 16 * ((i - 1) // STG) if i > STG else None)
                if i + 2 < TILES:
                    tokens_in(i + 2)
            with act.Fori(0, 3) as t:
                for cc in range(2):
                    for i in range(TILES):
                        tile = cc * TILES + i
                        tile_out(1 + cc, i, t * (2 * TILES) + (TILES + tile), t * (2 * CW) + (1 + cc) * CW,
                                 t * 64 + 16 * (2 + 2 * cc + (i - 1) // STG))
                        if tile % 4 == 3:
                            keyw_out_(t, tile // 4)
            for i in range(TILES):
                tile_out(NCH - 1, i, (NCH - 1) * TILES + i, (NCH - 1) * CW, 16 * (2 * (NCH - 1) + (i - 1) // STG))
                if i % 2 and i < 8:
                    keyw_out_(3, i // 2)

            def sample(step):
                if step == 2:
                    act.wait_ge(sm["qT"], 1)
                    copy(sT, acc[:, 0:96]).then_inc(sm["qT_out"], 1)
                    act.wait_ge(sm["kwT"], 1)
                    copy(kwT[:, 0:512], acc[:, 512:1024]).then_inc(sm["kwT_out"], 1)
                    nc.scalar.activation(works[0:NS, 512:1024], projs[0:NS, C_G:C_G + 512], ACT.Silu
                                         ).then_inc(sm["silu_out"], 1)
                elif step == 3:
                    act.wait_ge(sm["qS"], 1)
                    copy(osT, acc[:, 96:128]).then_inc(sm["qS_out"], 1)
                    act.wait_ge(sm["kwT"], 2)
                    copy(kwT[:, 512:1024], acc[:, 512:1024]).then_inc(sm["kwT_out"], 1)
                elif step == 4:
                    act.wait_ge(sm["s"], 1)
                    sv = ss.rearrange("p (s j i) -> p j s i", s=NS, j=KVH)
                    for j in range(KVH):
                        src = (acc[:, 128:160], acc[:, 512:544])[j]
                        ins = copy(sv[:, j], src.rearrange("p (s i) -> p s i", s=NS), scale=S_SCALE)
                    ins.then_inc(sm["s_out"], 1)
                elif step == 5:
                    act.wait_ge(sm["nmax"], 1)
                    nc.scalar.activation(sr[0:64, :], sr[0:64, :], ACT.Exp, bias=n64[0:64, :],
                                         accum_out=r64[0:64, :])
                    nc.scalar.activation(e64[0:64, :], sinks64[0:64, :], ACT.Exp, bias=n64[0:64, :]
                                         ).then_inc(sm["exp"], 1)
                    root(rstds[0:NS, :])
                elif step == 6:
                    act.wait_ge(sm["pT"], 1)
                    copy(pts, acc[:, 288:352]).then_inc(sm["pT_out"], 1)
                elif step == 7:
                    act.wait_ge(sm["mixT"], 1)
                    copy(mixTs[:, 32:64], acc[:, 352:384])
                    copy(mixTs[:, 0:32], acc[:, 384:416]).then_inc(sm["mixT_out"], 1)

            def transposes_out(b):
                act.wait_ge(qkT_mm, b + 1)
                copy(xT, FF(0, 2)).then_inc(qkT_out, 1)
                act.wait_ge(qsT_mm, b + 1)
                me.did(copy(kTb[:, 0:P], kTb[:, P:2 * P]))
                me.sync()
                me.did(copy(kTb[:, P:2 * P], F[3][:, 0:P]))
                copy(qsT[:], F[2]).then_inc(qsT_out, 1)

            def silu(b):
                act.wait_ge(ret_mm, b + 1)
                nc.scalar.activation(x2[:, 0:512], proj[:, C_G:C_G + 512], ACT.Silu).then_inc(silu_ready, 1)
                root(rstd)

            def window_exp(b):
                act.wait_ge(sw_nmax, b + 1)
                for q in range(QH):
                    me.did(nc.scalar.activation(work[:, q * 256:(q + 1) * 256], work[:, q * 256:(q + 1) * 256],
                                                ACT.Exp, bias=nmx[:, q:q + 1], accum_out=rs[:, q:q + 1]))
                nc.scalar.activation(es, es, ACT.Exp).then_inc(sw_exp, 1)

            def probs_out(b):
                for j in range(KVH):
                    act.wait_ge(pT_mm, b * 2 + (j + 1))
                    copy(work[:, j * D:(j + 1) * D], FF(2 * j, 2 * j + 2)).then_inc(pT_out, 1)

            def mix_out(b):
                act.wait_ge(sw_o, b + 1)
                copy(vprev[:], proj[:, C_VS:D_IN])
                act.wait_ge(mixT_mm, b + 1)
                copy(xT, FF(0, 2)).then_inc(mixT_out, 1)

            def tokens_out(b, rows=P):
                act.wait_ge(x2T_mm, b + 1)
                src, dst = FF(0, 2), xT
                if rows < P:
                    src = src.rearrange("p (k t) -> p k t", k=KC)[:, :, 0:rows]
                    dst = dst.rearrange("p (k t) -> p k t", k=KC)[:, :, 0:rows]
                copy(dst, src).then_inc(x2T_out, 1)

            def scores_out(b, half, rows=P):
                act.wait_ge(sc_mm, b * 4 + (2 * half + 2))
                copy(proj[0:rows, half * D:(half + 1) * D], FF(2 + 2 * half, 4 + 2 * half)[0:rows, :]
                     ).then_inc(sc_out, 1)

            def gates_exp(b, half, rows=P):
                act.wait_ge(best_shift, b * 2 + (half + 1))
                part_ = gates[0:rows, half * HALF:(half + 1) * HALF]
                nc.scalar.activation(part_, part_, ACT.Exp).then_inc(best_exp, 1)

            def front(step, b, rows=P):
                if step == 2:
                    transposes_out(b)
                elif step == 4:
                    silu(b)
                elif step == 5:
                    window_exp(b)
                elif step == 6:
                    probs_out(b)
                elif step == 8 and rows == P:
                    mix_out(b)
                elif step == 9:
                    root(hs2[0:rows, :])
                elif step == 10:
                    tokens_out(b, rows)
                elif step == 11:
                    scores_out(b, 0, rows)
                elif step == 12:
                    scores_out(b, 1, rows)
                    gates_exp(b, 0, rows)
                elif step == 14:
                    gates_exp(b, 1, rows)

            def expert_gelus(b, g):
                for p in range(PAIRS):
                    act.wait_ge(dots, b * (GROUPS * PAIRS) + (g * PAIRS + p + 1))
                    nc.scalar.activation(gel[:, p * PAIR:(p + 1) * PAIR], dot[:, p * PAIR:(p + 1) * PAIR],
                                         ACT.Gelu).then_inc(gelus, 1)

            def sum_out(b):
                act.wait_ge(topk_done, b * 2 + 4)
                act.nop(nofuse=True)
                act.wait_ge(used, b * SLOTS + (SLOTS + RING))
                copy(xT, acc).then_inc(acc_out, 1)

            for step in range(1, GROUPS):
                front(step, 0)
                sample(step - SAMPLE_LAG)
            expert_gelus(0, 0)
            with act.Fori(0, NB - 1) as b:
                me.enter(b, 2 + QH)
                roots.enter(b, 3)
                for g in range(1, GROUPS):
                    expert_gelus(b, g)
                    front(g, b + 1)
                sum_out(b)
                expert_gelus(b + 1, 0)
                root(fs2)
                me.leave(NB - 1)
                roots.leave(NB - 1)
            for g in range(1, GROUPS):
                expert_gelus(NB - 1, g)
                if g >= SAMPLE_STEP:
                    front(g + 8 - SAMPLE_STEP, NB, NS)
            act.wait_ge(sm["rowsx"], 1)
            sum_out(NB - 1)
            root(fs2)
            expert_gelus(NB, 0)
            root(fs2[0:NS, :])

        @block.vector
        def _(v):
            me, roots = Steps(v, dve_steps), Steps(v, root_out)
            tt = nc.vector.tensor_tensor
            stt = nc.vector.scalar_tensor_tensor
            ts = nc.vector.tensor_scalar

            def tell(sem_, n=1):
                v.nop(nofuse=True).then_inc(sem_, n)

            me.did(nc.vector.memset(state[:], 0.0))
            me.did(nc.vector.memset(kTb[:], 0.0))
            me.did(nc.vector.memset(vprev[:], 0.0))
            me.sync()
            tell(zeroed, 1)
            tell(used, RING)
            tell(keyw_out, 2)

            def root(o, i, scale):
                ts(o, i, scale, EPS, ALU.mult, ALU.add).then_inc(root_in, 1)
                roots.n += 1
                roots.sync()
                me.did(nc.vector.reciprocal(o, o))
                me.sync()

            for n in range(TILES):
                rows = P if n < NB else NS
                xv, total, root_ = xa[n % 2][0:rows, :], tok_sum[n % 2][0:rows, :], tok_root[n % 2][0:rows, :]
                v.wait_ge(ld_x[n % 2], n // 2 * 16 + 16)
                me.did(stt(keyw[0:rows, n % 2, 0:D], xv, 1.0, xv,
                           ALU.mult, ALU.mult, accum_out=total))
                me.sync()
                root(root_, total, 1.0 / D)
                ts(xv, xv, root_, None, ALU.mult).then_inc(xn_ready, 1)

            def rotate(rows, pj, rp, temp):
                qk4 = pj[0:rows, 0:1024].rearrange("p (c h d t) -> p c h d t", c=2, h=RH, t=2)
                tab = rp[0:rows, :].rearrange("p (c f d) -> p c f d", c=2, f=2)
                t1 = temp[0:rows, :].rearrange("p (n c h d) -> p n c h d", n=4, c=2, h=RH)
                for n, (half, trig) in enumerate(((0, 0), (1, 1), (0, 1), (1, 0))):
                    for c in range(2):
                        me.did(tt(t1[:, n, c], qk4[:, c, :, :, half],
                                  tab[:, c, trig, :].rearrange("p (a d) -> p a d", a=1).to_broadcast([rows, RH, 64]),
                                  ALU.mult))
                me.sync()
                for half, (a, b_, op) in enumerate(((0, 1, ALU.subtract), (2, 3, ALU.add))):
                    for c in range(2):
                        me.did(tt(qk4[:, c, :, :, half], t1[:, a, c], t1[:, b_, c], op))
                me.sync()

            def gated_norm(rows, pj, o, sq, silu, sums, root_, silu_sem, count):
                ov = o.rearrange("p (h e) -> p h e", h=RH)
                me.did(tt(sq, o, o, ALU.mult))
                me.sync()
                me.did(nc.vector.tensor_reduce(sums[0:rows, :], sq.rearrange("p (h e) -> p h e", h=RH), AX, ALU.add))
                me.sync()
                root(root_[0:rows, :], sums[0:rows, :], 1.0 / HD)
                me.did(tt(ov, ov, root_[0:rows, :].rearrange("p (h a) -> p h a", a=1).to_broadcast([rows, RH, HD]),
                          ALU.mult))
                v.wait_ge(silu_sem, count)
                v.nop(nofuse=True)
                me.sync()
                return tt(pj[0:rows, C_MIX:C_MIX + 512], o, silu, ALU.mult)

            prod, o_s = works[0:NS, 1024:1536], works[0:NS, 0:512]

            def sample(step):
                if step == 1:
                    v.wait_ge(sm["columns"], 32)
                    rotate(NS, projs, ropes, works)
                    tell(sm["roped"])
                    me.did(tt(prod, projs[0:NS, C_Q:C_Q + 512], projs[0:NS, C_K:C_K + 512], ALU.mult))
                    me.sync()
                    me.did(nc.vector.tensor_reduce(qk[0:NS, :], prod.rearrange("p (h e) -> p h e", h=RH), AX,
                                                   ALU.add))
                    me.sync()
                elif step == 5:
                    s64, sp64 = acc[0:64, 160:288], sr[0:64, :]
                    v.wait_ge(sm["sr"], 1)
                    me.did(nc.vector.tensor_copy(sp64, s64))
                    me.did(nc.vector.tensor_reduce(m64[0:64, :], s64, AX, ALU.max))
                    me.sync()
                    me.did(tt(m64[0:64, :], m64[0:64, :], sinks64[0:64, :], ALU.max))
                    me.sync()
                    ts(n64[0:64, :], m64[0:64, :], -1.0, None, ALU.mult).then_inc(sm["nmax"], 1)
                    v.wait_ge(sm["exp"], 1)
                    me.did(tt(m64[0:64, :], r64[0:64, :], e64[0:64, :], ALU.add))
                    me.sync()
                    me.did(nc.vector.reciprocal(m64[0:64, :], m64[0:64, :]))
                    me.sync()
                    ts(sp64, sp64, m64[0:64, :], None, ALU.mult).then_inc(sm["p"], 1)
                    v.wait_ge(sm["qSn"], 1)
                    for hh in range(RH):
                        me.did(ts(prod[:, hh * P:(hh + 1) * P], acc[0:NS, 512 + hh * P:512 + (hh + 1) * P],
                                  STEP_DECAY[hh], None, ALU.mult))
                    me.sync()
                    for hh in range(RH):
                        me.did(stt(o_s[:, hh * P:(hh + 1) * P], projs[0:NS, C_V + hh * P:C_V + (hh + 1) * P],
                                   qk[0:NS, hh:hh + 1], prod[:, hh * P:(hh + 1) * P], ALU.mult, ALU.add))
                    me.sync()
                    gated_norm(NS, projs, o_s, prod, works[0:NS, 512:1024], ssqs, rstds, sm["silu_out"], 1
                               ).then_inc(sm["mixr"], 1)
                elif step == 6:
                    v.wait_ge(sm["qS_out"], 1)
                    for hh in range(RH):
                        me.did(ts(st_s[:, :, hh, :], st_s[:, :, hh, :], STEP_DECAY[hh], None, ALU.mult))
                    me.sync()
                elif step == 8:
                    for s in range(NS):
                        v.wait_ge(sm["vb"], s + 1)
                        for hh in range(RH):
                            me.did(stt(st_s[:, s, hh, :], acc[:, s % 2 * 512 + hh * P:s % 2 * 512 + (hh + 1) * P],
                                       sT[:, 32 + hh * NS + s:33 + hh * NS + s], st_s[:, s, hh, :],
                                       ALU.mult, ALU.add))
                        me.sync()
                        tell(sm["vb_used"])
                    tell(sm["st"])

            def rotation(b):
                if isinstance(b, int):
                    v.wait_ge(ld_const, 16 * N_CONST)
                    v.wait_ge(pj_out, NCH * TILES)
                    for q in st_pj:
                        v.wait_ge(q, 16 * NCH * NB // STG)
                else:
                    v.wait_ge(ld_proj, b * 32)
                    v.nop(nofuse=True)
                rotate(P, proj, rope, work)
                tell(roped)
                tt(x2[:, 512:1024].rearrange("p (h e) -> p h e", h=RH),
                   proj[:, C_K:C_K + 512].rearrange("p (h e) -> p h e", h=RH),
                   kdec.rearrange("p (h a) -> p h a", a=1).to_broadcast([P, RH, HD]), ALU.mult).then_inc(kd_ready, 1)

            def decay_scores(b):
                v.wait_ge(st_mm, b + 1)
                tt(x2[:, 0:512], F[0], dmaskT[:].rearrange("p h m -> p (h m)"), ALU.mult).then_inc(stm_ready, 1)

            def retention_out(b):
                v.wait_ge(ret_mm, b + 1)
                o = xT[:, 0:512]
                me.did(tt(o.rearrange("p (h e) -> p h e", h=RH), F[3].rearrange("p (h e) -> p h e", h=RH),
                          qdec.rearrange("p (h a) -> p h a", a=1).to_broadcast([P, RH, HD]), ALU.mult))
                for hh in range(RH):
                    me.did(stt(state[:, hh, :], state[:, hh, :], BLOCK_DECAY[hh], F[4][:, hh * P:(hh + 1) * P],
                               ALU.mult, ALU.add))
                me.sync()
                me.did(tt(o, o, F[5], ALU.add))
                me.sync()
                gated_norm(P, proj, o, xT[:, 512:1024], x2[:, 0:512], ssq, rstd, silu_ready, b + 1
                           ).then_inc(mixr_ready, 1)

            def window_max(b, mask):
                if isinstance(b, int):
                    v.wait_ge(ld_mask0, 16)
                v.wait_ge(sw_mm, b + 1)
                v.nop(nofuse=True)
                v.wait_ge(mixr_ready, b + 1)
                s3 = work[:].rearrange("p (q s) -> p q s", q=QH)
                me.did(stt(s3, FF(2, 6).rearrange("p (q s) -> p q s", q=QH), S_SCALE,
                           mask.rearrange("p (a s) -> p a s", a=1).to_broadcast([P, QH, 2 * P]), ALU.mult, ALU.add))
                me.sync()
                me.did(nc.vector.tensor_reduce(mx, s3, AX, ALU.max))
                me.sync()
                me.did(tt(mx, mx, sinkb, ALU.max))
                me.sync()
                me.did(tt(es, sinkb, mx, ALU.subtract))
                me.sync()
                ts(nmx, mx, -1.0, None, ALU.mult).then_inc(sw_nmax, 1)

            def window_out(b):
                v.wait_ge(sw_exp, b + 1)
                me.did(tt(rden, rs, es, ALU.add))
                me.sync()
                me.did(nc.vector.reciprocal(rden, rden))
                v.wait_ge(sw_o, b + 1)
                v.nop(nofuse=True)
                me.sync()
                tt(proj[:, C_MIX + 512:C_MIX + 1024].rearrange("p (q d) -> p q d", q=QH),
                   F[4].rearrange("p (q d) -> p q d", q=QH),
                   rden.rearrange("p (q a) -> p q a", a=1).to_broadcast([P, QH, SD]), ALU.mult
                   ).then_inc(mixs_ready, 1)

            def norm_output(b, rows=P):
                v.wait_ge(ld_res, b * 16 + 16)
                v.nop(nofuse=True)
                v.wait_ge(o_mm, b * 2 + 2)
                hv, xv = h[0:rows, :], x2[0:rows, :]
                me.did(tt(hv, hv, FF(2, 4)[0:rows, :], ALU.add))
                me.sync()
                me.did(stt(xv, hv, 1.0, hv, ALU.mult, ALU.mult, accum_out=hs1[0:rows, :]))
                me.sync()
                root(hs2[0:rows, :], hs1[0:rows, :], 1.0 / D)
                stt(xv, hv, hs2[0:rows, :], g2b[0:rows, :], ALU.mult, ALU.mult).then_inc(x2_ready, 1)

            sc3 = proj[:, 0:NSC].rearrange("p (c n) -> p c n", c=NHC)
            cand8 = proj[:, 0:NSC].rearrange("p (h c) -> p h c", h=PH)
            HH = PH // 2

            def beside(at_, n, like=None):
                return proj[:, NSC + at_:NSC + at_ + n]

            vals, inds, indf = beside(0, 2 * HALF), beside(128, 2 * HALF), beside(256, 2 * HALF)
            best, posn, chosen = beside(384, HALF), beside(448, HALF), beside(512, 2 * HALF)
            ab, abf, numbers = vals, inds, beside(640, SLOTS)

            def rank(js, rowsof, v16, i16):
                for r8 in range(2):
                    for j in js:
                        me.did(nc.vector.max(v16(j)[:, r8 * 8:r8 * 8 + 8], rowsof(j)))
                    hold(v, me.sem, me.base + me.n)
                    for j in js:
                        me.did(nc.vector.max_index(i16(j)[:, r8 * 8:r8 * 8 + 8], v16(j)[:, r8 * 8:r8 * 8 + 8],
                                                   rowsof(j)))
                    hold(v, me.sem, me.base + me.n)
                    if r8 == 0:
                        for j in js:
                            me.did(nc.vector.match_replace(rowsof(j), v16(j)[:, 0:8], rowsof(j), TAKEN))
                        hold(v, me.sem, me.base + me.n)

            def rank_halves(b, half, rows=P):
                hold(v, sc_out, b * 2 + (half + 1))
                v3 = vals[0:rows].rearrange("p (c k) -> p c k", k=TK)
                i3 = inds.bitcast(U32)[0:rows].rearrange("p (c k) -> p c k", k=TK)
                rank(range(PH), lambda j: sc3[0:rows, half * PH + j, :], lambda j: v3[:, j, :],
                     lambda j: i3[:, j, :])
                for hh in range(HH):
                    me.did(tt(cand8[0:rows, half * HH + hh, :].rearrange("p (a b) -> p a b", a=TK),
                              v3[:, 2 * hh, :].rearrange("p (k a) -> p k a", a=1).to_broadcast([rows, TK, TK]),
                              v3[:, 2 * hh + 1, :].rearrange("p (a k) -> p a k", a=1).to_broadcast([rows, TK, TK]),
                              ALU.add))
                me.did(nc.vector.tensor_copy(indf[0:rows], inds.bitcast(U32)[0:rows]))
                hold(v, me.sem, me.base + me.n)

            def choose(b, half, rows=P):
                b3 = best[0:rows].rearrange("p (h k) -> p h k", h=HH)
                pu = posn.bitcast(U32)[0:rows]
                p3 = pu.rearrange("p (h k) -> p h k", h=HH)
                rank(range(HH), lambda j: cand8[0:rows, half * HH + j, :], lambda j: b3[:, j, :],
                     lambda j: p3[:, j, :])
                abu = ab.bitcast(U32)[0:rows]
                me.did(ts(abu[:, 0:HALF], pu, 4, None, ALU.logical_shift_right))
                me.did(ts(abu[:, HALF:], pu, 15, None, ALU.bitwise_and))
                g3 = gates[0:rows, half * HALF:(half + 1) * HALF].rearrange("p (h k) -> p h k", h=HH)
                tt(g3, b3, b3[:, :, 0:1].to_broadcast([rows, HH, TK]), ALU.subtract).then_inc(best_shift, 1)
                me.sync()
                me.did(nc.vector.tensor_copy(abf[0:rows], abu))
                me.sync()
                one = proj[0:rows, half * D:(half + 1) * D].rearrange("p (n a) -> p n a", a=TK)
                iot = iota16[0:rows, :].rearrange("p (a k) -> p a k", a=1).to_broadcast([rows, HALF, TK])
                i4 = indf[0:rows].rearrange("p (h c k) -> p h c k", h=HH, c=2)
                for c in range(2):
                    me.did(tt(one, abf[0:rows, c * HALF:(c + 1) * HALF].rearrange("p (n a) -> p n a", a=1)
                              .to_broadcast([rows, HALF, TK]), iot, ALU.is_equal))
                    me.sync()
                    for hh in range(HH):
                        o3 = one[:, hh * TK:(hh + 1) * TK, :]
                        me.did(tt(o3, o3, i4[:, hh, c, :].rearrange("p (a k) -> p a k", a=1)
                                  .to_broadcast([rows, TK, TK]), ALU.mult))
                    me.sync()
                    me.did(nc.vector.tensor_reduce(chosen[0:rows, c * HALF:(c + 1) * HALF], one, AX, ALU.add))
                    me.sync()
                num = numbers[0:rows, half * HALF:(half + 1) * HALF]
                me.did(stt(num, chosen[0:rows, 0:HALF], float(NK), chosen[0:rows, HALF:], ALU.mult, ALU.add))
                v.wait_ge(best_exp, b * 2 + (half + 1))
                v.nop(nofuse=True)
                me.sync()
                if not isinstance(b, int) or b > 0:
                    v.wait_ge(idx_taken, b * 2)
                me.did(nc.vector.tensor_copy(idx[0:rows, half * HALF:(half + 1) * HALF], num))
                me.did(nc.vector.tensor_reduce(ssum[0:rows, 0:HH], g3, AX, ALU.add))
                me.sync()
                me.did(nc.vector.reciprocal(srec[0:rows, 0:HH], ssum[0:rows, 0:HH]))
                me.sync()
                tt(g3, g3, srec[0:rows, 0:HH].rearrange("p (h a) -> p h a", a=1).to_broadcast([rows, HH, TK]),
                   ALU.mult).then_inc(topk_done, 1)

            def front(step, b, mask, rows=P):
                if step == 1:
                    rotation(b)
                elif step == 3:
                    decay_scores(b)
                elif step == 4:
                    retention_out(b)
                elif step == 5:
                    window_max(b, mask)
                elif step == 7:
                    window_out(b)
                elif step == 9:
                    norm_output(b, rows)
                elif step == 11:
                    rank_halves(b, 0, rows)
                elif step == 12:
                    choose(b, 0, rows)
                elif step == 13:
                    hold(v, topk_done, b * 2 + 1)
                    rank_halves(b, 1, rows)
                elif step == 14:
                    choose(b, 1, rows)

            def take_over(b):
                v.wait_ge(topk_done, b * 2 + 2)
                if not isinstance(b, int) or b > 0:
                    v.nop(nofuse=True)
                    v.wait_ge(diags, b * (GROUPS * PAIRS))
                me.did(nc.vector.tensor_copy(x2g[:], x2))
                me.did(nc.vector.tensor_copy(gateg[:], gates[:]))
                me.sync()

            def expert_dots(b, g):
                def diagonals(p):
                    v.wait_ge(gelus, b * (GROUPS * PAIRS) + (g * PAIRS + p + 1))
                    for r in range(p * PAIR, (p + 1) * PAIR):
                        ins = ts(row_u[r][:, 0:P], ident[:], gel[:, r:r + 1],
                                 gateg[:, g * RING + r:g * RING + r + 1], ALU.mult, ALU.mult)
                    ins.then_inc(diags, 1)

                for p in range(PAIRS):
                    for r in range(p * PAIR, (p + 1) * PAIR):
                        v.wait_ge(ld_row[r], b * (GROUPS * 16) + (g * 16 + 16))
                        ins = stt(row_u[r], row_u[r], 1.0, x2g[:], ALU.mult, ALU.mult, accum_out=dot[:, r:r + 1])
                    ins.then_inc(dots, 1)
                    if p:
                        diagonals(p - 1)
                diagonals(PAIRS - 1)

            def block_out(b):
                v.wait_ge(acc_out, b + 1)
                me.did(stt(x2, xT, 1.0, xT, ALU.mult, ALU.mult, accum_out=fs1))
                me.sync()
                root(fs2, fs1, 1.0 / D)
                stt(xT, xT, fs2, gfb[:], ALU.mult, ALU.mult).then_inc(y_ready, 1)

            for step in range(1, GROUPS):
                front(step, 0, mask0)
                sample(step - SAMPLE_LAG)
            take_over(0)
            expert_dots(0, 0)
            with v.Fori(0, NB - 1) as b:
                me.enter(b, STEPS_PER_BLOCK)
                roots.enter(b, 3)
                for g in range(1, GROUPS):
                    expert_dots(b, g)
                    front(g, b + 1, wmask[:])
                take_over(b + 1)
                expert_dots(b + 1, 0)
                block_out(b)
                me.leave(NB - 1)
                roots.leave(NB - 1)
            for g in range(1, GROUPS):
                expert_dots(NB - 1, g)
                if g >= SAMPLE_STEP:
                    front(g + 8 - SAMPLE_STEP, NB, None, NS)
                if g + 8 - SAMPLE_STEP == 15:
                    v.wait_ge(topk_done, NB * 2 + 2)
                    nc.vector.tensor_copy(xT[0:NS, 0:P], numbers[0:NS, :]).then_inc(sm["spread"], 1)
            v.wait_ge(sm["rowsx"], 1)
            xr = x2g[:]
            me.did(nc.vector.tensor_copy(xr, FF(0, 2)))
            pick = qsT[:, P:2 * P]
            both = proj[:, 0:2 * P]
            for n in range(2):
                me.did(tt(both[:, n * P:(n + 1) * P], F[2][:, n * P:(n + 1) * P], pick, ALU.mult))
            me.sync()
            me.did(nc.vector.tensor_reduce(proj[:, 256:256 + 2 * PH],
                                           both.rearrange("p (n k) -> p n k", k=TK), AX, ALU.add))
            me.sync()
            nc.vector.tensor_copy(idx[:, 0:PH], proj[:, 256:256 + PH]).then_inc(sm["idx8"], 1)
            block_out(NB - 1)
            v.wait_ge(sm["idx8"], 1)
            for p in range(PAIRS):
                for r in range(p * PAIR, (p + 1) * PAIR):
                    v.wait_ge(ld_row[r], NB * GROUPS * 16 + 16)
                    ins = stt(row_u[r], row_u[r], 1.0, xr, ALU.mult, ALU.mult, accum_out=dot[:, r:r + 1])
                ins.then_inc(dots, 1)
            own = qsT[:, 2 * P:2 * P + NS]
            for p in range(PAIRS):
                v.wait_ge(gelus, NB * GROUPS * PAIRS + p + 1)
                for r in range(p * PAIR, (p + 1) * PAIR):
                    ins = ts(row_u[r][:, 0:NS], own, gel[:, r:r + 1], proj[:, 256 + PH + r:257 + PH + r],
                             ALU.mult, ALU.mult)
                ins.then_inc(diags, 1)
            v.wait_ge(used, NB * SLOTS + 2 * RING)
            ys = work[0:NS, 0:D]
            me.did(nc.vector.tensor_copy(ys, acc[0:NS, :]))
            me.sync()
            me.did(stt(row_u[0][0:NS, :], ys, 1.0, ys, ALU.mult, ALU.mult, accum_out=fs1[0:NS, :]))
            me.sync()
            root(fs2[0:NS, :], fs1[0:NS, :], 1.0 / D)
            stt(ys, ys, fs2[0:NS, :], gfb[0:NS, :], ALU.mult, ALU.mult).then_inc(y_ready, 1)


SAMPLE_LAG = 2
SAMPLE_STEP = 4
STEPS_PER_BLOCK = 203


_INS = ["x_prompt", "x_sample", "state_ret", "cache_swa_k", "cache_swa_v", "norm1_g", "swa_sinks", "w_out",
        "norm2_g", "final_g"]
_OUTS = [(1, SEQ, D), (NS, 1, D), (1, RH, HD, HD), (1, P, KVH, SD), (1, P, KVH, SD), (NS, RH, HD, HD),
         (NS, P, KVH, SD), (NS, P, KVH, SD)]


def constants():
    f = np.float32
    half = HD // 2
    inv = (f(1.0) / (f(10000.0) ** np.linspace(0.0, 1.0, half, dtype=f))).astype(f)
    pos = np.concatenate([np.arange(SEQ), np.full(NS, SEQ)]).astype(f)
    ang = (pos[:, None] * inv[None, :]).astype(f).astype(np.float64)
    cos, sin = np.cos(ang), np.sin(ang)
    t = np.arange(P)
    diff = t[None, :] - t[:, None]
    dmask = np.where(diff[:, None, :] >= 0, np.exp(np.maximum(diff, 0)[:, None, :] * LOG_DECAY[None, :, None]), 0.0)
    prev = np.where(t[None, :] > t[:, None], 0.0, MASKED)
    cur = np.where(t[None, :] <= t[:, None], 0.0, MASKED)
    s8, p16 = np.arange(NS), t // TK
    pick = np.tile(t[:, None] % TK == np.arange(TK)[None, :], (1, PH))
    out = {
        "c_rope": np.concatenate([cos, sin, cos * K_SCALE, sin * K_SCALE], 1),
        "c_ident": np.eye(P),
        "c_dmaskT": dmask.reshape(P, RH * P),
        "c_qdec": np.exp((t[:, None] + 1.0) * LOG_DECAY[None, :]),
        "c_kdec": np.exp((P - 1.0 - t[:, None]) * LOG_DECAY[None, :]),
        "c_iota": np.tile(np.arange(TK), (P, 1)),
        "c_wmask": np.concatenate([prev, cur], 1),
        "c_wmask0": np.concatenate([np.full((P, P), MASKED), cur], 1),
        "c_sel8": np.repeat(np.eye(NS), P, axis=1),
        "c_spread": (s8[:, None] == p16[None, :]),
        "c_pick": np.concatenate([pick, p16[:, None] == s8[None, :]], 1),
    }
    return {k: np.ascontiguousarray(v.astype(f)) for k, v in out.items()}


def kernel(**inputs):
    import concourse.bacc as _bacc
    from concourse.bass_utils import run_bass_kernel_spmd as _run

    nc = _bacc.Bacc("TRN2", target_bir_lowering=False, num_devices=1)
    arrays = {n: np.ascontiguousarray(inputs[n]) for n in _INS}
    w_in = np.asarray(inputs["w_in"])
    qs = w_in[:, C_QS:C_KS].reshape(D, KVH, GRP, SD).transpose(0, 2, 1, 3).reshape(D, QH * SD)
    arrays["w_in"] = np.concatenate([w_in[:, :C_QS], qs, w_in[:, C_KS:]], axis=1)
    arrays["wqT"] = np.ascontiguousarray(np.asarray(inputs["peer_w_q"]).reshape(D, NHC, NK).transpose(1, 2, 0))
    arrays["sub_keysT"] = np.ascontiguousarray(
        np.asarray(inputs["peer_sub_keys"]).transpose(3, 0, 1, 2).reshape(NK, NSC))
    arrays["peer_uv"] = np.concatenate([np.asarray(inputs["peer_u"]), np.asarray(inputs["peer_v"])], axis=1)
    arrays.update(constants())
    args = {n: nc.dram_tensor("in_" + n, a.shape, mybir.dt.from_np(a.dtype), kind="ExternalInput").ap()
            for n, a in arrays.items()}
    outs = [nc.dram_tensor(f"out_{i}", shape, F32, kind="ExternalOutput").ap() for i, shape in enumerate(_OUTS)]
    build(nc, args, outs)
    r = _run(nc, [{"in_" + n: a for n, a in arrays.items()}], core_ids=[0])
    return tuple(r.results[0][f"out_{i}"] for i in range(len(_OUTS)))
```

```python
from contextlib import ExitStack

import numpy as np

import concourse.bass as bass
from concourse import mybir

F32 = mybir.dt.float32
U32 = mybir.dt.uint32
ALU = mybir.AluOpType
ACT = mybir.ActivationFunctionType
AX = mybir.AxisListType.X

P = 128
D = 1024
KC = D // P
SEQ = 1024
NB = SEQ // P
NS = 8
NTOK = SEQ + NS
RH, HD = 4, 128
QH, KVH, SD = 8, 2, 64
GRP = QH // KVH
D_IN = 4 * RH * HD + QH * SD + 2 * KVH * SD
C_Q, C_K, C_V, C_G = 0, 512, 1024, 1536
C_QS, C_KS, C_VS = 2048, 2560, 2688
C_MIX = C_G
PH, TK, NK = 8, 16, 128
NHC = 2 * PH
NSC = NHC * NK
SLOTS = PH * TK
HALF = SLOTS // 2
RING = 8
ROWW = 2 * D
GROUPS = SLOTS // RING
PAIR = 2
PAIRS = RING // PAIR
NCH = 8
CW = D_IN // NCH
BANKS = 4
STG = 4
TILES = NB + 1
FIRST = 2 * NCH
REST = (NB - 1) * NCH
EPS = 1e-6
K_SCALE = HD ** -0.5
S_SCALE = SD ** -0.5
LOG_DECAY = np.log(1.0 - 2.0 ** (-5.0 - np.arange(RH)))
STEP_DECAY = [float(v) for v in np.exp(LOG_DECAY)]
BLOCK_DECAY = [float(v) for v in np.exp(P * LOG_DECAY)]
MASKED = -1e30
TAKEN = -3.0e38


def step_at(table, tiles):
    return next((step for step, at in table.items() if at == tiles), 0)


class Steps:

    def __init__(self, eng, sem):
        self.eng, self.sem, self.n, self.base = eng, sem, 0, 0

    def did(self, ins):
        self.n += 1
        ins.then_inc(self.sem, 1)

    def sync(self):
        self.eng.wait_ge(self.sem, self.base + self.n)

    def enter(self, turn, per):
        self.first, self.per = self.n, per
        self.base = turn * per

    def leave(self, turns):
        assert self.n - self.first == self.per, (self.n - self.first, self.per)
        self.base, self.n = 0, self.first + turns * self.per


def hold(eng, sem, count):
    eng.wait_ge(sem, count)
    eng.nop(nofuse=True)


def build(nc, A, out):
    ctx = ExitStack()
    with ctx:
        def sb(name, shape, dt=F32):
            return ctx.enter_context(nc.sbuf_tensor(name, shape, dt))

        def sem(name):
            return ctx.enter_context(nc.semaphore(name))

        ring = sb("ring", [P, RING * ROWW])
        keyw = sb("keyw", [P, KC, NSC])
        wo = sb("wo", [P, KC, D])
        proj = sb("proj", [P, D_IN])
        work = sb("work", [P, 2 * D])
        h = sb("h", [P, D])
        x2g = sb("x2g", [P, D])
        g2b = sb("g2b", [P, D])
        gfb = sb("gfb", [P, D])
        qsT = sb("qsT", [P, 512])
        kTb = sb("kTb", [P, 2 * P])
        vprev = sb("vprev", [P, P])
        state = sb("state", [P, RH, HD])
        dmaskT = sb("dmaskT", [P, RH, P])
        wmask = sb("wmask", [P, 2 * P])
        ident = sb("ident", [P, P])
        idx = sb("idx", [P, SLOTS], U32)
        gates = sb("gates", [P, SLOTS])
        idxg = sb("idxg", [P, SLOTS], U32)
        gateg = sb("gateg", [P, SLOTS])
        idxst = sb("idxst", [P, 2 * RING], U32)
        small = sb("small", [P, 160])
        mixTs = sb("mixTs", [P, KC * NS])
        ps = ctx.enter_context(nc.psum_tensor("ps", [P, 8, 512], F32))
        acc = ps[:, 0:2, :].rearrange("p a b -> p (a b)")
        F = [ps[:, 2 + i, :] for i in range(6)]

        def FF(a, b):
            return ps[:, 2 + a:2 + b, :].rearrange("p a b -> p (a b)")

        row_u = [ring[:, r * ROWW:r * ROWW + D] for r in range(RING)]
        row_v = [ring[:, r * ROWW + D:(r + 1) * ROWW] for r in range(RING)]
        row = [ring[:, r * ROWW:(r + 1) * ROWW] for r in range(RING)]
        x2, xT = work[:, 0:D], work[:, D:2 * D]
        rope = qsT[:, 0:256]

        at = [0]

        def cols(n):
            at[0] += n
            return small[:, at[0] - n:at[0]]

        g1c, qdec, kdec, sinkb, iota16 = cols(8), cols(4), cols(4), cols(8), cols(16)
        ssq, rstd, mx, nmx, rs, es, rden = cols(4), cols(4), cols(8), cols(8), cols(8), cols(8), cols(8)
        hs1, hs2, fs1, fs2 = cols(1), cols(1), cols(1), cols(1)
        ssum, srec = cols(8), cols(8)
        dot, gel = cols(RING), cols(RING)
        qk, sinks64, m64, n64, r64, e64 = cols(4), cols(1), cols(1), cols(1), cols(1), cols(1)
        ssqs, rstds = cols(4), cols(4)
        tok_sum, tok_root = (hs1, fs1), (hs2, fs2)

        o1 = [0]

        def part(n):
            o1[0] += n
            return ring[:, o1[0] - n:o1[0]]

        projs = part(D_IN)
        ropes = part(256)
        sT = part(96)
        ss = part(64)
        sr = part(P)
        pts = part(64)
        osT = part(32)
        wbuf = [part(KC * CW).rearrange("p (k n) -> p k n", k=KC)]
        early_rows = o1[0] // ROWW
        wbuf.append(part(KC * CW).rearrange("p (k n) -> p k n", k=KC))
        xTrest = part(KC * (NB - 1) * P).rearrange("p (k t) -> p k t", k=KC)
        xa = [h[:, :], x2g[:, :]]
        wqT = [work[:, 0:D], work[:, D:2 * D]]
        staging = [(x2g, gfb)[i // 2][:, i % 2 * CW:(i % 2 + 1) * CW] for i in range(STG)]
        mask0 = x2g[:, 2 * CW:2 * CW + 2 * P]

        wof = wo[:].rearrange("p k n -> p (k n)")
        skT = wof[:, 0:NSC]
        xTfirst = wof[:, NSC:NSC + KC * (P + NS)].rearrange("p (k t) -> p k t", k=KC)
        kw = wof[:, 0:NS * P].rearrange("p (s c) -> p s c", s=NS)
        vw = wof[:, D:D + NS * P].rearrange("p (s c) -> p s c", s=NS)
        kwT, sel8 = wof[:, 2 * D:3 * D], wof[:, 3 * D:4 * D]
        st_s = wof[:, 4 * D:8 * D].rearrange("p (s h e) -> p s h e", s=NS, h=RH)

        def token_rows(n):
            return NS if n == 1 else P

        def tokens_T(n, k):
            if n < 2:
                return xTfirst[:, k, n * P:n * P + token_rows(n)]
            return xTrest[:, k, (n - 2) * P:(n - 1) * P]

        ld_first, ld_const, ld_skT = sem("ld_first"), sem("ld_const"), sem("ld_skT")
        ld_wq = [sem("ld_wq0"), sem("ld_wq1")]
        ld_x = [sem("ld_x0"), sem("ld_x1")]
        ld_w = [sem("ld_w0"), sem("ld_w1")]
        ld_wo, ld_gf = sem("ld_wo"), sem("ld_gf")
        keyw_mm, keyw_out = sem("keyw_mm"), sem("keyw_out")
        root_in, root_out = sem("root_in"), sem("root_out")
        xn_ready, xn_T, xn_out = sem("xn_ready"), sem("xn_T"), sem("xn_out")
        pj_mm, pj_out = sem("pj_mm"), sem("pj_out")
        st_pj = [sem(f"st_pj{i}") for i in range(STG)]
        zeroed = sem("zeroed")
        dve_steps, act_steps = sem("dve_steps"), sem("act_steps")
        ld_proj, ld_res, ld_mask0 = sem("ld_proj"), sem("ld_res"), sem("ld_mask0")
        roped, kd_ready = sem("roped"), sem("kd_ready")
        qkT_mm, qkT_out = sem("qkT_mm"), sem("qkT_out")
        st_mm, stm_ready, ret_mm, silu_ready, mixr_ready = (sem("st_mm"), sem("stm_ready"), sem("ret_mm"),
                                                            sem("silu_ready"), sem("mixr_ready"))
        qsT_mm, qsT_out, sw_mm, sw_nmax, sw_exp = (sem("qsT_mm"), sem("qsT_out"), sem("sw_mm"), sem("sw_nmax"),
                                                   sem("sw_exp"))
        pT_mm, pT_out, sw_o, mixs_ready = (sem("pT_mm"), sem("pT_out"), sem("sw_o"),
                                                        sem("mixs_ready"))
        mixT_mm, mixT_out, o_mm, x2_ready = sem("mixT_mm"), sem("mixT_out"), sem("o_mm"), sem("x2_ready")
        x2T_mm, x2T_out, sc_mm, sc_out = sem("x2T_mm"), sem("x2T_out"), sem("sc_mm"), sem("sc_out")
        best_shift, best_exp, topk_done = sem("best_shift"), sem("best_exp"), sem("topk_done")
        idx_taken, acc_out = sem("idx_taken"), sem("acc_out")
        ld_row = [sem(f"ld_row{r}") for r in range(RING)]
        staged, dots, gelus, diags, used = sem("staged"), sem("dots"), sem("gelus"), sem("diags"), sem("used")
        residual_in, y_ready, st_y = sem("residual_in"), sem("y_ready"), sem("st_y")
        st_misc, st_state = sem("st_misc"), sem("st_state")
        sm = {n: sem("smp_" + n) for n in (
            "kw", "vw", "sel", "qT", "qT_out", "kwT", "kwT_out", "s", "s_out", "sr", "nmax", "exp", "p", "pT",
            "pT_out", "qS", "qS_out", "qSn", "mixr", "mixT", "mixT_out", "vb", "vb_used", "st", "spread", "idx8",
            "rowsx", "roped", "columns", "silu_out", "kv")}

        proj_d = nc.dram_tensor("proj_scratch", [NTOK, D_IN], F32).ap()
        w_in_v = A["w_in"].rearrange("(k p) n -> p k n", p=P)
        x_p = A["x_prompt"].rearrange("a t d -> (a t) d")
        x_s = A["x_sample"].rearrange("a t d -> (a t) d")
        y_p = out[0].rearrange("a t d -> (a t) d")
        y_s = out[1].rearrange("a t d -> (a t) d")
        N_CONST = 8 + NS

        block = ctx.enter_context(nc.Block())

        def rows_of(vector, n):
            return vector.rearrange("(a n) -> a n", a=1).to_broadcast([P, n])

        @block.sync
        def _(sp):
            def load_x(n):
                if n >= 2:
                    sp.wait_ge(xn_T, n - 1)
                src = x_s if n == 1 else x_p[max(n - 1, 0) * P:max(n, 1) * P, :]
                sp.dma_start(xa[n % 2][0:token_rows(n), :], src).then_inc(ld_x[n % 2], 16)

            def load_w(n):
                if n >= 2:
                    sp.wait_ge(pj_mm, 2 * (n - 1) if n - 2 < NCH else FIRST + (NB - 1) * (n - 1 - NCH))
                c = n % NCH
                sp.dma_start(wbuf[n % 2], w_in_v[:, :, c * CW:(c + 1) * CW]).then_inc(ld_w[n % 2], 16)

            def load_wqT(n):
                if n >= 2:
                    sp.wait_ge(keyw_mm, 2 * n - 2)
                sp.dma_start(wqT[n % 2], A["wqT"][n]).then_inc(ld_wq[n % 2], 16)

            load_x(0)
            for dst, src in [(ident[:], A["c_ident"]), (g1c, A["norm1_g"].rearrange("(k p) -> p k", p=P))]:
                sp.dma_start(dst, src, allow_slow_non_contiguous=True).then_inc(ld_first, 16)
            load_x(1)
            load_w(0)
            load_x(2)
            load_w(1)
            load_x(3)
            sp.dma_start(skT, A["sub_keysT"]).then_inc(ld_skT, 16)
            load_wqT(0)
            load_wqT(1)
            for c in range(NCH):
                if c + 4 < TILES:
                    load_x(c + 4)
                if 2 * c + 2 < NHC:
                    load_wqT(2 * c + 2)
                load_w(c + 2)
                if 2 * c + 3 < NHC:
                    load_wqT(2 * c + 3)

            sp.wait_ge(pj_out, FIRST)
            sp.dma_start(proj_d[SEQ:NTOK, C_KS:D_IN], projs[0:NS, C_KS:D_IN]).then_inc(sm["kv"], 16)
            sp.dma_start(ropes[0:NS, :], A["c_rope"][SEQ:NTOK, :]).then_inc(sm["columns"], 16)
            sp.wait_ge(pj_mm, FIRST)
            sp.wait_ge(keyw_mm, 2 * NHC)
            for s in range(NS):
                sp.dma_start(kw[0:P - 1, s, :], A["cache_swa_k"][s, 1:P].rearrange("w k d -> w (k d)")
                             ).then_inc(sm["kw"], 16)
            sp.dma_start(st_s.rearrange("p s h e -> p (s h) e"),
                         A["state_ret"].rearrange("s h d e -> d (s h) e")).then_inc(sm["kw"], 16)
            sp.wait_ge(sm["kv"], 16)
            sp.dma_start(kw[P - 1:P, :, :], proj_d[SEQ:NTOK, C_KS:C_VS].rearrange("(a s) c -> a s c", a=1)
                         ).then_inc(sm["kw"], 16)
            for s in range(NS):
                sp.dma_start(vw[0:P - 1, s, :], A["cache_swa_v"][s, 1:P].rearrange("w k d -> w (k d)")
                             ).then_inc(sm["vw"], 16)
            sp.dma_start(vw[P - 1:P, :, :], proj_d[SEQ:NTOK, C_VS:D_IN].rearrange("(a s) c -> a s c", a=1)
                         ).then_inc(sm["vw"], 16)
            sp.dma_start(sel8[0:NS, :], A["c_sel8"]).then_inc(sm["vw"], 16)
            sp.wait_ge(xn_T, TILES)
            sp.dma_start(mask0, A["c_wmask0"]).then_inc(ld_mask0, 16)
            loads = [(qdec, A["c_qdec"]), (kdec, A["c_kdec"]), (iota16, A["c_iota"]),
                     (sinkb, rows_of(A["swa_sinks"], QH)),
                     (dmaskT[:].rearrange("p h m -> p (h m)"), A["c_dmaskT"]), (wmask[:], A["c_wmask"]),
                     (g2b[:], rows_of(A["norm2_g"], D)), (rope, A["c_rope"][0:P, :])]
            loads += [(sinks64[s * QH:(s + 1) * QH, :], A["swa_sinks"].rearrange("(q a) -> q a", a=1))
                      for s in range(NS)]
            for dst, src in loads:
                sp.dma_start(dst, src, allow_slow_non_contiguous=True).then_inc(ld_const, 16)

            for q in range(REST):
                c, i = q // (NB - 1), q % (NB - 1) + 1
                sp.wait_ge(pj_out, FIRST + q + 1)
                sp.dma_start(proj_d[i * P:(i + 1) * P, c * CW:(c + 1) * CW], staging[q % STG]
                             ).then_inc(st_pj[q % STG], 16)
                if i == NB - 1 and c + 2 < NCH:
                    load_w(NCH + c + 2)
                if q == 8:
                    sp.wait_ge(sm["kw"], 16 * (NS + 2))
                    sp.wait_ge(sm["vw"], 16 * (NS + 2))
                    sp.dma_start(out[6].rearrange("s w k d -> w s (k d)"), kw).then_inc(st_misc, 16)
                    sp.dma_start(out[7].rearrange("s w k d -> w s (k d)"), vw).then_inc(st_misc, 16)
                if q == 18:
                    sp.wait_ge(sm["mixr"], 1)
                    sp.dma_start(h[:], x_p[0:P, :]).then_inc(ld_res, 16)
                    sp.wait_ge(sm["st"], 1)
                    sp.dma_start(out[5].rearrange("s h d e -> d (s h) e"), st_s.rearrange("p s h e -> p (s h) e")
                                 ).then_inc(st_state, 16)
                    sp.wait_ge(st_state, 16)
                    sp.wait_ge(st_misc, 32)
                    sp.dma_start(wo[:], A["w_out"].rearrange("(k p) n -> p k n", p=P)).then_inc(ld_wo, 16)
            for q in st_pj:
                sp.wait_ge(q, 16 * REST // STG)
            sp.dma_start(gfb[:], rows_of(A["final_g"], D), allow_slow_non_contiguous=True).then_inc(ld_gf, 16)
            sp.dma_start(out[3][0].rearrange("w k d -> w (k d)"), proj_d[SEQ - P:SEQ, C_KS:C_VS]).then_inc(st_misc, 16)
            sp.dma_start(out[4][0].rearrange("w k d -> w (k d)"), proj_d[SEQ - P:SEQ, C_VS:D_IN]).then_inc(st_misc, 16)

            def load_columns(b):
                sp.dma_start(proj[:], proj_d[bass.ds(b * P, P), :]).then_inc(ld_proj, 16)
                sp.dma_start(rope, A["c_rope"][bass.ds(b * P, P), :]).then_inc(ld_proj, 16)

            def load_residual(b):
                sp.wait_ge(residual_in, b)
                sp.dma_start(h[:], x_p[bass.ds(b * P, P), :]).then_inc(ld_res, 16)

            def store_y(b):
                sp.wait_ge(y_ready, b + 1)
                sp.dma_start(y_p[bass.ds(b * P, P), :], xT).then_inc(st_y, 16)

            sp.wait_ge(topk_done, 2)
            load_columns(1)
            with sp.Fori(0, NB - 2) as b:
                load_residual(b + 1)
                store_y(b)
                sp.wait_ge(st_y, b * 16 + 16)
                load_columns(b + 2)
            load_residual(NB - 1)
            store_y(NB - 2)
            sp.wait_ge(st_y, 16 * (NB - 1))
            sp.wait_ge(residual_in, NB)
            sp.dma_start(h[0:NS, :], x_s).then_inc(ld_res, 16)
            sp.wait_ge(mixs_ready, NB)
            sp.dma_start(out[2][0].rearrange("h d e -> d h e"), state[:]).then_inc(st_misc, 16)
            sp.dma_start(qsT[0:NS, 0:P], A["c_spread"]).then_inc(sm["sel"], 16)
            sp.dma_start(qsT[:, P:2 * P + NS], A["c_pick"]).then_inc(sm["sel"], 16)
            sp.wait_ge(y_ready, NB)
            sp.dma_start(y_p[(NB - 1) * P:NB * P, :], xT).then_inc(st_y, 16)
            sp.wait_ge(y_ready, NB + 1)
            sp.dma_start(y_s, work[0:NS, 0:D]).then_inc(st_y, 16)
            sp.wait_ge(st_y, 16 * (NB + 1))
            sp.wait_ge(st_misc, 80)

        @block.gpsimd
        def _(pool):
            pool.wait_ge(sm["vb_used"], NS)
            pool.wait_ge(pj_mm, FIRST + REST - (NB - 1))

            def fetch(r, col):
                nc.gpsimd.indirect_dma_start(row[r], None, A["peer_uv"],
                                             bass.IndirectOffsetOnAxis(ap=idxst[:, col:col + 1], axis=0)
                                             ).then_inc(ld_row[r], 16)

            with pool.Fori(0, NB) as b:
                for half in range(2):
                    hold(pool, topk_done, b * 2 + (half + 1))
                    own = slice(half * HALF, (half + 1) * HALF)
                    nc.gpsimd.tensor_copy(idxg[:, own], idx[:, own]).then_inc(idx_taken, 1)
                    hold(pool, idx_taken, b * 2 + (half + 1))
                    with pool.Fori(0, PH // 2) as hd:
                        for part_ in range(2):
                            c0 = part_ * RING
                            nc.gpsimd.tensor_copy(idxst[:, c0:c0 + RING],
                                                  idxg[:, bass.ds(hd * TK + (half * HALF + c0), RING)]
                                                  ).then_inc(staged, 1)
                            hold(pool, staged, b * (2 * PH) + hd * 2 + (half * PH + part_ + 1))
                            for r in range(RING):
                                if r == early_rows:
                                    hold(pool, pj_mm, FIRST + REST)
                                hold(pool, used, b * SLOTS + hd * TK + (half * HALF + c0 + r + 1))
                                fetch(r, c0 + r)
            pool.wait_ge(sm["idx8"], 1)
            for hd in range(PH):
                hold(pool, used, NB * SLOTS + hd + 1)
                nc.gpsimd.indirect_dma_start(row[hd], None, A["peer_uv"],
                                             bass.IndirectOffsetOnAxis(ap=idx[:, hd:hd + 1], axis=0)
                                             ).then_inc(ld_row[hd], 16)

        @block.tensor
        def _(pe):
            def T(o, i, n=P):
                return nc.tensor.transpose(o, i, ident[0:n, 0:n])

            pe.wait_ge(ld_first, 32)

            def token_transposes(n):
                rows = token_rows(n)
                pe.wait_ge(xn_ready, n + 1)
                if n:
                    pe.wait_ge(xn_out, n)
                for k in range(KC):
                    t = T(acc[:, k * P:k * P + rows], xa[n % 2][0:rows, k * P:(k + 1) * P], rows)
                t.then_inc(xn_T, 1)

            def project(bank, n, buf):
                for k in range(KC):
                    mm = nc.tensor.matmul(bank[0:token_rows(n), 0:CW], tokens_T(n, k), buf[:, k, :],
                                          start=(k == 0), stop=(k == KC - 1))
                mm.then_inc(pj_mm, 1)

            def project_first(c, n):
                tile = 2 * c + n
                if tile >= BANKS:
                    pe.wait_ge(pj_out, tile - (BANKS - 1))
                project(F[tile % BANKS], n, wbuf[c % 2])

            def project_rest(q):
                c, i = q // (NB - 1), q % (NB - 1) + 1
                if i == 1:
                    pe.wait_ge(ld_w[c % 2], 16 * ((NCH + c) // 2 + 1))
                if q >= 2:
                    pe.wait_ge(pj_out, FIRST + q - 1)
                project(acc[:, q % 2 * 512:(q % 2 + 1) * 512], i + 1, wbuf[c % 2])

            def key_weights(n):
                pe.wait_ge(ld_wq[n % 2], 16 * (n // 2 + 1))
                for half in range(2):
                    pe.wait_ge(keyw_out, 2 * n + half + 1)
                    for k in range(4):
                        mm = nc.tensor.matmul(acc[:, (half * 4 + k) * P:(half * 4 + k + 1) * P],
                                              wqT[n % 2][:, (half * 4 + k) * P:(half * 4 + k + 1) * P],
                                              skT[:, n * NK:(n + 1) * NK], start=True, stop=True)
                    mm.then_inc(keyw_mm, 1)

            token_transposes(0)
            token_transposes(1)
            for c in range(NCH):
                if c + 2 < TILES:
                    pe.wait_ge(keyw_out, 4 * c + 2)
                    token_transposes(c + 2)
                pe.wait_ge(ld_w[c % 2], 16 * (c // 2 + 1))
                project_first(c, 0)
                if c == 0:
                    pe.wait_ge(ld_skT, 16)
                pe.wait_ge(xn_out, min(c + 3, TILES))
                key_weights(2 * c)
                project_first(c, 1)
                key_weights(2 * c + 1)

            SA, SB = F[0], F[1]
            sq = sT[:, 64:96].rearrange("p (i s) -> p i s", i=GRP)

            def sample(step):
                if step == 2:
                    pe.wait_ge(sm["roped"], 1)
                    pe.wait_ge(pj_out, FIRST)
                    for j in range(8):
                        T(SA[:, j * NS:(j + 1) * NS], projs[0:NS, j * P:(j + 1) * P], NS)
                    for j in range(4):
                        t = T(SA[:, 64 + j * NS:64 + (j + 1) * NS], projs[0:NS, C_QS + j * P:C_QS + (j + 1) * P], NS)
                    t.then_inc(sm["qT"], 1)
                    pe.wait_ge(sm["kw"], 16 * (NS + 2))
                    for s in range(4):
                        t = T(SB[:, s * P:(s + 1) * P], kw[:, s, :])
                    t.then_inc(sm["kwT"], 1)
                elif step == 3:
                    pe.wait_ge(sm["qT_out"], 1)
                    for hh in range(RH):
                        for s in range(NS):
                            mm = nc.tensor.matmul(SA[:, 96 + hh * NS + s:97 + hh * NS + s], st_s[:, s, hh, :],
                                                  sT[:, hh * NS + s:hh * NS + s + 1], start=True, stop=True)
                    mm.then_inc(sm["qS"], 1)
                    pe.wait_ge(sm["kwT_out"], 1)
                    for s in range(4, NS):
                        t = T(SB[:, (s - 4) * P:(s - 3) * P], kw[:, s, :])
                    t.then_inc(sm["kwT"], 1)
                elif step == 4:
                    pe.wait_ge(sm["kwT_out"], 2)
                    for s in range(NS):
                        for j in range(KVH):
                            o = (SA[:, 128:160], SB[:, 0:32])[j]
                            mm = nc.tensor.matmul(o[:, s * GRP:(s + 1) * GRP],
                                                  kwT[j * SD:(j + 1) * SD, s * P:(s + 1) * P],
                                                  sq[j * SD:(j + 1) * SD, :, s], start=True, stop=True)
                    mm.then_inc(sm["s"], 1)
                elif step == 5:
                    pe.wait_ge(sm["s_out"], 1)
                    T(SA[0:64, 160:288], ss).then_inc(sm["sr"], 1)
                    pe.wait_ge(sm["qS_out"], 1)
                    for hh in range(RH):
                        t = T(SB[0:NS, hh * P:(hh + 1) * P], osT[:, hh * NS:(hh + 1) * NS])
                    t.then_inc(sm["qSn"], 1)
                elif step == 6:
                    pe.wait_ge(sm["p"], 1)
                    T(SA[:, 288:352], sr[0:64, :], 64).then_inc(sm["pT"], 1)
                elif step == 7:
                    pe.wait_ge(sm["pT_out"], 1)
                    pe.wait_ge(sm["vw"], 16 * (NS + 2))
                    ov = SA[:, 352:384].rearrange("p (c s) -> p c s", c=4)
                    pv = pts.rearrange("p (s j a b) -> p s j a b", s=NS, j=KVH, a=2)
                    for s in range(NS):
                        for j in range(KVH):
                            for half in range(2):
                                nc.tensor.matmul(ov[half * SD:(half + 1) * SD, 2 * j:2 * j + 2, s],
                                                 vw[:, s, j * SD:(j + 1) * SD], pv[:, s, j, :, half],
                                                 start=True, stop=True)
                    pe.wait_ge(sm["mixr"], 1)
                    for hh in range(RH):
                        t = T(SA[:, 384 + hh * NS:384 + (hh + 1) * NS],
                              projs[0:NS, C_MIX + hh * P:C_MIX + (hh + 1) * P], NS)
                    t.then_inc(sm["mixT"], 1)
                elif step == 8:
                    pe.wait_ge(sm["mixT_out"], 1)
                    for s in range(NS):
                        if s >= 2:
                            pe.wait_ge(sm["vb_used"], s - 1)
                        nc.tensor.matmul((SA, SB)[s % 2], sel8[0:NS, s * P:(s + 1) * P], projs[0:NS, C_V:C_V + 512],
                                         start=True, stop=True).then_inc(sm["vb"], 1)

            def transposes(b):
                pe.wait_ge(roped, b + 1)
                for j in range(8):
                    t = T(FF(0, 2)[:, j * P:(j + 1) * P], proj[:, j * P:(j + 1) * P])
                t.then_inc(qkT_mm, 1)
                for j in range(4):
                    T(F[2][:, j * P:(j + 1) * P], proj[:, C_QS + j * P:C_QS + (j + 1) * P])
                T(F[3][:, 0:P], proj[:, C_KS:C_VS]).then_inc(qsT_mm, 1)

            def retention_scores(b):
                pe.wait_ge(qkT_out, b + 1)
                for hh in range(RH):
                    mm = nc.tensor.matmul(F[0][:, hh * P:(hh + 1) * P], xT[:, 512 + hh * P:512 + (hh + 1) * P],
                                          xT[:, hh * P:(hh + 1) * P], start=True, stop=True)
                mm.then_inc(st_mm, 1)
                pe.wait_ge(qsT_out, b + 1)
                for hh in range(RH):
                    nc.tensor.matmul(F[3][:, hh * P:(hh + 1) * P], xT[:, hh * P:(hh + 1) * P], state[:, hh, :],
                                     start=True, stop=True)
                pe.wait_ge(kd_ready, b + 1)
                for hh in range(RH):
                    nc.tensor.matmul(F[4][:, hh * P:(hh + 1) * P], x2[:, 512 + hh * P:512 + (hh + 1) * P],
                                     proj[:, C_V + hh * P:C_V + (hh + 1) * P], start=True, stop=True)

            def retention_values(b):
                pe.wait_ge(stm_ready, b + 1)
                for hh in range(RH):
                    mm = nc.tensor.matmul(F[5][:, hh * P:(hh + 1) * P], x2[:, hh * P:(hh + 1) * P],
                                          proj[:, C_V + hh * P:C_V + (hh + 1) * P], start=True, stop=True)
                mm.then_inc(ret_mm, 1)

            def window_scores(b):
                pe.wait_ge(mixr_ready, b + 1)
                for j in range(KVH):
                    for i in range(GRP):
                        bank = F[2 + 2 * j + i // 2]
                        mm = nc.tensor.matmul(bank[:, i % 2 * 256:i % 2 * 256 + 256],
                                              qsT[j * SD:(j + 1) * SD, i * P:(i + 1) * P],
                                              kTb[j * SD:(j + 1) * SD, :], start=True, stop=True)
                mm.then_inc(sw_mm, 1)

            def window_transposes(b):
                pe.wait_ge(sw_exp, b + 1)
                for j in range(KVH):
                    for q in range(8):
                        t = T(FF(2 * j, 2 * j + 2)[:, q * P:(q + 1) * P],
                              work[:, j * D + q * P:j * D + (q + 1) * P])
                    t.then_inc(pT_mm, 1)

            def window_values(b):
                pe.wait_ge(pT_out, b * 2 + 2)
                for j in range(KVH):
                    for i in range(GRP):
                        o = F[4][:, (j * GRP + i) * SD:(j * GRP + i + 1) * SD]
                        pT = work[:, j * D + i * 256:j * D + (i + 1) * 256]
                        nc.tensor.matmul(o, pT[:, 0:P], vprev[:, j * SD:(j + 1) * SD], start=True, stop=False)
                        mm = nc.tensor.matmul(o, pT[:, P:2 * P], proj[:, C_VS + j * SD:C_VS + (j + 1) * SD],
                                              start=False, stop=True)
                mm.then_inc(sw_o, 1)

            def mix_transposes(b):
                pe.wait_ge(mixs_ready, b + 1)
                for k in range(KC):
                    t = T(FF(0, 2)[:, k * P:(k + 1) * P], proj[:, C_MIX + k * P:C_MIX + (k + 1) * P])
                t.then_inc(mixT_mm, 1)

            def output_projection(b, n, rows=P):
                if rows == P and n == 0:
                    pe.wait_ge(mixT_out, b + 1)
                for k in range(KC):
                    lhsT = xT[:, k * P:(k + 1) * P] if rows == P else mixTs[:, k * NS:(k + 1) * NS]
                    mm = nc.tensor.matmul(F[2 + n][0:rows, :], lhsT, wo[:, k, n * 512:(n + 1) * 512],
                                          start=(k == 0), stop=(k == KC - 1))
                mm.then_inc(o_mm, 1)

            def token_transposes2(b, rows=P):
                pe.wait_ge(x2_ready, b + 1)
                for k in range(KC):
                    t = T(FF(0, 2)[:, k * P:k * P + rows], x2[0:rows, k * P:(k + 1) * P], rows)
                t.then_inc(x2T_mm, 1)

            def key_scores(b, n, rows=P):
                if n == 0:
                    pe.wait_ge(x2T_out, b + 1)
                for k in range(KC):
                    mm = nc.tensor.matmul(F[2 + n][0:rows, :], xT[:, k * P:k * P + rows],
                                          keyw[:, k, n * 512:(n + 1) * 512],
                                          start=(k == 0), stop=(k == KC - 1))
                mm.then_inc(sc_mm, 1)

            def front_mid(step, b, rows=P):
                if step == 9:
                    output_projection(b, 1, rows)
                elif step == 11:
                    key_scores(b, 1, rows)
                elif step == 12:
                    key_scores(b, 3, rows)

            def front(step, b, rows=P):
                if step == 1:
                    transposes(b)
                elif step == 2:
                    retention_scores(b)
                elif step == 3:
                    retention_values(b)
                elif step == 4:
                    window_scores(b)
                elif step == 5:
                    window_transposes(b)
                elif step == 6:
                    window_values(b)
                elif step == 7:
                    mix_transposes(b)
                elif step == 8:
                    output_projection(b, 0, rows)
                elif step == 9:
                    token_transposes2(b, rows)
                elif step == 10:
                    key_scores(b, 0, rows)
                elif step == 11:
                    key_scores(b, 2, rows)

            def add_residual(b):
                for n in range(2):
                    mm = nc.tensor.matmul(acc[:, n * 512:(n + 1) * 512], ident[:], h[:, n * 512:(n + 1) * 512],
                                          start=True, stop=False, skip_group_check=True)
                mm.then_inc(residual_in, 1)

            def add_experts(b, g, pairs=range(PAIRS)):
                for p in pairs:
                    pe.wait_ge(diags, b * (GROUPS * PAIRS) + (g * PAIRS + p + 1))
                    for r in range(p * PAIR, (p + 1) * PAIR):
                        for n in range(2):
                            mm = nc.tensor.matmul(acc[:, n * 512:(n + 1) * 512], row_u[r][:, 0:P],
                                                  row_v[r][:, n * 512:(n + 1) * 512],
                                                  start=False, stop=False, skip_group_check=True)
                        mm.then_inc(used, 1)

            def spread_samples():
                pe.wait_ge(sm["spread"], 1)
                pe.wait_ge(sm["sel"], 32)
                spread = qsT[0:NS, 0:P]
                for n in range(2):
                    nc.tensor.matmul(F[n], spread, x2[0:NS, n * 512:(n + 1) * 512], start=True, stop=True)
                nc.tensor.matmul(F[2][:, 0:P], spread, xT[0:NS, 0:P], start=True, stop=True)
                nc.tensor.matmul(F[2][:, P:2 * P], spread, gates[0:NS, :], start=True, stop=True
                                 ).then_inc(sm["rowsx"], 1)

            pe.wait_ge(zeroed, 1)
            pe.wait_ge(keyw_out, 2 * NHC + 2)
            for q in range(REST):
                project_rest(q)
                sample(step_at(SAMPLE_AT, q + 1))
                step = step_at(PE_FRONT_AT, q + 1)
                if step == 1:
                    pe.wait_ge(sm["vb_used"], NS)
                elif step == 8:
                    pe.wait_ge(ld_wo, 16)
                front_mid(step_at(PE_MID_AT, q + 1), 0)
                front(step, 0)
            pe.wait_ge(pj_out, FIRST + REST)
            add_residual(0)
            add_experts(0, 0)
            with pe.Fori(0, NB - 1) as b:
                for g in range(1, GROUPS):
                    add_experts(b, g, range(0, 2))
                    front_mid(g, b + 1)
                    add_experts(b, g, range(2, PAIRS))
                    front(g, b + 1)
                pe.wait_ge(acc_out, b + 1)
                add_residual(b + 1)
                add_experts(b + 1, 0)
            for g in range(1, GROUPS):
                add_experts(NB - 1, g, range(0, 2))
                if g >= SAMPLE_STEP:
                    front_mid(g + 8 - SAMPLE_STEP, NB, NS)
                add_experts(NB - 1, g, range(2, PAIRS))
                if g >= SAMPLE_STEP:
                    front(g + 8 - SAMPLE_STEP, NB, NS)
                if g == SPREAD_STEP:
                    spread_samples()
            pe.wait_ge(acc_out, NB)
            for n in range(2):
                mm = nc.tensor.matmul(acc[0:NS, n * 512:(n + 1) * 512], ident[0:NS, 0:NS],
                                      h[0:NS, n * 512:(n + 1) * 512], start=True, stop=False, skip_group_check=True)
            mm.then_inc(residual_in, 1)
            for p in range(PAIRS):
                pe.wait_ge(diags, NB * GROUPS * PAIRS + p + 1)
                for r in range(p * PAIR, (p + 1) * PAIR):
                    for n in range(2):
                        mm = nc.tensor.matmul(acc[0:NS, n * 512:(n + 1) * 512], row_u[r][:, 0:NS],
                                              row_v[r][:, n * 512:(n + 1) * 512],
                                              start=False, stop=(r == RING - 1), skip_group_check=True)
                    mm.then_inc(used, 1)

        @block.scalar
        def _(act):
            me = Steps(act, act_steps)

            def copy(o, i, **kw_):
                return nc.scalar.activation(o, i, ACT.Copy, **kw_)

            roots = Steps(act, root_in)

            def root(o):
                roots.n += 1
                roots.sync()
                nc.scalar.activation(o, o, ACT.Sqrt).then_inc(root_out, 1)

            def tokens_in(n):
                act.wait_ge(xn_T, n + 1)
                for k in range(KC):
                    ins = copy(tokens_T(n, k), acc[:, k * P:k * P + token_rows(n)], scale=g1c[:, k:k + 1])
                ins.then_inc(xn_out, 1)

            def first_out(c, n):
                tile = 2 * c + n
                act.wait_ge(pj_mm, tile + 1)
                dst, rows = (proj, projs)[n], token_rows(n)
                copy(dst[0:rows, c * CW:(c + 1) * CW], F[tile % BANKS][0:rows, 0:CW]).then_inc(pj_out, 1)

            def rest_out(q):
                act.wait_ge(pj_mm, FIRST + q + 1)
                if q >= STG:
                    act.nop(nofuse=True)
                    act.wait_ge(st_pj[q % STG], 16 * (q // STG))
                copy(staging[q % STG], acc[:, q % 2 * 512:q % 2 * 512 + CW]).then_inc(pj_out, 1)

            def keyw_out_(n):
                for half in range(2):
                    act.wait_ge(keyw_mm, 2 * n + half + 1)
                    copy(keyw[:, half * 4:half * 4 + 4, n * NK:(n + 1) * NK],
                         acc[:, half * 512:(half + 1) * 512].rearrange("p (k n) -> p k n", k=4)).then_inc(keyw_out, 1)

            act.wait_ge(ld_first, 32)
            for n in range(3):
                root(tok_root[n % 2][0:token_rows(n), :])
                if n < 2:
                    tokens_in(n)
            for c in range(NCH):
                if c + 2 < TILES:
                    tokens_in(c + 2)
                if c + 3 < TILES:
                    root(tok_root[(c + 3) % 2])
                first_out(c, 0)
                keyw_out_(2 * c)
                first_out(c, 1)
                keyw_out_(2 * c + 1)

            def sample(step):
                if step == 2:
                    act.wait_ge(sm["qT"], 1)
                    copy(sT, F[0][:, 0:96]).then_inc(sm["qT_out"], 1)
                    act.wait_ge(sm["kwT"], 1)
                    copy(kwT[:, 0:512], F[1]).then_inc(sm["kwT_out"], 1)
                    nc.scalar.activation(projs[0:NS, C_G:C_G + 512], projs[0:NS, C_G:C_G + 512], ACT.Silu
                                         ).then_inc(sm["silu_out"], 1)
                elif step == 3:
                    act.wait_ge(sm["qS"], 1)
                    copy(osT, F[0][:, 96:128]).then_inc(sm["qS_out"], 1)
                    act.wait_ge(sm["kwT"], 2)
                    copy(kwT[:, 512:1024], F[1]).then_inc(sm["kwT_out"], 1)
                elif step == 4:
                    act.wait_ge(sm["s"], 1)
                    sv = ss.rearrange("p (s j i) -> p j s i", s=NS, j=KVH)
                    for j in range(KVH):
                        src = (F[0][:, 128:160], F[1][:, 0:32])[j]
                        ins = copy(sv[:, j], src.rearrange("p (s i) -> p s i", s=NS), scale=S_SCALE)
                    ins.then_inc(sm["s_out"], 1)
                elif step == 5:
                    act.wait_ge(sm["nmax"], 1)
                    nc.scalar.activation(sr[0:64, :], sr[0:64, :], ACT.Exp, bias=n64[0:64, :],
                                         accum_out=r64[0:64, :])
                    nc.scalar.activation(e64[0:64, :], sinks64[0:64, :], ACT.Exp, bias=n64[0:64, :]
                                         ).then_inc(sm["exp"], 1)
                    root(rstds[0:NS, :])
                elif step == 6:
                    act.wait_ge(sm["pT"], 1)
                    copy(pts, F[0][:, 288:352]).then_inc(sm["pT_out"], 1)
                elif step == 7:
                    act.wait_ge(sm["mixT"], 1)
                    copy(mixTs[:, 32:64], F[0][:, 352:384])
                    copy(mixTs[:, 0:32], F[0][:, 384:416]).then_inc(sm["mixT_out"], 1)

            def transposes_out(b):
                act.wait_ge(qkT_mm, b + 1)
                copy(xT, FF(0, 2)).then_inc(qkT_out, 1)
                act.wait_ge(qsT_mm, b + 1)
                me.did(copy(kTb[:, 0:P], kTb[:, P:2 * P]))
                me.sync()
                me.did(copy(kTb[:, P:2 * P], F[3][:, 0:P]))
                copy(qsT[:], F[2]).then_inc(qsT_out, 1)

            def silu(b):
                act.wait_ge(ret_mm, b + 1)
                nc.scalar.activation(x2[:, 0:512], proj[:, C_G:C_G + 512], ACT.Silu).then_inc(silu_ready, 1)
                root(rstd)

            def window_exp(b):
                act.wait_ge(sw_nmax, b + 1)
                for q in range(QH):
                    me.did(nc.scalar.activation(work[:, q * 256:(q + 1) * 256], work[:, q * 256:(q + 1) * 256],
                                                ACT.Exp, bias=nmx[:, q:q + 1], accum_out=rs[:, q:q + 1]))
                nc.scalar.activation(es, es, ACT.Exp).then_inc(sw_exp, 1)

            def probs_out(b):
                for j in range(KVH):
                    act.wait_ge(pT_mm, b * 2 + (j + 1))
                    copy(work[:, j * D:(j + 1) * D], FF(2 * j, 2 * j + 2)).then_inc(pT_out, 1)

            def mix_out(b):
                act.wait_ge(sw_o, b + 1)
                copy(vprev[:], proj[:, C_VS:D_IN])
                act.wait_ge(mixT_mm, b + 1)
                copy(xT, FF(0, 2)).then_inc(mixT_out, 1)

            def tokens_out(b, rows=P):
                act.wait_ge(x2T_mm, b + 1)
                src, dst = FF(0, 2), xT
                if rows < P:
                    src = src.rearrange("p (k t) -> p k t", k=KC)[:, :, 0:rows]
                    dst = dst.rearrange("p (k t) -> p k t", k=KC)[:, :, 0:rows]
                copy(dst, src).then_inc(x2T_out, 1)

            def scores_out(b, half, rows=P):
                act.wait_ge(sc_mm, b * 4 + (2 * half + 2))
                copy(proj[0:rows, half * D:(half + 1) * D], FF(2 + 2 * half, 4 + 2 * half)[0:rows, :]
                     ).then_inc(sc_out, 1)

            def gates_exp(b, half, rows=P):
                act.wait_ge(best_shift, b * 2 + (half + 1))
                part_ = gates[0:rows, half * HALF:(half + 1) * HALF]
                nc.scalar.activation(part_, part_, ACT.Exp).then_inc(best_exp, 1)

            def front(step, b, rows=P):
                if step == 2:
                    transposes_out(b)
                elif step == 4:
                    silu(b)
                elif step == 5:
                    window_exp(b)
                elif step == 6:
                    probs_out(b)
                elif step == 8 and rows == P:
                    mix_out(b)
                elif step == 9:
                    root(hs2[0:rows, :])
                elif step == 10:
                    tokens_out(b, rows)
                elif step == 11:
                    scores_out(b, 0, rows)
                elif step == 12:
                    scores_out(b, 1, rows)
                elif step in (13, 15):
                    gates_exp(b, step // 15, rows)

            def expert_gelus(b, g):
                for p in range(PAIRS):
                    act.wait_ge(dots, b * (GROUPS * PAIRS) + (g * PAIRS + p + 1))
                    nc.scalar.activation(gel[:, p * PAIR:(p + 1) * PAIR], dot[:, p * PAIR:(p + 1) * PAIR],
                                         ACT.Gelu).then_inc(gelus, 1)

            def sum_out(b):
                act.wait_ge(topk_done, b * 2 + 4)
                act.nop(nofuse=True)
                act.wait_ge(used, b * SLOTS + (SLOTS + RING))
                copy(xT, acc).then_inc(acc_out, 1)

            for q in range(REST):
                rest_out(q)
                sample(step_at(SAMPLE_AT, q + 1))
                front(step_at(ACT_FRONT_AT, q + 1), 0)
            expert_gelus(0, 0)
            with act.Fori(0, NB - 1) as b:
                me.enter(b, 2 + QH)
                roots.enter(b, 3)
                for g in range(1, GROUPS):
                    expert_gelus(b, g)
                    front(g, b + 1)
                sum_out(b)
                expert_gelus(b + 1, 0)
                root(fs2)
                me.leave(NB - 1)
                roots.leave(NB - 1)
            for g in range(1, GROUPS):
                expert_gelus(NB - 1, g)
                if g >= SAMPLE_STEP:
                    front(g + 8 - SAMPLE_STEP, NB, NS)
            act.wait_ge(sm["rowsx"], 1)
            sum_out(NB - 1)
            root(fs2)
            expert_gelus(NB, 0)
            root(fs2[0:NS, :])

        @block.vector
        def _(v):
            me, roots = Steps(v, dve_steps), Steps(v, root_out)
            tt = nc.vector.tensor_tensor
            stt = nc.vector.scalar_tensor_tensor
            ts = nc.vector.tensor_scalar

            def tell(sem_, n=1):
                v.nop(nofuse=True).then_inc(sem_, n)

            me.did(nc.vector.memset(state[:], 0.0))
            me.did(nc.vector.memset(kTb[:], 0.0))
            me.did(nc.vector.memset(vprev[:], 0.0))
            me.sync()
            tell(zeroed, 1)
            tell(used, RING)
            tell(keyw_out, 2)

            def root(o, i, scale):
                ts(o, i, scale, EPS, ALU.mult, ALU.add).then_inc(root_in, 1)
                roots.n += 1
                roots.sync()
                me.did(nc.vector.reciprocal(o, o))
                me.sync()

            for n in range(TILES):
                rows = token_rows(n)
                xv, total, root_ = xa[n % 2][0:rows, :], tok_sum[n % 2][0:rows, :], tok_root[n % 2][0:rows, :]
                v.wait_ge(ld_x[n % 2], n // 2 * 16 + 16)
                me.did(stt(g2b[0:rows, :], xv, 1.0, xv, ALU.mult, ALU.mult, accum_out=total))
                me.sync()
                root(root_, total, 1.0 / D)
                ts(xv, xv, root_, None, ALU.mult).then_inc(xn_ready, 1)

            def rotate(rows, pj, rp, temp):
                qk4 = pj[0:rows, 0:1024].rearrange("p (c h d t) -> p c h d t", c=2, h=RH, t=2)
                tab = rp[0:rows, :].rearrange("p (c f d) -> p c f d", c=2, f=2)
                t1 = temp[0:rows, :].rearrange("p (n c h d) -> p n c h d", n=4, c=2, h=RH)
                for n, (half, trig) in enumerate(((0, 0), (1, 1), (0, 1), (1, 0))):
                    for c in range(2):
                        me.did(tt(t1[:, n, c], qk4[:, c, :, :, half],
                                  tab[:, c, trig, :].rearrange("p (a d) -> p a d", a=1).to_broadcast([rows, RH, 64]),
                                  ALU.mult))
                me.sync()
                for half, (a, b_, op) in enumerate(((0, 1, ALU.subtract), (2, 3, ALU.add))):
                    for c in range(2):
                        me.did(tt(qk4[:, c, :, :, half], t1[:, a, c], t1[:, b_, c], op))
                me.sync()

            def gated_norm(rows, pj, o, sq, silu, sums, root_, silu_sem, count):
                ov = o.rearrange("p (h e) -> p h e", h=RH)
                me.did(tt(sq, o, o, ALU.mult))
                me.sync()
                me.did(nc.vector.tensor_reduce(sums[0:rows, :], sq.rearrange("p (h e) -> p h e", h=RH), AX, ALU.add))
                me.sync()
                root(root_[0:rows, :], sums[0:rows, :], 1.0 / HD)
                me.did(tt(ov, ov, root_[0:rows, :].rearrange("p (h a) -> p h a", a=1).to_broadcast([rows, RH, HD]),
                          ALU.mult))
                v.wait_ge(silu_sem, count)
                v.nop(nofuse=True)
                me.sync()
                return tt(pj[0:rows, C_MIX:C_MIX + 512], o, silu, ALU.mult)

            prod, o_s = h[0:NS, 512:1024], h[0:NS, 0:512]

            def sample(step):
                if step == 1:
                    v.wait_ge(sm["columns"], 16)
                    v.nop(nofuse=True)
                    v.wait_ge(pj_out, FIRST)
                    v.nop(nofuse=True)
                    v.wait_ge(keyw_mm, 2 * NHC)
                    v.nop(nofuse=True)
                    v.wait_ge(xn_T, TILES)
                    rotate(NS, projs, ropes, work)
                    tell(sm["roped"])
                    me.did(tt(prod, projs[0:NS, C_Q:C_Q + 512], projs[0:NS, C_K:C_K + 512], ALU.mult))
                    me.sync()
                    me.did(nc.vector.tensor_reduce(qk[0:NS, :], prod.rearrange("p (h e) -> p h e", h=RH), AX,
                                                   ALU.add))
                    me.sync()
                elif step == 5:
                    s64, sp64 = F[0][0:64, 160:288], sr[0:64, :]
                    v.wait_ge(sm["sr"], 1)
                    me.did(nc.vector.tensor_copy(sp64, s64))
                    me.did(nc.vector.tensor_reduce(m64[0:64, :], s64, AX, ALU.max))
                    me.sync()
                    me.did(tt(m64[0:64, :], m64[0:64, :], sinks64[0:64, :], ALU.max))
                    me.sync()
                    ts(n64[0:64, :], m64[0:64, :], -1.0, None, ALU.mult).then_inc(sm["nmax"], 1)
                    v.wait_ge(sm["exp"], 1)
                    me.did(tt(m64[0:64, :], r64[0:64, :], e64[0:64, :], ALU.add))
                    me.sync()
                    me.did(nc.vector.reciprocal(m64[0:64, :], m64[0:64, :]))
                    me.sync()
                    ts(sp64, sp64, m64[0:64, :], None, ALU.mult).then_inc(sm["p"], 1)
                    v.wait_ge(sm["qSn"], 1)
                    for hh in range(RH):
                        me.did(ts(prod[:, hh * P:(hh + 1) * P], F[1][0:NS, hh * P:(hh + 1) * P],
                                  STEP_DECAY[hh], None, ALU.mult))
                    me.sync()
                    for hh in range(RH):
                        me.did(stt(o_s[:, hh * P:(hh + 1) * P], projs[0:NS, C_V + hh * P:C_V + (hh + 1) * P],
                                   qk[0:NS, hh:hh + 1], prod[:, hh * P:(hh + 1) * P], ALU.mult, ALU.add))
                    me.sync()
                    gated_norm(NS, projs, o_s, prod, projs[0:NS, C_G:C_G + 512], ssqs, rstds, sm["silu_out"], 1
                               ).then_inc(sm["mixr"], 1)
                elif step == 6:
                    v.wait_ge(sm["qS_out"], 1)
                    for hh in range(RH):
                        me.did(ts(st_s[:, :, hh, :], st_s[:, :, hh, :], STEP_DECAY[hh], None, ALU.mult))
                    me.sync()
                elif step == 8:
                    for s in range(NS):
                        v.wait_ge(sm["vb"], s + 1)
                        for hh in range(RH):
                            me.did(stt(st_s[:, s, hh, :], F[s % 2][:, hh * P:(hh + 1) * P],
                                       sT[:, 32 + hh * NS + s:33 + hh * NS + s], st_s[:, s, hh, :],
                                       ALU.mult, ALU.add))
                        me.sync()
                        tell(sm["vb_used"])
                    tell(sm["st"])

            def rotation(b):
                if isinstance(b, int):
                    v.wait_ge(ld_const, 16 * N_CONST)
                else:
                    v.wait_ge(ld_proj, b * 32)
                    v.nop(nofuse=True)
                rotate(P, proj, rope, work)
                tell(roped)
                tt(x2[:, 512:1024].rearrange("p (h e) -> p h e", h=RH),
                   proj[:, C_K:C_K + 512].rearrange("p (h e) -> p h e", h=RH),
                   kdec.rearrange("p (h a) -> p h a", a=1).to_broadcast([P, RH, HD]), ALU.mult).then_inc(kd_ready, 1)

            def decay_scores(b):
                v.wait_ge(st_mm, b + 1)
                tt(x2[:, 0:512], F[0], dmaskT[:].rearrange("p h m -> p (h m)"), ALU.mult).then_inc(stm_ready, 1)

            def retention_out(b):
                v.wait_ge(ret_mm, b + 1)
                o = xT[:, 0:512]
                me.did(tt(o.rearrange("p (h e) -> p h e", h=RH), F[3].rearrange("p (h e) -> p h e", h=RH),
                          qdec.rearrange("p (h a) -> p h a", a=1).to_broadcast([P, RH, HD]), ALU.mult))
                for hh in range(RH):
                    me.did(stt(state[:, hh, :], state[:, hh, :], BLOCK_DECAY[hh], F[4][:, hh * P:(hh + 1) * P],
                               ALU.mult, ALU.add))
                me.sync()
                me.did(tt(o, o, F[5], ALU.add))
                me.sync()
                gated_norm(P, proj, o, xT[:, 512:1024], x2[:, 0:512], ssq, rstd, silu_ready, b + 1
                           ).then_inc(mixr_ready, 1)

            def window_max(b, mask):
                if isinstance(b, int):
                    v.wait_ge(ld_mask0, 16)
                v.wait_ge(sw_mm, b + 1)
                v.nop(nofuse=True)
                v.wait_ge(mixr_ready, b + 1)
                s3 = work[:].rearrange("p (q s) -> p q s", q=QH)
                me.did(stt(s3, FF(2, 6).rearrange("p (q s) -> p q s", q=QH), S_SCALE,
                           mask.rearrange("p (a s) -> p a s", a=1).to_broadcast([P, QH, 2 * P]), ALU.mult, ALU.add))
                me.sync()
                me.did(nc.vector.tensor_reduce(mx, s3, AX, ALU.max))
                me.sync()
                me.did(tt(mx, mx, sinkb, ALU.max))
                me.sync()
                me.did(tt(es, sinkb, mx, ALU.subtract))
                me.sync()
                ts(nmx, mx, -1.0, None, ALU.mult).then_inc(sw_nmax, 1)

            def window_out(b):
                v.wait_ge(sw_exp, b + 1)
                me.did(tt(rden, rs, es, ALU.add))
                me.sync()
                me.did(nc.vector.reciprocal(rden, rden))
                v.wait_ge(sw_o, b + 1)
                v.nop(nofuse=True)
                me.sync()
                tt(proj[:, C_MIX + 512:C_MIX + 1024].rearrange("p (q d) -> p q d", q=QH),
                   F[4].rearrange("p (q d) -> p q d", q=QH),
                   rden.rearrange("p (q a) -> p q a", a=1).to_broadcast([P, QH, SD]), ALU.mult
                   ).then_inc(mixs_ready, 1)

            def norm_output(b, rows=P):
                v.wait_ge(ld_res, b * 16 + 16)
                v.nop(nofuse=True)
                v.wait_ge(o_mm, b * 2 + 2)
                hv, xv = h[0:rows, :], x2[0:rows, :]
                me.did(tt(hv, hv, FF(2, 4)[0:rows, :], ALU.add))
                me.sync()
                me.did(stt(xv, hv, 1.0, hv, ALU.mult, ALU.mult, accum_out=hs1[0:rows, :]))
                me.sync()
                root(hs2[0:rows, :], hs1[0:rows, :], 1.0 / D)
                stt(xv, hv, hs2[0:rows, :], g2b[0:rows, :], ALU.mult, ALU.mult).then_inc(x2_ready, 1)

            sc3 = proj[:, 0:NSC].rearrange("p (c n) -> p c n", c=NHC)
            cand8 = proj[:, 0:NSC].rearrange("p (h c) -> p h c", h=PH)
            HH = PH // 2

            def beside(at_, n, like=None):
                return proj[:, NSC + at_:NSC + at_ + n]

            vals, inds, indf = beside(0, 2 * HALF), beside(128, 2 * HALF), beside(256, 2 * HALF)
            best, posn, chosen = beside(384, HALF), beside(448, HALF), beside(512, 2 * HALF)
            ab, abf, numbers = vals, inds, beside(640, SLOTS)

            def rank(js, rowsof, v16, i16):
                for r8 in range(2):
                    for j in js:
                        me.did(nc.vector.max(v16(j)[:, r8 * 8:r8 * 8 + 8], rowsof(j)))
                    hold(v, me.sem, me.base + me.n)
                    for j in js:
                        me.did(nc.vector.max_index(i16(j)[:, r8 * 8:r8 * 8 + 8], v16(j)[:, r8 * 8:r8 * 8 + 8],
                                                   rowsof(j)))
                    hold(v, me.sem, me.base + me.n)
                    if r8 == 0:
                        for j in js:
                            me.did(nc.vector.match_replace(rowsof(j), v16(j)[:, 0:8], rowsof(j), TAKEN))
                        hold(v, me.sem, me.base + me.n)

            def rank_halves(b, half, rows=P):
                hold(v, sc_out, b * 2 + (half + 1))
                v3 = vals[0:rows].rearrange("p (c k) -> p c k", k=TK)
                i3 = inds.bitcast(U32)[0:rows].rearrange("p (c k) -> p c k", k=TK)
                rank(range(PH), lambda j: sc3[0:rows, half * PH + j, :], lambda j: v3[:, j, :],
                     lambda j: i3[:, j, :])
                for hh in range(HH):
                    me.did(tt(cand8[0:rows, half * HH + hh, :].rearrange("p (a b) -> p a b", a=TK),
                              v3[:, 2 * hh, :].rearrange("p (k a) -> p k a", a=1).to_broadcast([rows, TK, TK]),
                              v3[:, 2 * hh + 1, :].rearrange("p (a k) -> p a k", a=1).to_broadcast([rows, TK, TK]),
                              ALU.add))
                me.did(nc.vector.tensor_copy(indf[0:rows], inds.bitcast(U32)[0:rows]))
                hold(v, me.sem, me.base + me.n)

            def choose(b, half, rows=P):
                b3 = best[0:rows].rearrange("p (h k) -> p h k", h=HH)
                pu = posn.bitcast(U32)[0:rows]
                p3 = pu.rearrange("p (h k) -> p h k", h=HH)
                rank(range(HH), lambda j: cand8[0:rows, half * HH + j, :], lambda j: b3[:, j, :],
                     lambda j: p3[:, j, :])
                abu = ab.bitcast(U32)[0:rows]
                me.did(ts(abu[:, 0:HALF], pu, 4, None, ALU.logical_shift_right))
                me.did(ts(abu[:, HALF:], pu, 15, None, ALU.bitwise_and))
                g3 = gates[0:rows, half * HALF:(half + 1) * HALF].rearrange("p (h k) -> p h k", h=HH)
                tt(g3, b3, b3[:, :, 0:1].to_broadcast([rows, HH, TK]), ALU.subtract).then_inc(best_shift, 1)
                me.sync()
                me.did(nc.vector.tensor_copy(abf[0:rows], abu))
                me.sync()

            def number(b, half, rows=P):
                g3 = gates[0:rows, half * HALF:(half + 1) * HALF].rearrange("p (h k) -> p h k", h=HH)
                one = proj[0:rows, half * D:(half + 1) * D].rearrange("p (n a) -> p n a", a=TK)
                iot = iota16[0:rows, :].rearrange("p (a k) -> p a k", a=1).to_broadcast([rows, HALF, TK])
                i4 = indf[0:rows].rearrange("p (h c k) -> p h c k", h=HH, c=2)
                for c in range(2):
                    me.did(tt(one, abf[0:rows, c * HALF:(c + 1) * HALF].rearrange("p (n a) -> p n a", a=1)
                              .to_broadcast([rows, HALF, TK]), iot, ALU.is_equal))
                    me.sync()
                    for hh in range(HH):
                        o3 = one[:, hh * TK:(hh + 1) * TK, :]
                        me.did(tt(o3, o3, i4[:, hh, c, :].rearrange("p (a k) -> p a k", a=1)
                                  .to_broadcast([rows, TK, TK]), ALU.mult))
                    me.sync()
                    me.did(nc.vector.tensor_reduce(chosen[0:rows, c * HALF:(c + 1) * HALF], one, AX, ALU.add))
                    me.sync()
                num = numbers[0:rows, half * HALF:(half + 1) * HALF]
                me.did(stt(num, chosen[0:rows, 0:HALF], float(NK), chosen[0:rows, HALF:], ALU.mult, ALU.add))
                v.wait_ge(best_exp, b * 2 + (half + 1))
                v.nop(nofuse=True)
                me.sync()
                if not isinstance(b, int) or b > 0:
                    v.wait_ge(idx_taken, b * 2)
                me.did(nc.vector.tensor_copy(idx[0:rows, half * HALF:(half + 1) * HALF], num))
                me.did(nc.vector.tensor_reduce(ssum[0:rows, 0:HH], g3, AX, ALU.add))
                me.sync()
                me.did(nc.vector.reciprocal(srec[0:rows, 0:HH], ssum[0:rows, 0:HH]))
                me.sync()
                tt(g3, g3, srec[0:rows, 0:HH].rearrange("p (h a) -> p h a", a=1).to_broadcast([rows, HH, TK]),
                   ALU.mult).then_inc(topk_done, 1)

            def front(step, b, mask, rows=P):
                if step == 1:
                    rotation(b)
                elif step == 3:
                    decay_scores(b)
                elif step == 4:
                    retention_out(b)
                elif step == 5:
                    window_max(b, mask)
                elif step == 7:
                    window_out(b)
                elif step == 9:
                    norm_output(b, rows)
                elif step in (13, 15):
                    number(b, step // 15, rows)

            def front_mid(step, b, rows=P):
                if step in (12, 14):
                    if step == 14:
                        hold(v, topk_done, b * 2 + 1)
                    rank_halves(b, step // 14, rows)
                elif step in (13, 15):
                    choose(b, step // 15, rows)

            def take_over(b):
                v.wait_ge(topk_done, b * 2 + 2)
                if not isinstance(b, int) or b > 0:
                    v.nop(nofuse=True)
                    v.wait_ge(diags, b * (GROUPS * PAIRS))
                me.did(nc.vector.tensor_copy(x2g[:], x2))
                me.did(nc.vector.tensor_copy(gateg[:], gates[:]))
                me.sync()

            def expert_dots(b, g, pairs=range(PAIRS)):
                def diagonals(p):
                    v.wait_ge(gelus, b * (GROUPS * PAIRS) + (g * PAIRS + p + 1))
                    for r in range(p * PAIR, (p + 1) * PAIR):
                        ins = ts(row_u[r][:, 0:P], ident[:], gel[:, r:r + 1],
                                 gateg[:, g * RING + r:g * RING + r + 1], ALU.mult, ALU.mult)
                    ins.then_inc(diags, 1)

                for p in pairs:
                    for r in range(p * PAIR, (p + 1) * PAIR):
                        v.wait_ge(ld_row[r], b * (GROUPS * 16) + (g * 16 + 16))
                        ins = stt(row_u[r], row_u[r], 1.0, x2g[:], ALU.mult, ALU.mult, accum_out=dot[:, r:r + 1])
                    ins.then_inc(dots, 1)
                    if p > pairs[0]:
                        diagonals(p - 1)
                diagonals(pairs[-1])

            def block_out(b):
                v.wait_ge(acc_out, b + 1)
                me.did(stt(x2, xT, 1.0, xT, ALU.mult, ALU.mult, accum_out=fs1))
                me.sync()
                root(fs2, fs1, 1.0 / D)
                stt(xT, xT, fs2, gfb[:], ALU.mult, ALU.mult).then_inc(y_ready, 1)

            for step in range(1, SAMPLE_STEPS + 1):
                sample(step)
            for step in range(1, GROUPS):
                front_mid(step, 0)
                front(step, 0, mask0)
            for q in st_pj:
                v.wait_ge(q, 16 * REST // STG)
            v.wait_ge(ld_gf, 16)
            take_over(0)
            expert_dots(0, 0)
            with v.Fori(0, NB - 1) as b:
                me.enter(b, STEPS_PER_BLOCK)
                roots.enter(b, 3)
                for g in range(1, GROUPS):
                    if g in (12, 13, 14, 15):
                        expert_dots(b, g, range(0, 2))
                        front_mid(g, b + 1)
                        expert_dots(b, g, range(2, PAIRS))
                    else:
                        expert_dots(b, g)
                    front(g, b + 1, wmask[:])
                take_over(b + 1)
                expert_dots(b + 1, 0)
                block_out(b)
                me.leave(NB - 1)
                roots.leave(NB - 1)
            for g in range(1, GROUPS):
                if g + 8 - SAMPLE_STEP in (12, 13, 14, 15):
                    expert_dots(NB - 1, g, range(0, 2))
                    front_mid(g + 8 - SAMPLE_STEP, NB, NS)
                    expert_dots(NB - 1, g, range(2, PAIRS))
                else:
                    expert_dots(NB - 1, g)
                if g >= SAMPLE_STEP:
                    front(g + 8 - SAMPLE_STEP, NB, None, NS)
                if g + 8 - SAMPLE_STEP == 15:
                    v.wait_ge(topk_done, NB * 2 + 2)
                    nc.vector.tensor_copy(xT[0:NS, 0:P], numbers[0:NS, :]).then_inc(sm["spread"], 1)
                if g == SPREAD_STEP + 1:
                    v.wait_ge(sm["rowsx"], 1)
                    pick = qsT[:, P:2 * P]
                    both = proj[:, 0:2 * P]
                    for n in range(2):
                        me.did(tt(both[:, n * P:(n + 1) * P], F[2][:, n * P:(n + 1) * P], pick, ALU.mult))
                    me.sync()
                    me.did(nc.vector.tensor_reduce(proj[:, 256:256 + 2 * PH],
                                                   both.rearrange("p (n k) -> p n k", k=TK), AX, ALU.add))
                    me.sync()
                    v.wait_ge(idx_taken, 2 * NB)
                    nc.vector.tensor_copy(idx[:, 0:PH], proj[:, 256:256 + PH]).then_inc(sm["idx8"], 1)
            xr = x2g[:]
            me.did(nc.vector.tensor_copy(xr, FF(0, 2)))
            me.sync()
            block_out(NB - 1)
            v.wait_ge(sm["idx8"], 1)
            for p in range(PAIRS):
                for r in range(p * PAIR, (p + 1) * PAIR):
                    v.wait_ge(ld_row[r], NB * GROUPS * 16 + 16)
                    ins = stt(row_u[r], row_u[r], 1.0, xr, ALU.mult, ALU.mult, accum_out=dot[:, r:r + 1])
                ins.then_inc(dots, 1)
            own = qsT[:, 2 * P:2 * P + NS]
            for p in range(PAIRS):
                v.wait_ge(gelus, NB * GROUPS * PAIRS + p + 1)
                for r in range(p * PAIR, (p + 1) * PAIR):
                    ins = ts(row_u[r][:, 0:NS], own, gel[:, r:r + 1], proj[:, 256 + PH + r:257 + PH + r],
                             ALU.mult, ALU.mult)
                ins.then_inc(diags, 1)
            v.wait_ge(used, NB * SLOTS + 2 * RING)
            ys = work[0:NS, 0:D]
            me.did(nc.vector.tensor_copy(ys, acc[0:NS, :]))
            me.sync()
            me.did(stt(row_u[0][0:NS, :], ys, 1.0, ys, ALU.mult, ALU.mult, accum_out=fs1[0:NS, :]))
            me.sync()
            root(fs2[0:NS, :], fs1[0:NS, :], 1.0 / D)
            stt(ys, ys, fs2[0:NS, :], gfb[0:NS, :], ALU.mult, ALU.mult).then_inc(y_ready, 1)


SAMPLE_STEPS = 8
SAMPLE_AT = {n: 2 * n for n in range(1, SAMPLE_STEPS + 1)}
PE_FRONT_AT = {1: 17, 2: 19, 3: 20, 4: 23, 5: 26, 6: 28, 7: 29, 8: 31, 9: 34, 10: 36, 11: 39}
PE_MID_AT = {9: 32, 11: 37, 12: 40}
ACT_FRONT_AT = {2: 18, 4: 21, 5: 24, 6: 27, 8: 30, 9: 33, 10: 35, 11: 38, 12: 41, 13: 42, 15: 46}
SPREAD_STEP = 12
SAMPLE_STEP = 4
STEPS_PER_BLOCK = 203


_INS = ["x_prompt", "x_sample", "state_ret", "cache_swa_k", "cache_swa_v", "norm1_g", "swa_sinks", "w_out",
        "norm2_g", "final_g"]
_OUTS = [(1, SEQ, D), (NS, 1, D), (1, RH, HD, HD), (1, P, KVH, SD), (1, P, KVH, SD), (NS, RH, HD, HD),
         (NS, P, KVH, SD), (NS, P, KVH, SD)]


def constants():
    f = np.float32
    half = HD // 2
    inv = (f(1.0) / (f(10000.0) ** np.linspace(0.0, 1.0, half, dtype=f))).astype(f)
    pos = np.concatenate([np.arange(SEQ), np.full(NS, SEQ)]).astype(f)
    ang = (pos[:, None] * inv[None, :]).astype(f).astype(np.float64)
    cos, sin = np.cos(ang), np.sin(ang)
    t = np.arange(P)
    diff = t[None, :] - t[:, None]
    dmask = np.where(diff[:, None, :] >= 0, np.exp(np.maximum(diff, 0)[:, None, :] * LOG_DECAY[None, :, None]), 0.0)
    prev = np.where(t[None, :] > t[:, None], 0.0, MASKED)
    cur = np.where(t[None, :] <= t[:, None], 0.0, MASKED)
    s8, p16 = np.arange(NS), t // TK
    pick = np.tile(t[:, None] % TK == np.arange(TK)[None, :], (1, PH))
    out = {
        "c_rope": np.concatenate([cos, sin, cos * K_SCALE, sin * K_SCALE], 1),
        "c_ident": np.eye(P),
        "c_dmaskT": dmask.reshape(P, RH * P),
        "c_qdec": np.exp((t[:, None] + 1.0) * LOG_DECAY[None, :]),
        "c_kdec": np.exp((P - 1.0 - t[:, None]) * LOG_DECAY[None, :]),
        "c_iota": np.tile(np.arange(TK), (P, 1)),
        "c_wmask": np.concatenate([prev, cur], 1),
        "c_wmask0": np.concatenate([np.full((P, P), MASKED), cur], 1),
        "c_sel8": np.repeat(np.eye(NS), P, axis=1),
        "c_spread": (s8[:, None] == p16[None, :]),
        "c_pick": np.concatenate([pick, p16[:, None] == s8[None, :]], 1),
    }
    return {k: np.ascontiguousarray(v.astype(f)) for k, v in out.items()}


def kernel(**inputs):
    import concourse.bacc as _bacc
    from concourse.bass_utils import run_bass_kernel_spmd as _run

    nc = _bacc.Bacc("TRN2", target_bir_lowering=False, num_devices=1)
    arrays = {n: np.ascontiguousarray(inputs[n]) for n in _INS}
    w_in = np.asarray(inputs["w_in"])
    qs = w_in[:, C_QS:C_KS].reshape(D, KVH, GRP, SD).transpose(0, 2, 1, 3).reshape(D, QH * SD)
    arrays["w_in"] = np.concatenate([w_in[:, :C_QS], qs, w_in[:, C_KS:]], axis=1)
    arrays["wqT"] = np.ascontiguousarray(np.asarray(inputs["peer_w_q"]).reshape(D, NHC, NK).transpose(1, 2, 0))
    arrays["sub_keysT"] = np.ascontiguousarray(
        np.asarray(inputs["peer_sub_keys"]).transpose(3, 0, 1, 2).reshape(NK, NSC))
    arrays["peer_uv"] = np.concatenate([np.asarray(inputs["peer_u"]), np.asarray(inputs["peer_v"])], axis=1)
    arrays.update(constants())
    args = {n: nc.dram_tensor("in_" + n, a.shape, mybir.dt.from_np(a.dtype), kind="ExternalInput").ap()
            for n, a in arrays.items()}
    outs = [nc.dram_tensor(f"out_{i}", shape, F32, kind="ExternalOutput").ap() for i, shape in enumerate(_OUTS)]
    build(nc, args, outs)
    r = _run(nc, [{"in_" + n: a for n, a in arrays.items()}], core_ids=[0])
    return tuple(r.results[0][f"out_{i}"] for i in range(len(_OUTS)))
```
